# Optimizing a Trainium2 kernel written in Bass

```python
import jax
import jax.numpy as jnp
from jax import lax
import numpy as np
import math
import jax, jax.numpy as jnp

D_MODEL = 1024
BATCH = 1
SEQ = 256
DEPTH = 1

GRID_W = 64
CTX_LEN = 256
NA_HEAD_DIM = 64
N_NA_HEADS = (D_MODEL // 2) // NA_HEAD_DIM
NA_WIDTH = N_NA_HEADS * NA_HEAD_DIM
NA_WIN_H = 8
NA_WIN_W = 16
NA_QBLOCK_W = 16
NA_KSPAN_W = NA_QBLOCK_W + NA_WIN_W
ROPE_BASE = 10000.0
HG_DK = 128
HG_DV = 128
N_HG_HEADS = (D_MODEL // 2) // HG_DV
HG_KEY_WIDTH = N_HG_HEADS * HG_DK
HG_WIDTH = N_HG_HEADS * HG_DV
HG_CHUNK = 32
MIX_WIDTH = NA_WIDTH + HG_WIDTH
IN_COLS = 3 * NA_WIDTH + 3 * HG_KEY_WIDTH + 2 * HG_WIDTH
N_EXPERTS = 16
EC_CAPACITY_FACTOR = 2
D_EXPERT = ((8 * D_MODEL // 3 + 63) // 64) * 64
RMS_EPS = 1e-6


def rms_norm(x, g):
    xf = x.astype(jnp.float32)
    y = xf * lax.rsqrt(jnp.mean(xf * xf, axis=-1, keepdims=True) + RMS_EPS)
    return (y * g.astype(jnp.float32)).astype(x.dtype)

def modulate(h, shift, scale):
    return h * (1.0 + scale) + shift

def to_heads(x, n_heads):
    b, t, w = x.shape
    return x.reshape(b, t, n_heads, w // n_heads).transpose(0, 2, 1, 3)

def from_heads(x):
    b, h, t, d = x.shape
    return x.transpose(0, 2, 1, 3).reshape(b, t, h * d)

def split_cols(p):
    sizes = (NA_WIDTH, NA_WIDTH, NA_WIDTH, HG_KEY_WIDTH, HG_KEY_WIDTH, HG_KEY_WIDTH, HG_WIDTH, HG_WIDTH)
    bounds = []
    acc = 0
    for s in sizes[:-1]:
        acc += s
        bounds.append(acc)
    return jnp.split(p, bounds, axis=-1)

def rope_1d(x, pos):
    d = x.shape[-1]
    inv_freq = ROPE_BASE ** (-jnp.arange(0, d, 2, dtype=jnp.float32) / d)
    ang = pos[:, None] * inv_freq[None, :]
    cos = jnp.cos(ang).astype(x.dtype)
    sin = jnp.sin(ang).astype(x.dtype)
    x1, x2 = x[..., : d // 2], x[..., d // 2:]
    return jnp.concatenate([x1 * cos - x2 * sin, x1 * sin + x2 * cos], axis=-1)

def axial_rope(x, row_pos, col_pos):
    half = x.shape[-1] // 2
    return jnp.concatenate([rope_1d(x[..., :half], row_pos), rope_1d(x[..., half:], col_pos)], axis=-1)

def neighbourhood_attention(q, k, v, k_ctx, v_ctx, rpb):
    bsz, nh, seq, dh = q.shape
    rows = seq // GRID_W
    kh = min(NA_WIN_H, rows)
    ncb = GRID_W // NA_QBLOCK_W
    scale = dh ** -0.5
    t = jnp.arange(seq)
    row_pos = (t // GRID_W).astype(jnp.float32)
    col_pos = (t % GRID_W).astype(jnp.float32)
    q_rot = axial_rope(q, row_pos, col_pos)
    k_rot = axial_rope(k, row_pos, col_pos)
    r = jnp.arange(rows)
    r0 = jnp.clip(r - kh // 2, 0, rows - kh)
    key_rows = r0[:, None] + jnp.arange(kh)[None, :]
    j = jnp.arange(ncb)
    c0 = jnp.clip(j * NA_QBLOCK_W - NA_WIN_W // 2, 0, GRID_W - NA_KSPAN_W)
    key_cols = c0[:, None] + jnp.arange(NA_KSPAN_W)[None, :]
    tok = key_rows[:, None, :, None] * GRID_W + key_cols[None, :, None, :]
    k_blk = k_rot[:, :, tok]
    v_blk = v[:, :, tok]
    q_cols = j[:, None] * NA_QBLOCK_W + jnp.arange(NA_QBLOCK_W)[None, :]
    win_c0 = jnp.clip(q_cols - NA_WIN_W // 2, 0, GRID_W - NA_WIN_W)
    kc = key_cols[:, None, :]
    in_win = (kc >= win_c0[:, :, None]) & (kc < win_c0[:, :, None] + NA_WIN_W)
    dr_idx = key_rows - r[:, None] + NA_WIN_H - 1
    dc_idx = jnp.clip(kc - q_cols[:, :, None] + NA_WIN_W - 1, 0, 2 * NA_WIN_W - 2)
    bias = rpb[:, dr_idx[:, None, None, :, None], dc_idx[None, :, :, None, :]]
    q_blk = q_rot.reshape(bsz, nh, rows, ncb, NA_QBLOCK_W, dh)
    s_win = jnp.einsum('bhrjqd,bhrjakd->bhrjqak', q_blk, k_blk).astype(jnp.float32) * scale
    s_win = jnp.where(in_win[:, :, None, :], s_win + bias.astype(jnp.float32), -jnp.inf)
    q_plain = q.reshape(bsz, nh, rows, ncb, NA_QBLOCK_W, dh)
    s_ctx = jnp.einsum('bhrjqd,bhld->bhrjql', q_plain, k_ctx).astype(jnp.float32) * scale
    n_win = kh * NA_KSPAN_W
    s_all = jnp.concatenate([s_win.reshape(bsz, nh, rows, ncb, NA_QBLOCK_W, n_win), s_ctx], axis=-1)
    p = jax.nn.softmax(s_all, axis=-1).astype(v.dtype)
    p_win = p[..., :n_win].reshape(bsz, nh, rows, ncb, NA_QBLOCK_W, kh, NA_KSPAN_W)
    o = (jnp.einsum('bhrjqak,bhrjakd->bhrjqd', p_win, v_blk)
         + jnp.einsum('bhrjql,bhld->bhrjqd', p[..., n_win:], v_ctx))
    return from_heads(o.reshape(bsz, nh, seq, dh))

def context_attention(q, k, v):
    scale = q.shape[-1] ** -0.5
    s = jnp.einsum('bhld,bhmd->bhlm', q, k).astype(jnp.float32) * scale
    p = jax.nn.softmax(s, axis=-1).astype(v.dtype)
    return jnp.einsum('bhlm,bhmd->bhld', p, v)

def log_forget(z, lb):
    lb_h = lb.reshape(N_HG_HEADS, 1, HG_DK)
    return jnp.log(lb_h + (1.0 - lb_h) * jax.nn.sigmoid(z.astype(jnp.float32)))

def gla_chunked(q, k, v, log_f, s0):
    bsz, nh, seq, dk = q.shape
    dv = v.shape[-1]
    n = seq // HG_CHUNK
    qc = q.astype(jnp.float32).reshape(bsz, nh, n, HG_CHUNK, dk)
    kc = k.astype(jnp.float32).reshape(bsz, nh, n, HG_CHUNK, dk)
    vc = v.astype(jnp.float32).reshape(bsz, nh, n, HG_CHUNK, dv)
    b = jnp.cumsum(log_f.reshape(bsz, nh, n, HG_CHUNK, dk), axis=3)
    b_end = b[:, :, :, -1:, :]
    q_dec = qc * jnp.exp(b)
    k_dec = kc * jnp.exp(-b)
    idx = jnp.arange(HG_CHUNK)
    lower = idx[:, None] >= idx[None, :]
    a = jnp.where(lower, jnp.einsum('bhnck,bhnsk->bhncs', q_dec, k_dec), 0.0)
    o_intra = jnp.einsum('bhncs,bhnsv->bhncv', a, vc)
    kv = jnp.einsum('bhnck,bhncv->bhnkv', kc * jnp.exp(b_end - b), vc)
    decay = jnp.exp(b_end[:, :, :, 0, :])

    def step(s, inp):
        dec, upd = inp
        return dec[..., None] * s + upd, s

    s_fin, s_prev = lax.scan(step, s0.astype(jnp.float32),
                             (jnp.moveaxis(decay, 2, 0), jnp.moveaxis(kv, 2, 0)))
    s_prev = jnp.moveaxis(s_prev, 0, 2)
    o_inter = jnp.einsum('bhnck,bhnkv->bhncv', q_dec, s_prev)
    return (o_intra + o_inter).reshape(bsz, nh, seq, dv), s_fin

def hgrn2_bidir(q, z_fwd, z_bwd, i, lb, s0_fwd, s0_bwd):
    lf_f = log_forget(z_fwd, lb)
    lf_b = log_forget(z_bwd, lb)
    o_f, s_f = gla_chunked(q, -jnp.expm1(lf_f), i, lf_f, s0_fwd)
    flip = lambda t: jnp.flip(t, axis=2)
    o_b, s_b = gla_chunked(flip(q), flip(-jnp.expm1(lf_b)), flip(i), flip(lf_b), s0_bwd)
    return o_f + flip(o_b), s_f, s_b

def hgrn2_readout(o, g, norm_g):
    return from_heads(rms_norm(o.astype(g.dtype), norm_g) * jax.nn.sigmoid(g))

def ec_moe(h, w_router, w_gate, w_up, w_down):
    bsz, n_tok, d = h.shape
    cap = EC_CAPACITY_FACTOR * n_tok // N_EXPERTS
    aff = jax.nn.softmax(jnp.einsum('btd,de->bte', h, w_router).astype(jnp.float32), axis=-1)
    gate, idx = lax.top_k(jnp.swapaxes(aff, 1, 2), cap)
    xs = jax.vmap(lambda hb, ib: hb[ib])(h, idx)
    hid = (jax.nn.silu(jnp.einsum('becd,edf->becf', xs, w_gate))
           * jnp.einsum('becd,edf->becf', xs, w_up))
    y = jnp.einsum('becf,efd->becd', hid, w_down) * gate[..., None].astype(h.dtype)
    return jax.vmap(lambda yb, ib: jnp.zeros((n_tok, d), y.dtype).at[ib.reshape(-1)].add(yb.reshape(-1, d)))(y, idx)

def first_inputs(seed: int = 0) -> dict:
    key = jax.random.key(seed)
    ks = jax.random.split(key, 19)
    nrm = jax.random.normal
    d = D_MODEL
    f32 = jnp.float32
    return {
        'x': nrm(ks[0], (BATCH, SEQ, d), f32),
        'c': nrm(ks[1], (BATCH, d), f32),
        'ctx': nrm(ks[2], (BATCH, CTX_LEN, d), f32),
        'c_ctx': nrm(ks[3], (d,), f32),
        'w_mod': 0.5 * d ** -0.5 * nrm(ks[4], (DEPTH, d, 6 * d), f32),
        'b_mod': 0.01 * nrm(ks[5], (DEPTH, 6 * d), f32),
        'g_pre1': 1.0 + 0.05 * nrm(ks[6], (DEPTH, d), f32),
        'g_post1': 1.0 + 0.05 * nrm(ks[7], (DEPTH, d), f32),
        'g_pre2': 1.0 + 0.05 * nrm(ks[8], (DEPTH, d), f32),
        'g_post2': 1.0 + 0.05 * nrm(ks[9], (DEPTH, d), f32),
        'w_in': d ** -0.5 * nrm(ks[10], (DEPTH, d, IN_COLS), f32),
        'w_out': MIX_WIDTH ** -0.5 * nrm(ks[11], (DEPTH, MIX_WIDTH, d), f32),
        'na_rpb': 0.1 * nrm(ks[12], (DEPTH, N_NA_HEADS, 2 * NA_WIN_H - 1, 2 * NA_WIN_W - 1), f32),
        'hg_lb_logits': 0.5 * nrm(ks[13], (DEPTH + 1, HG_KEY_WIDTH), f32),
        'hg_norm': 1.0 + 0.05 * nrm(ks[14], (DEPTH, HG_DV), f32),
        'w_router': d ** -0.5 * nrm(ks[15], (DEPTH, d, N_EXPERTS), f32),
        'w_gate': d ** -0.5 * nrm(ks[16], (DEPTH, N_EXPERTS, d, D_EXPERT), f32),
        'w_up': d ** -0.5 * nrm(ks[17], (DEPTH, N_EXPERTS, d, D_EXPERT), f32),
        'w_down': D_EXPERT ** -0.5 * nrm(ks[18], (DEPTH, N_EXPERTS, D_EXPERT, d), f32),
    }

def first_block(x, c, ctx, c_ctx, w_mod, b_mod, g_pre1, g_post1, g_pre2, g_post2, w_in, w_out,
              na_rpb, hg_lb_logits, hg_norm, w_router, w_gate, w_up, w_down):
    bsz = x.shape[0]
    silu_c = jax.nn.silu(c)
    silu_cc = jax.nn.silu(c_ctx)
    lb_all = jnp.cumsum(jax.nn.softmax(hg_lb_logits.astype(jnp.float32), axis=0), axis=0)
    for l in range(DEPTH):
        mod = silu_c @ w_mod[l] + b_mod[l]
        mod_c = silu_cc @ w_mod[l] + b_mod[l]
        sh1, sc1, gt1, sh2, sc2, gt2 = jnp.split(mod[:, None, :], 6, axis=-1)
        sh1c, sc1c, gt1c, sh2c, sc2c, gt2c = jnp.split(mod_c, 6)
        lb = lb_all[l]

        h = modulate(rms_norm(x, g_pre1[l]), sh1, sc1)
        hc = modulate(rms_norm(ctx, g_pre1[l]), sh1c, sc1c)
        qn, kn, vn, qh, zf, zb, ih, gh = split_cols(h @ w_in[l])
        qn_c, kn_c, vn_c, qh_c, zf_c, zb_c, ih_c, gh_c = split_cols(hc @ w_in[l])
        kn_ch = to_heads(kn_c, N_NA_HEADS)
        vn_ch = to_heads(vn_c, N_NA_HEADS)

        na_o = neighbourhood_attention(to_heads(qn, N_NA_HEADS), to_heads(kn, N_NA_HEADS),
                                       to_heads(vn, N_NA_HEADS), kn_ch, vn_ch, na_rpb[l])

        s0 = jnp.zeros((bsz, N_HG_HEADS, HG_DK, HG_DV), jnp.float32)
        o_hc, s_cf, s_cb = hgrn2_bidir(to_heads(qh_c, N_HG_HEADS), to_heads(zf_c, N_HG_HEADS),
                                       to_heads(zb_c, N_HG_HEADS), to_heads(ih_c, N_HG_HEADS), lb, s0, s0)
        o_hl, _, _ = hgrn2_bidir(to_heads(qh, N_HG_HEADS), to_heads(zf, N_HG_HEADS),
                                 to_heads(zb, N_HG_HEADS), to_heads(ih, N_HG_HEADS), lb, s_cf, s_cb)
        hg_o = hgrn2_readout(o_hl, to_heads(gh, N_HG_HEADS), hg_norm[l])

        mix = jnp.concatenate([na_o, hg_o], axis=-1) @ w_out[l]
        x = x + gt1 * rms_norm(mix, g_post1[l])

        h2 = modulate(rms_norm(x, g_pre2[l]), sh2, sc2)
        x = x + gt2 * rms_norm(ec_moe(h2, w_router[l], w_gate[l], w_up[l], w_down[l]), g_post2[l])

        if l < DEPTH - 1:
            o_cna = context_attention(to_heads(qn_c, N_NA_HEADS), kn_ch, vn_ch)
            hg_oc = hgrn2_readout(o_hc, to_heads(gh_c, N_HG_HEADS), hg_norm[l])
            mix_c = jnp.concatenate([from_heads(o_cna), hg_oc], axis=-1) @ w_out[l]
            ctx = ctx + gt1c * rms_norm(mix_c, g_post1[l])
            hc2 = modulate(rms_norm(ctx, g_pre2[l]), sh2c, sc2c)
            ctx = ctx + gt2c * rms_norm(ec_moe(hc2, w_router[l], w_gate[l], w_up[l], w_down[l]), g_post2[l])
    return x


DEPTH_2 = 2

HEAD_DIM = 64
A_HEADS = D_MODEL // (2 * HEAD_DIM)
B_HEADS = D_MODEL // (4 * HEAD_DIM)
C_HEADS = D_MODEL // (2 * HEAD_DIM)
D_HEADS = D_MODEL // (2 * HEAD_DIM)
D_KV_HEADS = D_HEADS // 4
A_W = A_HEADS * HEAD_DIM
B_W = B_HEADS * 2 * HEAD_DIM
C_W = C_HEADS * HEAD_DIM
D_W = D_HEADS * HEAD_DIM
D_KV_W = D_KV_HEADS * HEAD_DIM
EVEN_WIDTH = A_W + B_W
ODD_WIDTH = C_W + D_W
EVEN_SPLITS = (A_W, A_W, A_W, A_W, B_W, B_W, B_W, B_W)
ODD_SPLITS = (C_W, C_W, C_W, C_W, D_W, D_KV_W, D_KV_W, D_KV_W, D_KV_W, D_KV_W, D_KV_W, D_W, 3 * D_HEADS)
EVEN_COLS = 4 * A_W + 4 * B_W
ODD_COLS = 4 * C_W + 2 * D_W + 6 * D_KV_W + 3 * D_HEADS
N_EVEN = (DEPTH_2 + 1) // 2
N_ODD = DEPTH_2 // 2
DILATED_PATTERNS = ((128, 1), (512, 4), (2048, 16))
BAND_BLK = 128
DENSE_BLK = 128
MOBA_BLK = 256
MOBA_TOPK = 3
MOBA_CQ = 32
CMP_LEN = 32
CMP_STRIDE = 16
CMP_HIDDEN = 2 * HEAD_DIM
SLC_BLK = 64
SLC_TOPK = 16
NSA_WINDOW = 512
NSA_CQ = 64


def rmsnorm(x, g):
    xf = x.astype(jnp.float32)
    y = xf * lax.rsqrt(jnp.mean(xf * xf, axis=-1, keepdims=True) + RMS_EPS)
    return (y * g.astype(jnp.float32)).astype(x.dtype)

def alibi_slopes(n):
    return jnp.exp2(-8.0 * jnp.arange(1, n + 1, dtype=jnp.float32) / n)

def split_cols_2(h, sizes):
    out, off = [], 0
    for s in sizes:
        out.append(h[..., off:off + s])
        off += s
    return out

def softmax_parts(s, mask):
    s = jnp.where(mask, s, -jnp.inf)
    m = jnp.max(s, axis=-1, keepdims=True)
    m = jnp.where(jnp.isfinite(m), m, 0.0)
    p = jnp.exp(s - m)
    return p, m, jnp.sum(p, axis=-1, keepdims=True)

def take_blocks(blocks, idx):
    return jax.vmap(jax.vmap(lambda t, i: t[i]))(blocks, idx)

def banded_attention(q, k, v, max_dist, slopes, dist_scale=1):
    N, L, Hq, dh = q.shape
    Hkv = k.shape[2]
    G = Hq // Hkv
    nb = L // BAND_BLK
    nprev = -(-max_dist // BAND_BLK)
    C = (nprev + 1) * BAND_BLK

    def band(t):
        tb = jnp.pad(t.reshape(N, nb, BAND_BLK, Hkv, dh), ((0, 0), (nprev, 0), (0, 0), (0, 0), (0, 0)))
        return jnp.concatenate([tb[:, i:i + nb] for i in range(nprev + 1)], axis=2)

    kb, vb = band(k), band(v)
    qb = q.reshape(N, nb, BAND_BLK, Hkv, G, dh)
    s = jnp.einsum('nbqhgd,nbchd->nbhgqc', qb, kb, preferred_element_type=jnp.float32) * dh ** -0.5
    dist = jnp.arange(BAND_BLK)[:, None] + nprev * BAND_BLK - jnp.arange(C)[None, :]
    kglob = jnp.arange(nb)[:, None] * BAND_BLK - nprev * BAND_BLK + jnp.arange(C)[None, :]
    mask = ((dist >= 0) & (dist <= max_dist))[None, None, None, None] & (kglob >= 0)[None, :, None, None, None, :]
    bias = -slopes.astype(jnp.float32).reshape(Hkv, G, 1, 1) * (dist * dist_scale).astype(jnp.float32)
    p, m, l = softmax_parts(s + bias, mask)
    o = jnp.einsum('nbhgqc,nbchd->nbhgqd', p.astype(v.dtype), vb, preferred_element_type=jnp.float32) / l
    o = o.transpose(0, 1, 4, 2, 3, 5).reshape(N, L, Hq, dh)
    stat = lambda t: t[..., 0].transpose(0, 1, 4, 2, 3).reshape(N, L, Hq)
    return o, stat(m), stat(l)

def dilated_attention(q, k, v, slopes):
    B, S, H, dh = q.shape
    outs, maxes, dens = [], [], []
    for window, dil in DILATED_PATTERNS:
        span = dil * BAND_BLK
        Sp = -(-S // span) * span
        Lp = Sp // dil

        def to_phase(t):
            t = jnp.pad(t, ((0, 0), (0, Sp - S), (0, 0), (0, 0)))
            return jnp.swapaxes(t.reshape(B, Lp, dil, H, dh), 1, 2).reshape(B * dil, Lp, H, dh)

        def from_phase(t):
            rest = t.shape[2:]
            t = jnp.swapaxes(t.reshape(B, dil, Lp, *rest), 1, 2).reshape(B, Sp, *rest)
            return t[:, :S]

        o, m, l = banded_attention(to_phase(q), to_phase(k), to_phase(v), window // dil, slopes, dil)
        outs.append(from_phase(o))
        maxes.append(from_phase(m))
        dens.append(from_phase(l))
    m_all = jnp.stack(maxes)
    w = jnp.stack(dens) * jnp.exp(m_all - jnp.max(m_all, axis=0, keepdims=True))
    w = w / jnp.sum(w, axis=0, keepdims=True)
    return jnp.sum(w[..., None] * jnp.stack(outs), axis=0)

def diff_attention(q, k, v, lam, slopes):
    B, S, H, _, dh = q.shape
    nq = S // DENSE_BLK
    qb = jnp.moveaxis(q.reshape(B, nq, DENSE_BLK, H, 2, dh), 1, 0)
    kpos = jnp.arange(S)
    sl = slopes[None, :, None, None, None]

    def block(args):
        qi, i = args
        s = jnp.einsum('bqhcd,bkhcd->bhcqk', qi, k, preferred_element_type=jnp.float32) * dh ** -0.5
        dist = (i * DENSE_BLK + jnp.arange(DENSE_BLK))[:, None] - kpos[None, :]
        s = jnp.where(dist >= 0, s - sl * dist.astype(jnp.float32), -jnp.inf)
        p = jax.nn.softmax(s, axis=-1)
        a = p[:, :, 0] - lam * p[:, :, 1]
        return jnp.einsum('bhqk,bkhe->bqhe', a.astype(v.dtype), v, preferred_element_type=jnp.float32)

    o = lax.map(block, (qb, jnp.arange(nq)))
    return jnp.moveaxis(o, 0, 1).reshape(B, S, H, 2 * dh)

def moba_attention(q, k, v, slopes):
    B, S, H, dh = q.shape
    Sp = -(-S // MOBA_BLK) * MOBA_BLK
    pad = ((0, 0), (0, Sp - S), (0, 0), (0, 0))
    q, k, v = jnp.pad(q, pad), jnp.pad(k, pad), jnp.pad(v, pad)
    nblk = Sp // MOBA_BLK
    kbh = k.reshape(B, nblk, MOBA_BLK, H, dh).transpose(0, 3, 1, 2, 4)
    vbh = v.reshape(B, nblk, MOBA_BLK, H, dh).transpose(0, 3, 1, 2, 4)
    kmean = jnp.mean(kbh.astype(jnp.float32), axis=3)
    gate = jnp.einsum('bshd,bhnd->bhsn', q.astype(jnp.float32), kmean)
    past = jnp.arange(nblk)[None, :] < (jnp.arange(Sp) // MOBA_BLK)[:, None]
    n_sel = min(MOBA_TOPK, nblk)
    _, idx = lax.top_k(jnp.where(past, gate, -jnp.inf), n_sel)
    nch = Sp // MOBA_CQ
    qs = jnp.moveaxis(q.reshape(B, nch, MOBA_CQ, H, dh), 1, 0)
    idxs = idx.reshape(B, H, nch, MOBA_CQ, n_sel).transpose(2, 0, 1, 3, 4)
    scale = dh ** -0.5

    def chunk(args):
        qc, ic, c = args
        qpos = c * MOBA_CQ + jnp.arange(MOBA_CQ)
        own = (c * MOBA_CQ) // MOBA_BLK
        k_own = lax.dynamic_index_in_dim(kbh, own, axis=2, keepdims=False)
        v_own = lax.dynamic_index_in_dim(vbh, own, axis=2, keepdims=False)
        k_sel = take_blocks(kbh, ic)
        v_sel = take_blocks(vbh, ic)
        kpos_sel = ic[..., None] * MOBA_BLK + jnp.arange(MOBA_BLK)
        s_sel = jnp.einsum('bqhd,bhqnkd->bhqnk', qc, k_sel, preferred_element_type=jnp.float32) * scale
        s_sel = s_sel - slopes[None, :, None, None, None] * (qpos[None, None, :, None, None] - kpos_sel).astype(jnp.float32)
        valid_sel = jnp.broadcast_to((ic < own)[..., None], s_sel.shape)
        kpos_own = own * MOBA_BLK + jnp.arange(MOBA_BLK)
        s_own = jnp.einsum('bqhd,bhkd->bhqk', qc, k_own, preferred_element_type=jnp.float32) * scale
        s_own = s_own - slopes[None, :, None, None] * (qpos[:, None] - kpos_own[None, :]).astype(jnp.float32)
        mask_own = jnp.broadcast_to(kpos_own[None, :] <= qpos[:, None], s_own.shape)
        nk = n_sel * MOBA_BLK
        s = jnp.concatenate([s_sel.reshape(B, H, MOBA_CQ, nk), s_own], axis=-1)
        mask = jnp.concatenate([valid_sel.reshape(B, H, MOBA_CQ, nk), mask_own], axis=-1)
        p = jax.nn.softmax(jnp.where(mask, s, -jnp.inf), axis=-1)
        p_sel = p[..., :nk].reshape(B, H, MOBA_CQ, n_sel, MOBA_BLK).astype(v.dtype)
        p_own = p[..., nk:].astype(v.dtype)
        return (jnp.einsum('bhqnk,bhqnkd->bqhd', p_sel, v_sel, preferred_element_type=jnp.float32)
                + jnp.einsum('bhqk,bhkd->bqhd', p_own, v_own, preferred_element_type=jnp.float32))

    o = lax.map(chunk, (qs, idxs, jnp.arange(nch)))
    return jnp.moveaxis(o, 0, 1).reshape(B, Sp, H, dh)[:, :S]

def compress_blocks(t, pe, w1, w2):
    B, S, Hkv, dh = t.shape
    n_cmp = (S - CMP_LEN) // CMP_STRIDE + 1
    r = CMP_LEN // CMP_STRIDE
    ch = t.reshape(B, S // CMP_STRIDE, CMP_STRIDE, Hkv, dh)
    blocks = jnp.concatenate([ch[:, i:i + n_cmp] for i in range(r)], axis=2) + pe[None, None, :, None, :]
    flat = blocks.transpose(0, 1, 3, 2, 4).reshape(B, n_cmp, Hkv, CMP_LEN * dh)
    return jax.nn.silu(flat @ w1) @ w2

def nsa_attention(q, k_cmp, v_cmp, k_slc, v_slc, k_win, v_win, gates, slopes):
    B, S, Hq, dh = q.shape
    Hkv = k_slc.shape[2]
    G = Hq // Hkv
    n_cmp = k_cmp.shape[1]
    n_slc = S // SLC_BLK
    n_top = min(SLC_TOPK, n_slc)
    scale = dh ** -0.5
    cstart = jnp.arange(n_cmp) * CMP_STRIDE
    cend = cstart + CMP_LEN - 1
    sstart = jnp.arange(n_slc) * SLC_BLK
    cmp_in_slc = ((cstart[:, None] <= sstart[None, :] + SLC_BLK - 1) & (cend[:, None] >= sstart[None, :])).astype(jnp.float32)
    ksb = k_slc.reshape(B, n_slc, SLC_BLK, Hkv, dh).transpose(0, 3, 1, 2, 4)
    vsb = v_slc.reshape(B, n_slc, SLC_BLK, Hkv, dh).transpose(0, 3, 1, 2, 4)
    sl = slopes.reshape(Hkv, G)
    nch = S // NSA_CQ
    qs = jnp.moveaxis(q.reshape(B, nch, NSA_CQ, Hkv, G, dh), 1, 0)
    jb = jnp.arange(n_slc)[None, :]

    def chunk(args):
        qc, c = args
        qpos = c * NSA_CQ + jnp.arange(NSA_CQ)
        s = jnp.einsum('bqhgd,bnhd->bhgqn', qc, k_cmp, preferred_element_type=jnp.float32) * scale
        s = s - sl[:, :, None, None] * (qpos[:, None] - cend[None, :]).astype(jnp.float32)
        p, _, l = softmax_parts(s, cend[None, :] <= qpos[:, None])
        p = p / jnp.where(l > 0, l, 1.0)
        o_cmp = jnp.einsum('bhgqn,bnhd->bqhgd', p.astype(v_cmp.dtype), v_cmp, preferred_element_type=jnp.float32)
        imp = jnp.einsum('bhgqn,nj->bhqj', p, cmp_in_slc)
        qb = (qpos // SLC_BLK)[:, None]
        forced = (jb == 0) | (jb == qb) | (jb == qb - 1)
        imp = jnp.where(forced, jnp.inf, jnp.where(jb > qb, -jnp.inf, imp))
        _, idx = lax.top_k(imp, n_top)
        k_sel = take_blocks(ksb, idx)
        v_sel = take_blocks(vsb, idx)
        dist = qpos[None, None, :, None, None] - (idx[..., None] * SLC_BLK + jnp.arange(SLC_BLK))
        s2 = jnp.einsum('bqhgd,bhqnkd->bhgqnk', qc, k_sel, preferred_element_type=jnp.float32) * scale
        s2 = s2 - sl[None, :, :, None, None, None] * dist[:, :, None].astype(jnp.float32)
        mask2 = jnp.broadcast_to((dist >= 0)[:, :, None], s2.shape)
        nk = n_top * SLC_BLK
        p2 = jax.nn.softmax(jnp.where(mask2, s2, -jnp.inf).reshape(B, Hkv, G, NSA_CQ, nk), axis=-1)
        p2 = p2.reshape(B, Hkv, G, NSA_CQ, n_top, SLC_BLK).astype(v_sel.dtype)
        o_slc = jnp.einsum('bhgqnk,bhqnkd->bqhgd', p2, v_sel, preferred_element_type=jnp.float32)
        return o_cmp, o_slc

    o_cmp, o_slc = lax.map(chunk, (qs, jnp.arange(nch)))
    o_cmp = jnp.moveaxis(o_cmp, 0, 1).reshape(B, S, Hq, dh)
    o_slc = jnp.moveaxis(o_slc, 0, 1).reshape(B, S, Hq, dh)
    o_win, _, _ = banded_attention(q, k_win, v_win, NSA_WINDOW - 1, slopes)
    g = gates.astype(jnp.float32)
    return g[..., 0:1] * o_cmp + g[..., 1:2] * o_slc + g[..., 2:3] * o_win

def even_layer(x, ln, w_in, qkn, lam, subln, w_out, layer):
    B, S, _ = x.shape
    h = rmsnorm(x, ln)
    aq, ak, av, az, bq, bk, bv, bz = split_cols_2(h @ w_in, EVEN_SPLITS)
    heads = lambda t, n: t.reshape(B, S, n, -1)
    oa = dilated_attention(rmsnorm(heads(aq, A_HEADS), qkn[0]), rmsnorm(heads(ak, A_HEADS), qkn[1]),
                           heads(av, A_HEADS), alibi_slopes(A_HEADS)).astype(x.dtype)
    bq = rmsnorm(bq.reshape(B, S, B_HEADS, 2, HEAD_DIM), qkn[2])
    bk = rmsnorm(bk.reshape(B, S, B_HEADS, 2, HEAD_DIM), qkn[3])
    lam_init = 0.8 - 0.6 * math.exp(-0.3 * layer)
    lf = lam.astype(jnp.float32)
    lam_f = jnp.exp(jnp.sum(lf[0] * lf[1])) - jnp.exp(jnp.sum(lf[2] * lf[3])) + lam_init
    ob = diff_attention(bq, bk, heads(bv, B_HEADS), lam_f, alibi_slopes(B_HEADS))
    ob = (rmsnorm(ob, subln) * (1.0 - lam_init)).astype(x.dtype)
    mixed = jnp.concatenate([oa.reshape(B, S, A_W) * jax.nn.silu(az),
                             ob.reshape(B, S, B_W) * jax.nn.silu(bz)], axis=-1)
    return x + mixed @ w_out

def odd_layer(x, ln, w_in, qkn, phi_pe, phi_w1, phi_w2, w_out):
    B, S, _ = x.shape
    h = rmsnorm(x, ln)
    cq, ck, cv, cz, dq, dkc, dvc, dks, dvs, dkw, dvw, dz, dg = split_cols_2(h @ w_in, ODD_SPLITS)
    heads = lambda t, n: t.reshape(B, S, n, HEAD_DIM)
    oc = moba_attention(rmsnorm(heads(cq, C_HEADS), qkn[0]), rmsnorm(heads(ck, C_HEADS), qkn[1]),
                        heads(cv, C_HEADS), alibi_slopes(C_HEADS)).astype(x.dtype)
    k_cmp = rmsnorm(compress_blocks(heads(dkc, D_KV_HEADS), phi_pe[0], phi_w1[0], phi_w2[0]), qkn[3])
    v_cmp = compress_blocks(heads(dvc, D_KV_HEADS), phi_pe[1], phi_w1[1], phi_w2[1])
    od = nsa_attention(rmsnorm(heads(dq, D_HEADS), qkn[2]), k_cmp, v_cmp,
                       rmsnorm(heads(dks, D_KV_HEADS), qkn[4]), heads(dvs, D_KV_HEADS),
                       rmsnorm(heads(dkw, D_KV_HEADS), qkn[5]), heads(dvw, D_KV_HEADS),
                       jax.nn.sigmoid(dg.reshape(B, S, D_HEADS, 3)), alibi_slopes(D_HEADS)).astype(x.dtype)
    mixed = jnp.concatenate([oc.reshape(B, S, C_W) * jax.nn.silu(cz),
                             od.reshape(B, S, D_W) * jax.nn.silu(dz)], axis=-1)
    return x + mixed @ w_out

def second_inputs(seed: int = 0) -> dict:
    key = jax.random.key(seed)
    ks = jax.random.split(key, 14)
    nrm = lambda k, shape: jax.random.normal(k, shape, jnp.float32)
    w = lambda k, shape, fan_in: nrm(k, shape) * fan_in ** -0.5
    gain = lambda k, shape: 1.0 + 0.05 * nrm(k, shape)
    return {
        'x': nrm(ks[0], (BATCH, SEQ, D_MODEL)),
        'ln_e': gain(ks[1], (N_EVEN, D_MODEL)),
        'w_in_e': w(ks[2], (N_EVEN, D_MODEL, EVEN_COLS), D_MODEL),
        'qkn_e': gain(ks[3], (N_EVEN, 4, HEAD_DIM)),
        'lam_e': 0.1 * nrm(ks[4], (N_EVEN, 4, HEAD_DIM)),
        'subln_e': gain(ks[5], (N_EVEN, 2 * HEAD_DIM)),
        'w_out_e': w(ks[6], (N_EVEN, EVEN_WIDTH, D_MODEL), EVEN_WIDTH),
        'ln_o': gain(ks[7], (N_ODD, D_MODEL)),
        'w_in_o': w(ks[8], (N_ODD, D_MODEL, ODD_COLS), D_MODEL),
        'qkn_o': gain(ks[9], (N_ODD, 6, HEAD_DIM)),
        'phi_pe': 0.1 * nrm(ks[10], (N_ODD, 2, CMP_LEN, HEAD_DIM)),
        'phi_w1': w(ks[11], (N_ODD, 2, CMP_LEN * HEAD_DIM, CMP_HIDDEN), CMP_LEN * HEAD_DIM),
        'phi_w2': w(ks[12], (N_ODD, 2, CMP_HIDDEN, HEAD_DIM), CMP_HIDDEN),
        'w_out_o': w(ks[13], (N_ODD, ODD_WIDTH, D_MODEL), ODD_WIDTH),
    }

def second_block(x, ln_e, w_in_e, qkn_e, lam_e, subln_e, w_out_e, ln_o, w_in_o, qkn_o,
              phi_pe, phi_w1, phi_w2, w_out_o):
    for layer in range(DEPTH_2):
        i = layer // 2
        if layer % 2 == 0:
            x = even_layer(x, ln_e[i], w_in_e[i], qkn_e[i], lam_e[i], subln_e[i], w_out_e[i], layer)
        else:
            x = odd_layer(x, ln_o[i], w_in_o[i], qkn_o[i], phi_pe[i], phi_w1[i], phi_w2[i], w_out_o[i])
    return x


def setup_inputs(seed=0):
    out = dict(first_inputs(seed))
    for name, value in second_inputs(seed + 1).items():
        if name != "x":
            out[name + "_2"] = value
    return out


def reference(
    x, c, ctx, c_ctx, w_mod, b_mod, g_pre1, g_post1, g_pre2, g_post2, w_in, w_out, na_rpb,
    hg_lb_logits, hg_norm, w_router, w_gate, w_up, w_down, ln_e_2, w_in_e_2, qkn_e_2, lam_e_2,
    subln_e_2, w_out_e_2, ln_o_2, w_in_o_2, qkn_o_2, phi_pe_2, phi_w1_2, phi_w2_2, w_out_o_2,
):
    x = first_block(
        x, c, ctx, c_ctx, w_mod, b_mod, g_pre1, g_post1, g_pre2, g_post2, w_in, w_out, na_rpb,
        hg_lb_logits, hg_norm, w_router, w_gate, w_up, w_down,
    )
    return second_block(
        x, ln_e_2, w_in_e_2, qkn_e_2, lam_e_2, subln_e_2, w_out_e_2, ln_o_2, w_in_o_2, qkn_o_2,
        phi_pe_2, phi_w1_2, phi_w2_2, w_out_o_2,
    )


_drawn_inputs = setup_inputs


def setup_inputs(seed=0):
    import zlib

    import numpy as np

    out = dict(_drawn_inputs(seed))
    spreads = {}
    factors = {'g_post2': 3.341,
     'qkn_e_2': 3.253,
     'subln_e_2': 3.26,
     'ln_o_2': 3.444,
     'qkn_o_2': 6.894,
     'phi_pe_2': 5.562}
    for name, (base, spread) in spreads.items():
        noise = np.random.default_rng([zlib.crc32(name.encode()), seed]).standard_normal(out[name].shape)
        drawn = base * np.exp(spread * noise) if base else spread * noise
        out[name] = jnp.asarray(drawn.astype(out[name].dtype))
    for name, factor in factors.items():
        out[name] = (out[name] * factor).astype(out[name].dtype)
    return out
```

```python
import numpy as np
import concourse.bass as bass
from concourse import mybir
from contextlib import ExitStack

FP32 = mybir.dt.float32
I32 = mybir.dt.int32
ALU = mybir.AluOpType
ACT = mybir.ActivationFunctionType
AX = mybir.AxisListType.X

D = 1024
T = 256
KC = D // 128
EPS = 1e-6
NEG = -1e30
E = 16
CAP = 2 * T // E
F = 2752
FG = F // 4
FH = FG // 2
FS = [128] * (FG // 128) + [FG % 128]
LAM_INIT = 0.2
HG = 4
CH = 32
NCMP = (T - 32) // 16 + 1
GU_SLOTS, GU_W = 8, F
DN_SLOTS, DN_W = 4, 2 * D
WG_SLOTS, WG_W = 3, KC * 512

W_IN_ORDER = [("zf", 4), ("zb", 5), ("qh", 3), ("ih", 6), ("gh", 7), ("kn", 1), ("vn", 2), ("qn", 0)]
GROUPS = ([("w_mod", [(512 * i, 512)]) for i in range(12)]
          + [("w_in", [(512 * c, 512)]) for _, c in W_IN_ORDER]
          + [("w_out", [(512 * i, 512)]) for i in range(2)]
          + [("w_in_e_2", [(512 * i, 512)]) for i in range(8)]
          + [("w_out_e_2", [(512 * i, 512)]) for i in range(2)]
          + [("w_in_o_2", [(512 * i, 512)]) for i in range(6)]
          + [("w_in_o_2", [(3328, 512)]), ("w_in_o_2", [(3072, 256), (3840, 24)])]
          + [("phi_w1_2", 0), ("phi_w1_2", 1)]
          + [("w_out_o_2", [(512 * i, 512)]) for i in range(2)])
G_MOD, G_IN, G_OUT, G_IN_E, G_OUT_E, G_IN_O, G_PHI, G_OUT_O = 0, 12, 20, 22, 30, 32, 40, 42


def constants():
    t = np.arange(T)
    p = np.arange(128)
    f32 = np.float32
    out = {"ident": np.eye(128, dtype=f32)}
    inv = (f32(10000.0) ** (-np.arange(0, 32, 2, dtype=f32) / f32(32))).astype(f32)
    ang = np.stack([(t // 64).astype(f32)[:, None] * inv, (t % 64).astype(f32)[:, None] * inv], 1)
    cos, sin = np.cos(ang).astype(f32), np.sin(ang).astype(f32)
    out["rope_cos"] = np.stack([cos, cos], 2).reshape(T, 64)
    out["rope_sin"] = np.stack([-sin, sin], 2).reshape(T, 64)
    qc, kc = np.arange(64)[:, None], np.arange(64)[None, :]
    w0 = np.clip(qc - 8, 0, 48)
    win = (kc >= w0) & (kc < w0 + 16)
    out["na_keep"] = np.tile(win.astype(f32), (2, 1))
    out["na_mask"] = np.tile(np.where(win, 0, NEG).astype(f32), (2, 1))
    dist = t[:, None] - t[None, :]
    causal = dist >= 0
    slopes = [2.0 ** -(h + 1) for h in range(8)]
    mult = causal * 1.0 + (causal & (dist % 4 == 0)) + (causal & (dist % 16 == 0))
    mult -= (dist > 128) * 1.0 * causal
    alibi = np.stack([np.where(causal, -s * dist, NEG) for s in slopes])
    dil = np.stack([np.where(mult > 0, -s * dist + np.log(np.maximum(mult, 1)), NEG) for s in slopes])

    def tiles(a):
        return np.concatenate([a[:, :128, :128], a[:, 128:, :]], 2).transpose(1, 0, 2).astype(f32)
    out["alibi"], out["dilated"] = tiles(alibi), tiles(dil)
    reset = np.ones((128, 2 * T), f32)
    reset[:, ::CH] = 0
    out["scan_reset"] = reset
    same = p[:, None] // CH == p[None, :] // CH
    fwd, bwd = same & (p[:, None] <= p[None, :]), same & (p[:, None] >= p[None, :])
    out["chunk_mask"] = np.stack([fwd, fwd, bwd, bwd], 1).astype(np.int32)
    out["slot_iota"] = np.tile(np.arange(1, CAP + 1, dtype=f32), (128, 1))
    out["ones"] = np.ones((128, 256), f32)
    cend = np.arange(16) * 16 + 31
    dc = t[:, None] - cend[None, :]
    ok = (dc >= 0) & (np.arange(16) < NCMP)[None, :]
    heads = np.array([[2 * hp + par for hp in range(4)] for par in range(2)])
    ca = np.where(ok[:, None, None, :], -np.array(slopes)[heads][None, :, :, None] * dc[:, None, None, :], NEG)
    out["cmp_bias"] = ca.reshape(2, 128, 128).transpose(1, 0, 2).astype(f32)
    out["cmp_keep"] = np.broadcast_to(ok[:, None, :], (T, 8, 16)).reshape(2, 128, 128).transpose(1, 0, 2).astype(f32)
    out["block_diag"] = ((2 * (p // 16 % 4) + p // 64)[:, None] == np.arange(8)[None, :]).astype(f32)
    sel = np.zeros((2, 128), f32)
    sel[0] = 1
    out["first_row"] = sel
    return {k: np.ascontiguousarray(v) for k, v in out.items()}


def build(nc, A, out):
    ctx = ExitStack()

    def sb(name, shape, dt=FP32):
        return ctx.enter_context(nc.sbuf_tensor(name, shape, dt))

    sems = {}

    def S(name):
        if name not in sems:
            sems[name] = ctx.enter_context(nc.semaphore(name))
        return sems[name]

    y_dram = nc.dram_tensor("y_scratch", (E * CAP, D), FP32).ap()

    DIAG = 2 * 64 - 1
    diag = nc.dram_tensor("rpb_rows", (8, 7, 64, DIAG), FP32).ap()

    X = sb("X", [128, 2, D])
    HT = sb("HT", [128, KC * 512])
    WG = sb("WG", [128, WG_SLOTS, WG_W])
    TAB = sb("TAB", [128, 4096])
    BIG = sb("BIG", [128, GU_SLOTS * GU_W + DN_SLOTS * DN_W])
    GP2 = sb("GP2", [128, D])
    ident = sb("ident", [128, 128])
    cols = sb("cols", [128, 56])
    modc = sb("modc", [128, 48, 2])
    sc = sb("sc", [128, 512])
    BC = sb("BC", [128, 1152])
    PS = ctx.enter_context(nc.psum_tensor("PS", [128, 8, 512], FP32))

    def view(t, off, *dims):
        n = int(np.prod(dims))
        ap = t[:, off:off + n]
        if len(dims) == 2:
            ap = ap.rearrange("p (a b) -> p a b", b=dims[1])
        elif len(dims) == 3:
            ap = ap.rearrange("p (a b c) -> p a b c", b=dims[1], c=dims[2])
        elif len(dims) == 4:
            ap = ap.rearrange("p (a b c d) -> p a b c d", b=dims[1], c=dims[2], d=dims[3])
        return ap

    def laid(t, at=0):
        pos = [at]

        def place(*dims):
            n = int(np.prod(dims))
            pos[0] += n
            assert pos[0] <= t.shape[1], (pos[0], t.shape)
            return view(t, pos[0] - n, *dims)
        place.pos = pos
        return place

    s_at = laid(sc)
    stat = s_at(64)
    csil = s_at(8, 2)
    A1, A1c, A2 = s_at(8), s_at(8), s_at(8)
    lb, oml = s_at(4), s_at(4)
    lbt = s_at(12)
    negm, lsum, rls = s_at(8), s_at(96), s_at(96)
    lamt = s_at(8)
    aff = s_at(2, E)
    amax = s_at(2)
    best8 = s_at(8)

    bc_at = laid(BC)
    b_hg, b_qe, b_sub, b_qo, b_lam = bc_at(128), bc_at(4, 64), bc_at(128), bc_at(6, 64), bc_at(4, 64)

    at = laid(BIG)
    GP1 = at(D)
    z = at(2, HG, 2 * T)
    qh = at(HG, T)
    ih = at(4, 512)
    gh = at(2, 512)
    kn = at(4, 512)
    vn = at(4, 512)
    qn = at(2, 512)
    mixcat = at(2, D)
    free1 = at.pos[0]
    a0 = laid(BIG, D)
    modrow, bmod = a0(6 * D), a0(6 * D)
    rows, xctx, xn = a0(128), a0(2, D), a0(4, D)
    first_row = a0(128)
    ah = laid(BIG, free1)
    fgt, bcum, kk = ah(2, 512), ah(2, 512), ah(2, 512)
    eb, enb, qdec, kdec = ah(2, T), ah(2, T), ah(2, T), ah(2, T)
    kend = ah(2, 512)
    kendT, vbd = view(HT, 0, 2, 4, 128), view(HT, 1024, 4, 4, 128)
    aT = ah(4, 128)
    states = ah(2, 16, 128)
    decay = ah(2, 16)
    reset = ah(512)
    cmask = ah(4, 128)
    rcos, rsin, na_keep, na_mask = ah(2, 64), ah(2, 64), ah(64), ah(64)
    w_rt, ones, slot = ah(KC, E), ah(T), ah(CAP)
    an = laid(BIG, free1)
    qr, kr, rt = an(2, 512), an(2, 512), an(512)
    pbuf, ptbuf = an(2, 512), an(2, 512)
    qrT, krT, qT, kcT = (view(HT, 1024 * i, 4, T) for i in range(4))
    am = laid(BIG, free1)
    mixT, mixo = am(KC, T), am(2, D)
    xn2, h2T = am(2, D), am(KC, T)
    lg = am(2, E)
    affT, work, posm, pos = am(T), am(T), am(T), am(T)
    posT = am(2, E)
    oh, ohg = am(2, E, CAP), am(2, E, CAP)
    xs = view(HT, 0, KC, 512)
    tm = laid(TAB)
    sgt, xse, sig, hid = tm(4, T), tm(KC, CAP), tm(FG), tm(FG)
    hidT, ysb = tm(6, 128), tm(256)
    GU = view(BIG, 0, GU_SLOTS, GU_W)
    DN = view(BIG, GU_SLOTS * GU_W, DN_SLOTS, 2, D)
    na_tab = view(TAB, 0, 8, 2, T)

    ae = laid(BIG)
    ybuf = view(BIG, 0, 4, D)
    moeo = view(BIG, 4 * D, 2, D)
    qk = ae(4, 2, 512)
    vv, zz = ae(2, 2, 512), ae(2, 2, 512)
    tT = ae(4, 4, T)
    mixe = ae(2, D)
    mixeT = ae(KC, T)
    pb2, pt2 = ae(2, 512), ae(2, 512)
    tab_a, tab_c = ae(8, 384), ae(8, 384)
    t2 = ae(4096)
    xn3 = view(BIG, ae.pos[0] - 4096, 4, D)
    free2 = ae.pos[0]
    hTe = view(HT, 0, KC, T)
    mixo2 = view(HT, 2048, 2, D)
    ckv = view(BIG, 3 * 1024, 2, 512)
    kw = view(TAB, 0, 2, 280)
    to = laid(TAB, 560)
    gates = to(2, 24)
    dup = to(2, 2, 256)
    pe2, peT = to(2, 128), to(2, 32)
    w2 = to(2, 64)
    hidk, hidv = to(2, 16), to(8, 16)
    kcmp, kcmpT = to(2, 128), to(2, 16)
    cbias, ckeep = to(2, 128), to(2, 128)
    bdiag = to(8)
    ocmp = view(TAB, 560 + 2500, 2, 512)
    assert to.pos[0] <= 3060, to.pos[0]
    tab_a_off = 4096 + 2048 + 2048 + 4096 + 2048 + 2048 + 1024 + 1024
    ab = view(BIG, tab_a_off, 2, 32, 16)
    kcvT = view(BIG, tab_a_off + 1024, 2, T)
    vbd2 = view(BIG, tab_a_off + 1536, 8, 64)
    pc = view(BIG, tab_a_off + 2048, 2, 128)
    pcT = view(BIG, tab_a_off + 2304, 2, 128)
    dupT = view(BIG, tab_a_off + 2560, 2, 256)
    dupTw = view(HT, 2048, 2, 256)

    def bank(i):
        return PS[:, i, :]

    def unit(lq, rk, tab, vblocks, outp, l, first=False, last=False, wait=None):
        return dict(s=[(0, lq, rk)] if not isinstance(lq, list) else lq, tab=tab, v=vblocks,
                    out=outp, l=l, first=first, last=last, wait=wait)

    def half(h):
        return slice(64 * (h % 2), 64 * (h % 2) + 64)

    def na_units():
        r = []
        for qt in range(2):
            for h in range(8):
                q = slice(128 * qt, 128 * qt + 128)
                s = [(0, qrT[half(h), h // 2, q], krT[half(h), h // 2, :]),
                     (T, qT[half(h), h // 2, q], kcT[half(h), h // 2, :])]
                v = [vn[:, b, 64 * h:64 * h + 64] for b in range(4)]
                r.append(dict(s=s, tab=na_tab[:, h, qt, :], v=v, c=64 * h, w=64, n=512,
                              last=h == 7, wait=None))
        return r

    def causal_units(qT_, kT_, tabs, vals, heads, per, width, group):
        r = []
        for qt in range(2):
            for i, (qi, ki, ti, vi) in enumerate(heads):
                q = slice(128 * qt, 128 * qt + 128)
                n = 128 * (qt + 1)
                s = [(0, qT_[half(qi), qi // 2, q], kT_(qi, ki)[:, 0:n])]
                tab = tabs[:, ti, 0:128] if qt == 0 else tabs[:, ti, 128:384]
                v = [vals[:, b, width * vi:width * vi + width] for b in range(qt + 1)]
                r.append(dict(s=s, tab=tab, v=v, c=width * (i % per), w=width, n=n,
                              last=i % per == per - 1, wait=None))
        return r

    aqT, akT, bqT, bkT = (tT[:, i] for i in range(4))
    cqT, ckT, dqT = aqT, akT, bqT
    av, bv = vv[:, 0], vv[:, 1]
    same_head = lambda t: (lambda qi, ki: t[half(ki), ki // 2, :])
    shared_head = lambda t: (lambda qi, ki: t[half(qi), ki, :])
    ATT = {
        "na": na_units(),
        "a": causal_units(aqT, same_head(akT), tab_a, av, [(h, h, h, h) for h in range(8)], 8, 64, 0),
        "b": causal_units(bqT, same_head(bkT), tab_c, bv,
                          [(2 * h + c, 2 * h + c, 2 * h + 1, h) for h in range(4) for c in range(2)], 4, 128, 0),
        "c": causal_units(cqT, same_head(ckT), tab_c, vv[:, 0], [(h, h, h, h) for h in range(8)], 8, 64, 0),
        "s": causal_units(dqT, shared_head(dupT), tab_c, ckv[:, :, 384:512],
                          [(h, h // 4, h, h // 4) for h in range(8)], 8, 64, 0),
        "w": causal_units(dqT, shared_head(dupTw), tab_c, kw[:, :, 128:256],
                          [(h, h // 4, h, h // 4) for h in range(8)], 8, 64, 0),
    }
    n0 = g0 = 0
    for k in ("na", "a", "b", "c", "s", "w"):
        for u in ATT[k]:
            u["i"], u["g"] = n0, g0
            n0 += 1
            g0 += u["last"]
    PB = {"na": (pbuf, ptbuf)}

    PROJ = []
    dest = {"zf": z[:, 0], "zb": z[:, 1], "qh": qh, "ih": ih, "gh": gh, "kn": kn, "vn": vn, "qn": qn}
    for n, (name, _) in enumerate(W_IN_ORDER):
        g = G_IN + n
        if name in ("zf", "zb", "qh"):
            for h in range(HG):
                PROJ.append((g, "chan", h, T if name == "qh" else 2 * T, dest[name][:, h, :],
                             ACT.Copy if name == "qh" else ACT.Sigmoid, 1.0))
        else:
            for t in range(2 if name in ("gh", "qn") else 4):
                PROJ.append((g, "tok", t, 512, dest[name][:, t, :],
                             ACT.Sigmoid if name == "gh" else ACT.Copy, 0.125 if name == "qn" else 1.0))
    P_IN = (0, len(PROJ))

    def outs(g0_, dst):
        a = len(PROJ)
        for g in range(2):
            for t in range(2):
                PROJ.append((g0_ + g, "tok", t, 512, dst[:, t, 512 * g:512 * g + 512], ACT.Copy, 1.0))
        return a, len(PROJ)
    P_OUT = outs(G_OUT, mixo)
    P_E0 = len(PROJ)
    for g, (dst, fn) in enumerate([(qk[:, 0], ACT.Copy), (qk[:, 1], ACT.Copy), (vv[:, 0], ACT.Copy), (zz[:, 0], ACT.Silu),
                                   (qk[:, 2], ACT.Copy), (qk[:, 3], ACT.Copy), (vv[:, 1], ACT.Copy), (zz[:, 1], ACT.Silu)]):
        for t in range(2):
            PROJ.append((G_IN_E + g, "tok", t, 512, dst[:, t, :], fn, 1.0))
    P_E = (P_E0, len(PROJ))
    P_OUT_E = outs(G_OUT_E, mixo2)
    P_O0 = len(PROJ)
    for g, (dst, fn) in enumerate([(qk[:, 0], ACT.Copy), (qk[:, 1], ACT.Copy), (vv[:, 0], ACT.Copy), (zz[:, 0], ACT.Silu),
                                   (qk[:, 2], ACT.Copy), (ckv, ACT.Copy), (zz[:, 1], ACT.Silu), (kw, ACT.Copy)]):
        for t in range(2):
            PROJ.append((G_IN_O + g, "tok", t, 280 if g == 7 else 512, dst[:, t, :], fn, 1.0))
    P_O = (P_O0, len(PROJ))
    P_OUT_O = outs(G_OUT_O, mixo2)

    FILLS = []

    def fill(parts, dst, rows_=128):
        FILLS.append((parts, dst, rows_))
        return len(FILLS)

    def tok_fills(src, dst):
        for j in range(4):
            fill([(src[:, t, 128 * k:128 * k + 128], 256 * (k % 2) + 128 * t)
                  for k in (2 * j, 2 * j + 1) for t in range(2)], dst[:, 2 * j:2 * j + 2, :])

    def head_fills(src, dst):
        for j in range(2):
            fill([(src[:, t, 128 * k:128 * k + 128], 256 * (k % 2) + 128 * t)
                  for k in (2 * j, 2 * j + 1) for t in range(2)], dst[:, 2 * j:2 * j + 2, :])
    marks = {}

    def begin(name):
        marks[name] = [len(FILLS), None]

    def end(name):
        marks[name][1] = len(FILLS)
    for h in range(HG):
        begin(f"kend{h}")
        for d in range(2):
            fill([(kend[:, d, 128 * t:128 * t + 128], 128 * t) for t in range(4)], kendT[:, d])
        end(f"kend{h}")
    begin("na")
    for src, dst in ((qr, qrT), (kr, krT), (qn, qT), (kn[:, 2:4], kcT)):
        head_fills(src, dst)
    end("na")
    begin("mix"), tok_fills(mixcat, mixT), end("mix")
    begin("h2"), tok_fills(xn2, h2T), end("h2")
    begin("aff"), fill([(aff[:, t, :], 128 * t) for t in range(2)], affT[0:E, :], E), end("aff")
    begin("pos"), fill([(posm[0:E, 128 * t:128 * t + 128], E * t) for t in range(2)], posT), end("pos")
    begin("sg")
    for j in range(2):
        fill([(ohg[:, t, 4 * b:4 * b + 4, :].rearrange("p a b -> p (a b)"), 256 * (b % 2) + 128 * t) for b in (2 * j, 2 * j + 1) for t in range(2)],
             sgt[:, 2 * j:2 * j + 2, :])
    end("sg")
    begin("he"), tok_fills(xn3, hTe), end("he")
    begin("qke")
    for i in range(4):
        head_fills(qk[:, i], tT[:, i])
    end("qke")
    begin("mixe"), tok_fills(mixe, mixeT), end("mixe")
    begin("ho"), tok_fills(xn3, hTe), end("ho")
    begin("cmp")
    fill([(ckv[:, t, 128 * s:128 * s + 128], 256 * s + 128 * t) for s in range(2) for t in range(2)], kcvT)
    fill([(pe2[0:32, s], 32 * s) for s in range(2)], peT)
    end("cmp")
    begin("qko")
    for i in range(3):
        head_fills(qk[:, i], tT[:, i])
    for i, dst in ((0, dupT), (1, dupTw)):
        fill([(dup[:, i, t, 128 * k:128 * k + 128], 256 * k + 128 * t) for k in range(2) for t in range(2)], dst)
    end("qko")
    begin("kcmp"), fill([(kcmp[0:16, h], 16 * h) for h in range(2)], kcmpT), end("kcmp")
    begin("pc"), fill([(pc[:, t, :], 128 * t) for t in range(2)], pcT), end("pc")
    begin("mixo"), tok_fills(mixe, mixeT), end("mixo")

    need, landed = [], [0] * WG_SLOTS
    for n, (_, what) in enumerate(GROUPS):
        landed[n % WG_SLOTS] += 16 * (2 if isinstance(what, int) else len(what))
        need.append(landed[n % WG_SLOTS])
    last_unit = {}
    for n, u in enumerate(PROJ):
        last_unit[u[0]] = n
    used_by = [("mod_ready", g + 1) if g < G_IN else ("phi_psum", g - G_PHI + 1) if G_PHI <= g < G_OUT_O
               else ("proj_ready", last_unit[g] + 1) for g in range(len(GROUPS))]
    DBLK, dsum = [], [0] * DN_SLOTS
    for q in range(12):
        j, part = q // 3, q % 3
        dsum[q % DN_SLOTS] += 32 if part == 2 else 16
        DBLK.append((j, [2 * part, 2 * part + 1], q % DN_SLOTS, dsum[q % DN_SLOTS]))
    assert len(set(dsum)) == 1
    DSUM = dsum[0]

    def stepper(eng, chain):
        count = {}

        def step(ins, signal=chain):
            count[signal] = count.get(signal, 0) + 1
            ins.then_inc(S(signal), 1)
            eng.wait_ge(S(signal), count[signal])
        return step

    block = ctx.enter_context(nc.Block())

    @block.sync
    def _(sp):
        sp.dma_start(rows[0:8, :], A["g_pre1"][0].rearrange("(a b) -> a b", b=128)).then_inc(S("rows_in"), 16)
        sp.dma_start(rows[8:16, :], A["g_pre2"][0].rearrange("(a b) -> a b", b=128)).then_inc(S("rows_in"), 16)
        sp.dma_start(rows[16:24, :], A["ln_e_2"][0].rearrange("(a b) -> a b", b=128)).then_inc(S("rows_in"), 16)
        sp.dma_start(rows[24:32, :], A["ln_o_2"][0].rearrange("(a b) -> a b", b=128)).then_inc(S("rows_in"), 16)
        sp.dma_start(rows[32:40, :], A["hg_lb_logits"].rearrange("l (a b) -> (l a) b", b=128)).then_inc(S("rows_in"), 16)
        sp.dma_start(rows[40:48, :], A["c"][0].rearrange("(a b) -> a b", b=128)).then_inc(S("rows_in"), 16)
        sp.dma_start(rows[48:56, :], A["c_ctx"].rearrange("(a b) -> a b", b=128)).then_inc(S("rows_in"), 16)
        sp.dma_start(ident[:, :], A["ident"]).then_inc(S("rows_in"), 16)
        sp.dma_start(X[:, :, :], A["x"][0].rearrange("(t p) d -> p t d", p=128)).then_inc(S("x_in"), 16)
        sp.dma_start(xctx, A["ctx"][0].rearrange("(t p) d -> p t d", p=128)).then_inc(S("x_in"), 16)
        sp.dma_start(bmod[0:1, :], A["b_mod"]).then_inc(S("mod_in"), 16)
        sp.dma_start(bmod[1:2, :], A["b_mod"]).then_inc(S("mod_in"), 16)

        def load_group(n):
            name, what = GROUPS[n]
            slot_ = n % WG_SLOTS
            if n >= WG_SLOTS:
                sp.wait_ge(S(used_by[n - WG_SLOTS][0]), used_by[n - WG_SLOTS][1])
            if isinstance(what, int):
                src = A[name][0, what].rearrange("(l d) c -> d l c", d=64)
                for hf in range(2):
                    dst = view(WG[:, slot_, :], 0, 32, 128)[64 * hf:64 * hf + 64]
                    sp.dma_start(dst, src).then_inc(S(f"wg_in{slot_}"), 16)
                return
            width = sum(w for _, w in what)
            dst = view(WG[:, slot_, :], 0, KC, width)
            o = 0
            for c0, w in what:
                sp.dma_start(dst[:, :, o:o + w],
                             A[name][0].rearrange("(k p) c -> p k c", p=128)[:, :, c0:c0 + w]
                             ).then_inc(S(f"wg_in{slot_}"), 16)
                o += w
        for n in range(G_IN_E + WG_SLOTS):
            load_group(n)
        sp.wait_ge(S("xs_done"), KC)
        sp.wait_ge(S("tr_copied"), marks["sg"][1])
        gate_d, up_d, down_d = (A[n][0] for n in ("w_gate", "w_up", "w_down"))

        def load_expert(e, first):
            for i in range(2 * KC):
                src = (gate_d if i % 2 == 0 else up_d)[e, 128 * (i // 2):128 * (i // 2) + 128, :]
                if not (first and i < GU_SLOTS):
                    sp.wait_ge(S("gu_used"), 2 * KC * e + (i - GU_SLOTS + 1))
                sp.dma_start(GU[:, i % GU_SLOTS, :], src).then_inc(S(f"gu_in{i % GU_SLOTS}"), 16)
            for i, (j, (s0, s1), slot_, _) in enumerate(DBLK):
                if not (first and i < DN_SLOTS):
                    sp.wait_ge(S("dn_used"), 12 * e + (i - DN_SLOTS + 1))
                r0 = FG * j + 128 * s0
                if FS[s1] == 128:
                    sp.dma_start(DN[:, slot_, :, :], down_d[e, r0:r0 + 256, :].rearrange("(s p) d -> p s d", p=128)
                                 ).then_inc(S(f"dn_in{slot_}"), 16)
                else:
                    sp.dma_start(DN[:, slot_, 0, :], down_d[e, r0:r0 + 128, :]).then_inc(S(f"dn_in{slot_}"), 16)
                    sp.dma_start(DN[0:FS[s1], slot_, 1, :], down_d[e, r0 + 128:r0 + 128 + FS[s1], :]
                                 ).then_inc(S(f"dn_in{slot_}"), 16)
        load_expert(0, True)
        with sp.Fori(1, E) as e:
            load_expert(e, False)
        sp.wait_ge(S("y_stored"), 16 * E)
        sp.wait_ge(S("dn_used"), 12 * E)
        sp.dma_start(ybuf, y_dram.rearrange("(b p) d -> p b d", p=128)).then_inc(S("y_back"), 16)
        for n in range(G_IN_E + WG_SLOTS, len(GROUPS)):
            load_group(n)
        sp.wait_ge(S("x_final"), 1)
        sp.dma_start(out[0].rearrange("(t p) d -> p t d", p=128), X[:, :, :]).then_inc(S("out_done"), 16)
        sp.wait_ge(S("out_done"), 16)

    @block.gpsimd
    def _(pool):
        pool.dma_start(first_row[0:2, :], A["first_row"]).then_inc(S("gate_in"), 16)
        pool.dma_start(GP1, A["g_post1"][0].partition_broadcast(128)).then_inc(S("gate_in"), 16)
        pool.dma_start(GP2[:, :], A["g_post2"][0].partition_broadcast(128)).then_inc(S("gate_in"), 16)
        pool.dma_start(reset, A["scan_reset"]).then_inc(S("hg_in"), 16)
        pool.dma_start(cmask.bitcast(I32), A["chunk_mask"]).then_inc(S("hg_in"), 16)
        pool.dma_start(b_hg, A["hg_norm"][0].partition_broadcast(128)).then_inc(S("hg_in"), 16)
        pool.dma_start(na_keep, A["na_keep"]).then_inc(S("na_in"), 16)
        pool.dma_start(na_mask, A["na_mask"]).then_inc(S("na_in"), 16)
        for a, n in ((rcos, "rope_cos"), (rsin, "rope_sin")):
            pool.dma_start(a, A[n].rearrange("(t p) c -> p t c", p=128)).then_inc(S("na_in"), 16)
        pool.dma_start(w_rt, A["w_router"][0].rearrange("(k p) e -> p k e", p=128)).then_inc(S("rt_in"), 16)
        pool.dma_start(ones, A["ones"]).then_inc(S("rt_in"), 16)
        pool.dma_start(slot, A["slot_iota"]).then_inc(S("rt_in"), 16)
        rpb = A["na_rpb"]
        RH, RW = rpb.shape[2], rpb.shape[3]
        for h in range(8):
            src = bass.AP(tensor=rpb.tensor, offset=rpb.offset + h * RH * RW + 4 * RW + 15 - 63,
                          ap=[[0, 64], [RW, 7], [1, DIAG]])
            pool.dma_start(diag[h].rearrange("r q c -> q r c"), src).then_inc(S("diag_out"), 16)
        pool.wait_ge(S("diag_out"), 8 * 16)
        for r in range(4):
            for h in range(8):
                src = bass.AP(tensor=diag.tensor, offset=diag.offset + (h * 7 + 3 - r) * 64 * DIAG + 63,
                              ap=[[DIAG - 1, 64], [64 * DIAG, 4], [1, 64]])
                dst = na_tab[64 * (r % 2):64 * (r % 2) + 64, h, r // 2, :].rearrange("p (a b) -> p a b", b=64)
                pool.dma_start(dst, src).then_inc(S("rpb_in"), 16)
        pool.wait_ge(S("na_in"), 64)
        pool.wait_ge(S("rpb_in"), 32 * 16)
        tab = view(TAB, 0, 64, 64)
        bro = lambda a: a.unsqueeze(1).to_broadcast([128, 64, 64])
        nc.gpsimd.tensor_tensor(tab, tab, bro(na_keep), ALU.mult).then_inc(S("na_tab"), 1)
        pool.wait_ge(S("na_tab"), 1)
        nc.gpsimd.tensor_tensor(tab, tab, bro(na_mask), ALU.add).then_inc(S("na_tab"), 1)
        pool.wait_ge(S("proj_ready"), P_IN[1])
        nc.gpsimd.memset(vbd, 0.0).then_inc(S("vbd_zero"), 1)
        pool.wait_ge(S("vbd_zero"), 1)
        pool.wait_ge(S("proj_evac"), 16)
        for h in range(HG):
            if h:
                pool.wait_ge(S("hg_o"), h)
            for c in range(4):
                nc.gpsimd.tensor_copy(vbd[32 * c:32 * c + 32, :, c, :],
                                      ih[32 * c:32 * c + 32, :, 128 * h:128 * h + 128]).then_inc(S("vbd_ready"), 1)
        pool.wait_ge(S("x_moe"), 1)
        pool.dma_start(tab_a, A["dilated"]).then_inc(S("even_in"), 16)
        pool.dma_start(tab_c, A["alibi"]).then_inc(S("even_in"), 16)
        pool.dma_start(b_qe, A["qkn_e_2"][0].partition_broadcast(128)).then_inc(S("even_in"), 16)
        pool.dma_start(b_sub, A["subln_e_2"][0].partition_broadcast(128)).then_inc(S("even_in"), 16)
        pool.dma_start(b_lam, A["lam_e_2"][0].partition_broadcast(128)).then_inc(S("even_in"), 16)
        pool.dma_start(b_qo, A["qkn_o_2"][0].partition_broadcast(128)).then_inc(S("even_in"), 16)
        for s in range(2):
            for dd in range(2):
                pool.dma_start(pe2[0:32, s, 64 * dd:64 * dd + 64], A["phi_pe_2"][0, s]).then_inc(S("odd_in"), 16)
        pool.dma_start(w2, A["phi_w2_2"][0].rearrange("s p c -> p s c")).then_inc(S("odd_in"), 16)
        pool.dma_start(cbias, A["cmp_bias"]).then_inc(S("odd_in"), 16)
        pool.dma_start(ckeep, A["cmp_keep"]).then_inc(S("odd_in"), 16)
        pool.dma_start(bdiag, A["block_diag"]).then_inc(S("odd_in"), 16)

    @block.tensor
    def _(pe):
        mm = nc.tensor.matmul

        def do_fills(name):
            for i in range(*marks[name]):
                parts, dst, rows_ = FILLS[i]
                if i >= 2:
                    pe.wait_ge(S("tr_copied"), i - 1)
                for src, c in parts:
                    k, m = src.shape
                    last = nc.tensor.transpose(PS[0:m, 4 + i % 2, c:c + k], src, ident[0:k, 0:k])
                last.then_inc(S("tr_ready"), 1)

        def project(a, b, lhs):
            for n in range(a, b):
                g, kind, j, w, *_ = PROJ[n]
                if n == a or PROJ[n - 1][0] != g:
                    pe.wait_ge(S(f"wg_in{g % WG_SLOTS}"), need[g])
                if n - 4 >= 0:
                    pe.wait_ge(S("proj_evac"), n - 3)
                width = sum(x for _, x in GROUPS[g][1])
                wt = view(WG[:, g % WG_SLOTS, :], 0, KC, width)
                for k in range(KC):
                    if kind == "chan":
                        last = mm(bank(n % 4)[:, 0:w], wt[:, k, 128 * j:128 * j + 128], lhs[:, k, 0:w],
                                  start=k == 0, stop=k == KC - 1)
                    else:
                        last = mm(bank(n % 4)[:, 0:w], lhs[:, k, 128 * j:128 * j + 128], wt[:, k, 0:w],
                                  start=k == 0, stop=k == KC - 1)
                last.then_inc(S("proj_ready"), 1)
        
        def attention(name):
            us = ATT[name]
            pb, pt = PB.get(name, (pb2, pt2))

            def scores(u):
                i = u["i"]
                if i >= 2:
                    pe.wait_ge(S("exp_done"), i - 1)
                o = bank(i % 2)
                mm(o[:, 0:u["tab"].shape[1]], ident[:, :], u["tab"], start=True, stop=False)
                for c, q, k in u["s"]:
                    last = mm(o[:, c:c + k.shape[1]], q, k, start=c > 0, stop=True)
                last.then_inc(S("s_ready"), 1)

            def turn(u):
                i = u["i"]
                pe.wait_ge(S("exp_done"), i + 1)
                if i >= 2:
                    pe.wait_ge(S("pt_copied"), i - 1)
                for b in range(u["n"] // 128):
                    last = nc.tensor.transpose(bank(2 + i % 2)[:, 128 * b:128 * b + 128],
                                               pb[:, i % 2, 128 * b:128 * b + 128], ident[:, :])
                last.then_inc(S("pT_done"), 1)

            def values(u):
                i, g = u["i"], u["g"]
                pe.wait_ge(S("pt_copied"), i + 1)
                if g >= 2:
                    pe.wait_ge(S("o_read"), g - 1)
                nb = u["n"] // 128
                for b in range(nb):
                    last = mm(bank(6 + g % 2)[:, u["c"]:u["c"] + u["w"]], pt[:, i % 2, 128 * b:128 * b + 128],
                              u["v"][b], start=b == 0, stop=b == nb - 1)
                last.then_inc(S("pv_done"), 1)
            for k in range(len(us) + 2):
                if k < len(us):
                    scores(us[k])
                if 1 <= k <= len(us):
                    turn(us[k - 1])
                if k >= 2:
                    values(us[k - 2])

        pe.wait_ge(S("rows_in"), 8 * 16)
        nc.tensor.transpose(PS[:, 7, 0:56], rows[0:56, :], ident[0:56, 0:56]).then_inc(S("rowsT"), 1)
        pe.wait_ge(S("csil_ready"), 1)
        for g in range(12):
            pe.wait_ge(S(f"wg_in{g % WG_SLOTS}"), need[g])
            if g >= 4:
                pe.wait_ge(S("mod_evac"), g - 3)
            wt = view(WG[:, g % WG_SLOTS, :], 0, KC, 512)
            for k in range(KC):
                last = mm(PS[0:2, g % 4, :], csil[:, k, :], wt[:, k, :], start=k == 0, stop=k == KC - 1)
            last.then_inc(S("mod_ready"), 1)
        pe.wait_ge(S("mod_evac"), 12)
        for b in [*range(16), *range(24, 40)]:
            last = nc.tensor.transpose(PS[:, 4, 2 * b:2 * b + 2], modrow[0:2, 128 * b:128 * b + 128], ident[0:2, 0:2])
        last.then_inc(S("modT"), 1)
        pe.wait_ge(S("gate_in"), 48)
        for i, c0 in enumerate((2 * D, 2 * D + 512, 5 * D, 5 * D + 512)):
            last = mm(bank(i), first_row[0:2, :], modrow[0:2, c0:c0 + 512], start=True, stop=True)
        last.then_inc(S("gate_bcast"), 1)
        pe.wait_ge(S("xn_ready"), 4)
        for k in range(KC):
            if k >= 2:
                pe.wait_ge(S("hT_done"), 2 * (k - 1))
            for t in range(4):
                last = nc.tensor.transpose(bank(6 + k % 2)[:, 128 * t:128 * t + 128],
                                           xn[:, t, 128 * k:128 * k + 128], ident[:, :])
            last.then_inc(S("hT_ready"), 1)
        pe.wait_ge(S("hT_done"), 2 * KC)
        pe.wait_ge(S("gp_done"), 2)
        project(*P_IN, view(HT, 0, KC, 512))
        for h in range(HG):
            pe.wait_ge(S("hg_dec"), h + 1)
            do_fills(f"kend{h}")
            if h == 0:
                pe.wait_ge(S("proj_evac"), P_IN[1])
            else:
                pe.wait_ge(S("aT_ready"), h)
            for d in range(2):
                for t in range(2):
                    a = 2 * d + t
                    last = mm(bank(3)[:, 128 * a:128 * a + 128], kdec[:, d, 128 * t:128 * t + 128],
                              qdec[:, d, 128 * t:128 * t + 128], start=True, stop=True)
            last.then_inc(S("aT_psum"), 1)
            pe.wait_ge(S("tr_copied"), marks[f"kend{h}"][1])
            pe.wait_ge(S("vbd_ready"), 4 * (h + 1))
            for j in range(8):
                d = j % 2
                t = ((2, 3, 0, 1), (3, 2, 1, 0))[d][j // 2]
                n = 8 * h + j
                if n >= 3:
                    pe.wait_ge(S("kv_used"), n - 2)
                mm(bank(n % 3), kendT[:, d, t, :], vbd[:, t, :, :].rearrange("p a b -> p (a b)"),
                   start=True, stop=True).then_inc(S("kv_ready"), 1)
            pe.wait_ge(S("aT_ready"), h + 1)
            pe.wait_ge(S("states_ready"), h + 1)
            for t in range(2):
                o = PS[:, 6 + t, 128 * h:128 * h + 128]
                for d in range(2):
                    mm(o, aT[:, 2 * d + t, :], ih[:, t, 128 * h:128 * h + 128], start=d == 0, stop=False)
                for d in range(2):
                    for c in range(4):
                        n = 4 * t + c
                        s = 7 + n if d == 0 else 14 - n
                        last = mm(o[32 * c:32 * c + 32, :], qdec[:, d, 32 * n:32 * n + 32], states[:, d, s, :],
                                  start=False, stop=d == 1)
            last.then_inc(S("hg_o"), 1)
        pe.wait_ge(S("rope_ready"), 1)
        do_fills("na")
        pe.wait_ge(S("tr_copied"), marks["na"][1])
        pe.wait_ge(S("na_tab"), 2)
        pe.wait_ge(S("hg_read"), 2)
        attention("na")
        pe.wait_ge(S("mixcat_ready"), 2)
        do_fills("mix")
        pe.wait_ge(S("tr_copied"), marks["mix"][1])
        project(*P_OUT, mixT)
        pe.wait_ge(S("xn2_ready"), 2)
        do_fills("h2")
        pe.wait_ge(S("h2_ready"), KC)
        pe.wait_ge(S("rt_in"), 48)
        for t in range(2):
            for k in range(KC):
                last = mm(PS[:, 6, E * t:E * t + E], h2T[:, k, 128 * t:128 * t + 128], w_rt[:, k, :],
                          start=k == 0, stop=k == KC - 1)
        last.then_inc(S("lg_ready"), 1)
        pe.wait_ge(S("aff_ready"), 1)
        do_fills("aff")
        pe.wait_ge(S("pos_ready"), 1)
        do_fills("pos")
        pe.wait_ge(S("oh_ready"), 2)
        for k in range(KC):
            if k >= 2:
                pe.wait_ge(S("xs_done"), k - 1)
            for t in range(2):
                last = mm(bank(6 + k % 2), xn2[:, t, 128 * k:128 * k + 128],
                          oh[:, t].rearrange("p a b -> p (a b)"), start=t == 0, stop=t == 1)
            last.then_inc(S("xs_psum"), 1)
        pe.wait_ge(S("ohg_ready"), 2)
        do_fills("sg")

        def expert(e, first):
            pe.wait_ge(S("xse_ready"), e + 1)
            if not first:
                pe.wait_ge(S("hid_ready"), e)
            for i in range(2 * KC):
                k, up, slot_ = i // 2, i % 2, i % GU_SLOTS
                pe.wait_ge(S(f"gu_in{slot_}"), 32 * e + 16 * (i // GU_SLOTS + 1))
                for hf in range(2):
                    for g in range(4):
                        c0 = FG * g + FH * hf
                        last = mm(PS[32 * g:32 * g + 32, 2 * up + hf, 0:FH], xse[:, k, :],
                                  GU[:, slot_, c0:c0 + FH], start=k == 0, stop=k == KC - 1)
                last.then_inc(S("gu_used"), 1)
            pe.wait_ge(S("hid_ready"), e + 1)
            if not first:
                pe.wait_ge(S("hidT_copied"), 3 * e)
            for s, n in enumerate(FS):
                last = nc.tensor.transpose(PS[0:n, 4 + s // 4, 128 * (s % 4):128 * (s % 4) + 128],
                                           hid[:, 128 * s:128 * s + n], ident[:, :])
            last.then_inc(S("hidT_done"), 1)
            pe.wait_ge(S("hidT_copied"), 3 * e + 3)
            if not first:
                pe.wait_ge(S("y_copied"), e)
            for i, (j, ss, slot_, v) in enumerate(DBLK):
                pe.wait_ge(S(f"dn_in{slot_}"), DSUM * e + v)
                for s in ss:
                    for g in range(4):
                        last = mm(PS[32 * g:32 * g + 32, 6, 0:256], hidT[0:FS[s], s, 32 * j:32 * j + 32],
                                  DN[0:FS[s], slot_, s % 2, 256 * g:256 * g + 256],
                                  start=i == 0 and s == 0, stop=i == 11 and s == ss[-1])
                last.then_inc(S("dn_used"), 1)
        expert(0, True)
        with pe.Fori(1, E) as e:
            expert(e, False)
        pe.wait_ge(S("y_back"), 16)
        for t in range(2):
            for hf in range(2):
                for b in range(4):
                    last = mm(bank(2 * t + hf), sgt[:, b, 128 * t:128 * t + 128], ybuf[:, b, 512 * hf:512 * hf + 512],
                              start=b == 0, stop=b == 3)
                last.then_inc(S("moe_psum"), 1)
        pe.wait_ge(S("xn3_ready"), 2)
        do_fills("he")
        pe.wait_ge(S("he_ready"), KC)
        project(*P_E, hTe)
        pe.wait_ge(S("qke_ready"), 1)
        do_fills("qke")
        pe.wait_ge(S("tr_copied"), marks["qke"][1])
        pe.wait_ge(S("even_in"), 96)
        pe.wait_ge(S("proj_evac"), P_E[1])
        attention("a")
        attention("b")
        pe.wait_ge(S("mixe_ready"), 1)
        do_fills("mixe")
        pe.wait_ge(S("tr_copied"), marks["mixe"][1])
        project(*P_OUT_E, mixeT)
        pe.wait_ge(S("xn3_ready"), 4)
        do_fills("ho")
        pe.wait_ge(S("he_ready"), 2 * KC)
        project(*P_O, hTe)
        pe.wait_ge(S("proj_evac"), P_O[1])
        pe.wait_ge(S("odd_in"), 8 * 16)
        do_fills("cmp")
        pe.wait_ge(S("ab_ready"), 4)
        for s in range(2):
            g = G_PHI + s
            pe.wait_ge(S(f"wg_in{g % WG_SLOTS}"), need[g])
            wt = view(WG[:, g % WG_SLOTS, :], 0, 32, 128)
            for l in range(32):
                for h in range(2):
                    last = mm(PS[:, 2 + h, 16 * s:16 * s + NCMP], wt[64 * h:64 * h + 64, l, :],
                              ab[64 * h:64 * h + 64, s, l, 0:NCMP], start=l == 0, stop=l == 31)
            last.then_inc(S("phi_psum"), 1)
        pe.wait_ge(S("phi_hid"), 10)
        for h in range(2):
            mm(PS[0:16, 6, 64 * h:64 * h + 64], hidk[:, h, :], w2[:, 0, :], start=True, stop=True)
        mm(PS[:, 7, 0:64], hidv.rearrange("p a b -> p (a b)"), w2[:, 1, :], start=True, stop=True
           ).then_inc(S("kcmp_psum"), 1)
        pe.wait_ge(S("qko_ready"), 1)
        do_fills("qko")
        pe.wait_ge(S("kcmp_ready"), 1)
        do_fills("kcmp")
        pe.wait_ge(S("tr_copied"), marks["kcmp"][1])
        for t in range(2):
            for h in (0, 2, 4, 6, 1, 3, 5, 7):
                last = mm(PS[:, h % 2, 64 * t + 16 * (h // 2):64 * t + 16 * (h // 2) + 16],
                          dqT[half(h), h // 2, 128 * t:128 * t + 128], kcmpT[half(h), h // 4, :], start=True, stop=True)
        last.then_inc(S("sc_psum"), 1)
        pe.wait_ge(S("pc_ready"), 1)
        do_fills("pc")
        pe.wait_ge(S("tr_copied"), marks["pc"][1])
        pe.wait_ge(S("vbd2_ready"), 1)
        for t in range(2):
            last = mm(bank(6 + t), pcT[:, t, :], vbd2.rearrange("p a b -> p (a b)"), start=True, stop=True)
        last.then_inc(S("oc_psum"), 1)
        pe.wait_ge(S("oc_read"), 1)
        attention("c")
        attention("s")
        attention("w")
        pe.wait_ge(S("mixo_ready"), 1)
        do_fills("mixo")
        pe.wait_ge(S("tr_copied"), marks["mixo"][1])
        project(*P_OUT_O, mixeT)

    @block.scalar
    def _(act):
        fn = nc.scalar.activation
        step = stepper(act, "act_step")
        roots = [0]

        def root(n):
            roots[0] += 1
            act.wait_ge(S("ms_ready"), roots[0])
            fn(stat[:, 0:n], stat[:, 0:n], ACT.Sqrt).then_inc(S("root_ready"), 1)

        def copy_fills(name):
            for i in range(*marks[name]):
                _, dst, rows_ = FILLS[i]
                act.wait_ge(S("tr_ready"), i + 1)
                w = int(np.prod(dst.shape[1:]))
                src = view(PS[:, 4 + i % 2, :], 0, *dst.shape[1:])
                fn(dst if rows_ == 128 or dst.shape[0] == rows_ else dst[0:rows_], src[0:rows_], ACT.Copy
                   ).then_inc(S("tr_copied"), 1)

        def evacuate(a, b):
            for n in range(a, b):
                _, _, _, w, dst, f, scale = PROJ[n]
                act.wait_ge(S("proj_ready"), n + 1)
                fn(dst, bank(n % 4)[:, 0:w], f, scale=scale).then_inc(S("proj_evac"), 1)

        def attention(name):
            pb, _ = PB.get(name, (pb2, pt2))
            for u in ATT[name]:
                i, n = u["i"], u["n"]
                act.wait_ge(S("max_ready"), i + 1)
                if i >= 2:
                    act.wait_ge(S("pT_done"), i - 1)
                fn(pb[:, i % 2, 0:n], bank(i % 2)[:, 0:n], ACT.Exp, bias=negm[:, i % 8:i % 8 + 1],
                   accum_out=lsum[:, i:i + 1]).then_inc(S("exp_done"), 1)

        act.wait_ge(S("cols_ready"), 1)
        fn(csil.rearrange("p k w -> p w k"), view(cols, 40, 2, 8), ACT.Sigmoid).then_inc(S("csig"), 1)
        act.wait_ge(S("lb_in"), 1)
        fn(lbt[:, 0:8], lbt[:, 0:8], ACT.Exp).then_inc(S("lb_exp"), 1)
        root(4)
        evacuate(*P_IN)
        for h in range(HG):
            act.wait_ge(S("hg_f"), h + 1)
            step(fn(fgt, fgt, ACT.Ln), "hg_ln")
            act.wait_ge(S("hg_b"), h + 1)
            fn(eb, bcum[:, :, 0:T], ACT.Exp).then_inc(S("hg_exp"), 1)
            fn(enb, bcum[:, :, 0:T], ACT.Exp, scale=-1.0).then_inc(S("hg_exp"), 1)
            fn(kend, kend, ACT.Exp).then_inc(S("hg_exp"), 1)
            fn(decay[:, 0, :], bcum[:, 0, CH - 1::CH], ACT.Exp).then_inc(S("hg_exp"), 1)
            fn(decay[:, 1, :], bcum[:, 1, 0::CH], ACT.Exp).then_inc(S("hg_exp"), 1)
            copy_fills(f"kend{h}")
        act.wait_ge(S("hg_o"), HG)
        for t in range(2):
            fn(fgt[:, t], bank(6 + t), ACT.Square).then_inc(S("hg_sq"), 1)
        root(8)
        copy_fills("na")
        attention("na")
        copy_fills("mix")
        evacuate(*P_OUT)
        root(2)
        root(2)
        copy_fills("h2")
        act.wait_ge(S("lg_shift"), 1)
        fn(lg, lg, ACT.Exp).then_inc(S("lg_exp"), 1)
        copy_fills("aff")
        copy_fills("pos")
        copy_fills("sg")

        def expert(e, first):
            act.wait_ge(S("gu_used"), 2 * KC * e + 2 * KC)
            if not first:
                act.wait_ge(S("hid_ready"), e)
            fn(view(sig, 0, 2, FH), PS[:, 0:2, 0:FH], ACT.Sigmoid).then_inc(S("sig_ready"), 1)
            act.wait_ge(S("hidT_done"), e + 1)
            if not first:
                act.wait_ge(S("dn_used"), 12 * e)
            fn(hidT[:, 0:4, :], view(PS[:, 4, :], 0, 4, 128), ACT.Copy).then_inc(S("hidT_copied"), 1)
            fn(hidT[:, 4, :], PS[:, 5, 0:128], ACT.Copy).then_inc(S("hidT_copied"), 1)
            fn(hidT[0:FS[5], 5, :], PS[0:FS[5], 5, 128:256], ACT.Copy).then_inc(S("hidT_copied"), 1)
            act.wait_ge(S("dn_used"), 12 * e + 12)
            if not first:
                act.wait_ge(S("y_stored"), 16 * e)
            fn(ysb, PS[:, 6, 0:256], ACT.Copy).then_inc(S("y_copied"), 1)
            act.wait_ge(S("y_copied"), e + 1)
            dst = y_dram.rearrange("(e s) (g c) -> e g s c", s=CAP, c=256)
            act.dma_start(dst[e], ysb).then_inc(S("y_stored"), 16)
        expert(0, True)
        with act.Fori(1, E) as e:
            expert(e, False)
        for i in range(4):
            act.wait_ge(S("moe_psum"), i + 1)
            fn(moeo[:, i // 2, 512 * (i % 2):512 * (i % 2) + 512], bank(i), ACT.Copy).then_inc(S("moe_evac"), 1)
        root(2)
        root(2)
        copy_fills("he")
        evacuate(*P_E)
        act.wait_ge(S("lam_in"), 1)
        fn(lamt[:, 0:2], lamt[:, 0:2], ACT.Exp).then_inc(S("lam_exp"), 1)
        root(64)
        copy_fills("qke")
        attention("a")
        attention("b")
        root(8)
        copy_fills("mixe")
        evacuate(*P_OUT_E)
        root(2)
        copy_fills("ho")
        evacuate(*P_O)
        act.wait_ge(S("proj_evac"), P_O[1])
        fn(gates, kw[:, :, 256:280], ACT.Sigmoid).then_inc(S("gates_ready"), 1)
        copy_fills("cmp")
        act.wait_ge(S("hid_zero"), 2)
        act.wait_ge(S("phi_psum"), 2)
        for h in range(2):
            fn(hidk[:, h, 0:NCMP], PS[:, 2 + h, 0:NCMP], ACT.Silu).then_inc(S("phi_hid"), 1)
        for h in range(8):
            fn(hidv[:, h, 0:NCMP], PS[:, 2 + (h % 4) // 2, 16:16 + NCMP], ACT.Silu).then_inc(S("phi_hid"), 1)
        root(56)
        root(2)
        copy_fills("qko")
        copy_fills("kcmp")
        act.wait_ge(S("sc_shift"), 1)
        fn(pc, pc, ACT.Exp).then_inc(S("sc_exp"), 1)
        copy_fills("pc")
        attention("c")
        attention("s")
        attention("w")
        copy_fills("mixo")
        evacuate(*P_OUT_O)

    @block.vector
    def _(dve):
        v = nc.vector
        step = stepper(dve, "dve_step")
        roots = [0]

        def rms(items, n, width):
            for src, junk, c in items:
                step(v.tensor_tensor_reduce(out=junk, in0=src, in1=src, scale=1.0, scalar=0.0, op0=ALU.mult,
                                            op1=ALU.add, accum_out=stat[:, c:c + 1]))
            roots[0] += 1
            step(v.tensor_scalar(stat[:, 0:n], stat[:, 0:n], 1.0 / width, EPS, ALU.mult, ALU.add), "ms_ready")
            dve.wait_ge(S("root_ready"), roots[0])
            step(v.reciprocal(stat[:, 0:n], stat[:, 0:n]))

        def prenorm(dst, signal):
            rms([(X[:, t, :], dst[:, t, :], t) for t in range(2)], 2, D)
            for t in range(2):
                step(v.tensor_scalar(dst[:, t, :], X[:, t, :], stat[:, t:t + 1], None, ALU.mult), signal)

        def postnorm(src, gain, junk, signal="dve_step"):
            rms([(src[:, t, :], junk[:, t, :], t) for t in range(2)], 2, D)
            for t in range(2):
                step(v.scalar_tensor_tensor(src[:, t, :], src[:, t, :], stat[:, t:t + 1], gain, ALU.mult, ALU.mult))
            step(v.tensor_tensor(X[:, :, :], X[:, :, :], src, ALU.add), signal)

        def scale_chunks(hT_, col0, shift, name, signal):
            dve.wait_ge(S("tr_copied"), marks[name][1])
            for k in range(KC):
                step(v.tensor_scalar(hT_[:, k, :], hT_[:, k, :], col0[:, k:k + 1],
                                     None if shift is None else shift[:, k:k + 1], ALU.mult,
                                     ALU.bypass if shift is None else ALU.add), signal)

        def headed(ap, n, w):
            return ap.unsqueeze(2).to_broadcast([128, n, w])

        def attention(name, finish):
            us = ATT[name]
            pt = PB.get(name, (pb2, pt2))[1]
            for k in range(len(us) + 2):
                if k < len(us):
                    i, n = us[k]["i"], us[k]["n"]
                    dve.wait_ge(S("s_ready"), i + 1)
                    if i >= 8:
                        dve.wait_ge(S("exp_done"), i - 7)
                    v.tensor_reduce(negm[:, i % 8:i % 8 + 1], bank(i % 2)[:, 0:n], AX, ALU.max, negate=True
                                    ).then_inc(S("max_ready"), 1)
                if 1 <= k <= len(us):
                    i, n = us[k - 1]["i"], us[k - 1]["n"]
                    dve.wait_ge(S("pT_done"), i + 1)
                    if i >= 2:
                        dve.wait_ge(S("pv_done"), i - 1)
                    v.tensor_copy(pt[:, i % 2, 0:n], bank(2 + i % 2)[:, 0:n]).then_inc(S("pt_copied"), 1)
                if k >= 2 and us[k - 2]["last"]:
                    u = us[k - 2]
                    per = 512 // u["w"]
                    i0 = u["i"] - per + 1
                    dve.wait_ge(S("pv_done"), u["i"] + 1)
                    dve.wait_ge(S("exp_done"), u["i"] + 1)
                    step(v.reciprocal(rls[:, i0:i0 + per], lsum[:, i0:i0 + per]))
                    finish((k - 2) // per, bank(6 + u["g"] % 2), rls[:, i0:i0 + per])

        step(v.memset(aT, 0.0))
        dve.wait_ge(S("rowsT"), 1)
        step(v.tensor_copy(cols[:, :], PS[:, 7, 0:56]), "cols_ready")
        dve.wait_ge(S("csig"), 1)
        step(v.tensor_tensor(csil.rearrange("p k w -> p w k"), csil.rearrange("p k w -> p w k"),
                             view(cols, 40, 2, 8), ALU.mult), "csil_ready")
        step(v.tensor_tensor(lbt[:, 8:12], cols[:, 32:36], cols[:, 36:40], ALU.max))
        step(v.tensor_tensor(lbt[:, 4:8], cols[:, 36:40], lbt[:, 8:12], ALU.subtract))
        step(v.tensor_tensor(lbt[:, 0:4], cols[:, 32:36], lbt[:, 8:12], ALU.subtract), "lb_in")
        dve.wait_ge(S("lb_exp"), 1)
        step(v.tensor_tensor(lbt[:, 8:12], lbt[:, 0:4], lbt[:, 4:8], ALU.add))
        step(v.reciprocal(lbt[:, 8:12], lbt[:, 8:12]))
        step(v.tensor_tensor(lb, lbt[:, 0:4], lbt[:, 8:12], ALU.mult))
        step(v.tensor_scalar(oml, lb, -1.0, 1.0, ALU.mult, ALU.add))
        dve.wait_ge(S("x_in"), 32)
        toks = [X[:, 0, :], X[:, 1, :], xctx[:, 0, :], xctx[:, 1, :]]
        rms([(a, xn[:, t, :], t) for t, a in enumerate(toks)], 4, D)
        for t, a in enumerate(toks):
            step(v.tensor_scalar(xn[:, t, :], a, stat[:, t:t + 1], None, ALU.mult), "xn_ready")
        dve.wait_ge(S("mod_in"), 32)
        for g in range(12):
            dve.wait_ge(S("mod_ready"), g + 1)
            step(v.tensor_tensor(modrow[0:2, 512 * g:512 * g + 512], PS[0:2, g % 4, :],
                                 bmod[0:2, 512 * g:512 * g + 512], ALU.add), "mod_evac")
        dve.wait_ge(S("modT"), 1)
        for b in (0, 24):
            step(v.tensor_copy(modc[:, b:b + 16, :], view(PS[:, 4, :], 2 * b, 16, 2)))
        for dst, s0, w, g in ((A1, 8, 0, 0), (A1c, 8, 1, 0), (A2, 32, 0, 8)):
            step(v.scalar_tensor_tensor(dst, modc[:, s0:s0 + 8, w], 1.0, cols[:, g:g + 8], ALU.add, ALU.mult))
        dve.wait_ge(S("gate_bcast"), 1)
        for i, g in enumerate((GP1, GP2[:, :])):
            step(v.tensor_tensor(view(g, 0, 2, 512), view(g, 0, 2, 512), PS[:, 2 * i:2 * i + 2, :], ALU.mult), "gp_done")
        for k in range(KC):
            dve.wait_ge(S("hT_ready"), k + 1)
            for w, a in ((0, A1), (1, A1c)):
                step(v.tensor_scalar(view(HT, 0, KC, 512)[:, k, T * w:T * w + T], bank(6 + k % 2)[:, T * w:T * w + T],
                                     a[:, k:k + 1], modc[:, k, w:w + 1], ALU.mult, ALU.add), "hT_done")
        dve.wait_ge(S("proj_evac"), 12)
        dve.wait_ge(S("hg_in"), 48)
        for h in range(HG):
            if h:
                dve.wait_ge(S("hg_o"), h)
                dve.wait_ge(S("hg_exp"), 5 * h)
            for d in range(2):
                step(v.tensor_scalar(fgt[:, d], z[:, d, h, :], oml[:, h:h + 1], lb[:, h:h + 1], ALU.mult, ALU.add))
            step(v.tensor_scalar(kk, fgt, -1.0, 1.0, ALU.mult, ALU.add), "hg_f")
            dve.wait_ge(S("hg_ln"), h + 1)
            step(v.tensor_tensor_scan(bcum[:, 0], reset, fgt[:, 0], 0.0, ALU.mult, ALU.add))
            step(v.tensor_tensor_scan(bcum[:, 1, ::-1], reset, fgt[:, 1, ::-1], 0.0, ALU.mult, ALU.add))
            for d in range(2):
                b = bcum[:, d].rearrange("p (n c) -> p n c", c=CH)
                e = b[:, :, CH - 1:CH] if d == 0 else b[:, :, 0:1]
                step(v.tensor_tensor(kend[:, d].rearrange("p (n c) -> p n c", c=CH),
                                     e.to_broadcast([128, 16, CH]), b, ALU.subtract))
            dve.sem_inc(S("hg_b"), 1)
            dve.wait_ge(S("hg_exp"), 5 * h + 5)
            step(v.tensor_tensor(kdec, kk[:, :, 0:T], enb, ALU.mult))
            for d in range(2):
                step(v.tensor_tensor(qdec[:, d], qh[:, h], eb[:, d], ALU.mult))
            step(v.tensor_tensor(kend, kend, kk, ALU.mult), "hg_dec")
            dve.wait_ge(S("aT_psum"), h + 1)
            step(v.copy_predicated(aT, cmask.bitcast(I32), view(bank(3), 0, 4, 128)), "aT_ready")
            for j in range(8):
                d, s = j % 2, j // 2
                t = ((2, 3, 0, 1), (3, 2, 1, 0))[d][s]
                dve.wait_ge(S("kv_ready"), 8 * h + j + 1)
                for i in range(4):
                    c = i if d == 0 else 3 - i
                    kv = bank((8 * h + j) % 3)[:, 128 * c:128 * c + 128]
                    n = 4 * s + i
                    sig_ = "kv_used" if i == 3 else "dve_step"
                    if n == 0:
                        step(v.tensor_copy(states[:, d, 0, :], kv))
                    else:
                        step(v.scalar_tensor_tensor(states[:, d, n, :], states[:, d, n - 1, :],
                                                    decay[:, d, 4 * t + c:4 * t + c + 1], kv, ALU.mult, ALU.add), sig_)
            dve.sem_inc(S("states_ready"), 1)
        dve.wait_ge(S("hg_sq"), 2)
        step(v.tensor_reduce(stat[:, 0:8], view(fgt.rearrange("p a b -> p (a b)"), 0, 8, 128), AX, ALU.add))
        rms([], 8, HG * 32)
        for t in range(2):
            m = mixcat[:, t, 512:D].rearrange("p (h c) -> p h c", c=128)
            step(v.tensor_tensor(m, view(bank(6 + t), 0, 4, 128), headed(stat[:, 4 * t:4 * t + 4], 4, 128), ALU.mult), "hg_read")
            step(v.tensor_tensor(m, m, b_hg.unsqueeze(1).to_broadcast([128, 4, 128]), ALU.mult))
            step(v.tensor_tensor(mixcat[:, t, 512:D], mixcat[:, t, 512:D], gh[:, t, :], ALU.mult))
        dve.wait_ge(S("proj_evac"), P_IN[1])
        dve.wait_ge(S("na_in"), 64)
        for src, dst in ((qn, qr), (kn, kr)):
            for t in range(2):
                x3 = src[:, t, :].rearrange("p (h c) -> p h c", c=64)
                y3 = dst[:, t, :].rearrange("p (h c) -> p h c", c=64)
                step(v.tensor_tensor(y3, x3, rcos[:, t, :].unsqueeze(1).to_broadcast([128, 8, 64]), ALU.mult))
                for hf in range(2):
                    for j in range(2):
                        a, b = 32 * hf + 16 * j, 32 * hf + 16 * (1 - j)
                        step(v.tensor_tensor(view(rt, 0, 8, 64)[:, :, a:a + 16], x3[:, :, b:b + 16],
                                             rsin[:, t, a:a + 16].unsqueeze(1).to_broadcast([128, 8, 16]), ALU.mult))
                step(v.tensor_tensor(dst[:, t, :], dst[:, t, :], rt, ALU.add))
        dve.sem_inc(S("rope_ready"), 1)

        def na_finish(i, o, r):
            step(v.tensor_tensor(mixcat[:, i, 0:512].rearrange("p (h c) -> p h c", c=64), view(o, 0, 8, 64),
                                 headed(r, 8, 64), ALU.mult), "o_read")
            dve.sem_inc(S("mixcat_ready"), 1)
        attention("na", na_finish)
        dve.wait_ge(S("proj_evac"), P_OUT[1])
        postnorm(mixo, GP1, xn2)
        prenorm(xn2, "xn2_ready")
        scale_chunks(h2T, A2, modc[:, 24:32, 0], "h2", "h2_ready")
        dve.wait_ge(S("lg_ready"), 1)
        step(v.tensor_reduce(amax, view(PS[:, 6, :], 0, 2, E), AX, ALU.max, negate=True))
        step(v.tensor_tensor(lg, view(PS[:, 6, :], 0, 2, E), headed(amax, 2, E), ALU.add), "lg_shift")
        dve.wait_ge(S("lg_exp"), 1)
        step(v.tensor_reduce(amax, lg, AX, ALU.add))
        step(v.reciprocal(amax, amax))
        step(v.tensor_tensor(aff, lg, headed(amax, 2, E), ALU.mult), "aff_ready")
        dve.wait_ge(S("tr_copied"), marks["aff"][1])
        src = affT
        for i in range(CAP // 8):
            step(v.max(best8[0:E, :], src[0:E, :]))
            step(v.match_replace(work[0:E, :], best8[0:E, :], src[0:E, :], -1.0))
            src = work
        dve.wait_ge(S("rt_in"), 48)
        step(v.tensor_scalar(work[0:E, :], work[0:E, :], -1.0, None, ALU.is_equal))
        step(v.tensor_tensor_scan(pos[0:E, :], ones[0:E, :], work[0:E, :], 0.0, ALU.mult, ALU.add))
        step(v.tensor_tensor(posm[0:E, :], pos[0:E, :], work[0:E, :], ALU.mult), "pos_ready")
        dve.wait_ge(S("tr_copied"), marks["pos"][1])
        for t in range(2):
            step(v.tensor_tensor(oh[:, t], headed(posT[:, t, :], E, CAP),
                                 slot.unsqueeze(1).to_broadcast([128, E, CAP]), ALU.is_equal), "oh_ready")
        for t in range(2):
            step(v.tensor_tensor(ohg[:, t], oh[:, t], headed(aff[:, t, :], E, CAP), ALU.mult), "ohg_ready")
        for k in range(KC):
            dve.wait_ge(S("xs_psum"), k + 1)
            step(v.tensor_scalar(xs[:, k, :], bank(6 + k % 2), A2[:, k:k + 1], modc[:, 24 + k, 0:1],
                                 ALU.mult, ALU.add), "xs_done")

        def expert(e, first):
            if not first:
                dve.wait_ge(S("gu_used"), 2 * KC * e)
            v.tensor_copy(xse, xs[:, :, bass.ds(e * CAP, CAP)]).then_inc(S("xse_ready"), 1)
            dve.wait_ge(S("sig_ready"), e + 1)
            if not first:
                dve.wait_ge(S("hidT_done"), e)
            v.tensor_tensor(view(sig, 0, 2, FH), view(sig, 0, 2, FH), PS[:, 0:2, 0:FH], ALU.mult
                            ).then_inc(S("silu_ready"), 1)
            dve.wait_ge(S("silu_ready"), e + 1)
            v.tensor_tensor(view(hid, 0, 2, FH), view(sig, 0, 2, FH), PS[:, 2:4, 0:FH], ALU.mult
                            ).then_inc(S("hid_ready"), 1)
        expert(0, True)
        with dve.Fori(1, E) as e:
            expert(e, False)
        dve.wait_ge(S("moe_evac"), 4)
        postnorm(moeo, GP2[:, :], view(BIG, 6 * D, 2, D), "x_moe")

        def norm_heads(arrays, n, gains):
            x = view(BIG, 0, n, 64)
            step(v.tensor_tensor(view(BIG, t2_off, n, 64), x, x, ALU.mult))
            step(v.tensor_reduce(stat[:, 0:n], view(BIG, t2_off, n, 64), AX, ALU.add))
            return x
        t2_off = ae.pos[0] - 4096
        prenorm(xn3, "xn3_ready")
        scale_chunks(hTe, cols[:, 16:24], None, "he", "he_ready")
        dve.wait_ge(S("even_in"), 96)
        for b in (b_qe, b_qo):
            step(v.tensor_scalar(b[:, 0::2, :][:, 0:2], b[:, 0::2, :][:, 0:2], 0.125, None, ALU.mult))
        step(v.tensor_tensor(b_lam[:, 0::2, :], b_lam[:, 0::2, :], b_lam[:, 1::2, :], ALU.mult))
        step(v.tensor_reduce(lamt[:, 0:2], b_lam[:, 0::2, :], AX, ALU.add), "lam_in")
        dve.wait_ge(S("proj_evac"), P_E[1])
        dve.wait_ge(S("lam_exp"), 1)
        step(v.tensor_tensor(lamt[:, 2:3], lamt[:, 0:1], lamt[:, 1:2], ALU.subtract))
        step(v.tensor_scalar(lamt[:, 2:3], lamt[:, 2:3], LAM_INIT, None, ALU.add))
        x = norm_heads(None, 64, None)
        rms([], 64, 64)
        step(v.tensor_tensor(x, x, headed(stat[:, 0:64], 64, 64), ALU.mult))
        for i in range(4):
            xi = view(BIG, 1024 * i, 16, 64)
            step(v.tensor_tensor(xi, xi, b_qe[:, i, :].unsqueeze(1).to_broadcast([128, 16, 64]), ALU.mult))
        dve.sem_inc(S("qke_ready"), 1)

        def plain_finish(dst, zz_):
            def finish(i, o, r):
                m = dst[:, i, 0:512].rearrange("p (h c) -> p h c", c=64)
                step(v.tensor_tensor(m, view(o, 0, 8, 64), headed(r, 8, 64), ALU.mult), "o_read")
                step(v.tensor_tensor(dst[:, i, 0:512], dst[:, i, 0:512], zz_[:, i, :], ALU.mult))
            return finish

        def diff_finish(i, o, r):
            qt, pair = i // 2, i % 2
            ov = view(o, 0, 2, 2, 128)
            r2 = r.rearrange("p (h c) -> p h c", c=2)
            step(v.tensor_scalar(r2[:, :, 1], r2[:, :, 1], lamt[:, 2:3], None, ALU.mult))
            t0, t1 = view(BIG, t2_off, 2, 128), view(BIG, t2_off + 256, 2, 128)
            for c, t_ in ((0, t0), (1, t1)):
                step(v.tensor_tensor(t_, ov[:, :, c, :], headed(r2[:, :, c], 2, 128), ALU.mult))
            m = mixe[:, qt, 512 + 256 * pair:768 + 256 * pair].rearrange("p (h c) -> p h c", c=128)
            step(v.tensor_tensor(m, t0, t1, ALU.subtract), "o_read")
        attention("a", plain_finish(mixe, zz[:, 0]))
        attention("b", diff_finish)
        ob = [mixe[:, t, 512:D].rearrange("p (h c) -> p h c", c=128) for t in range(2)]
        for t in range(2):
            sq = view(BIG, t2_off + 512 * t, 4, 128)
            step(v.tensor_tensor(sq, ob[t], ob[t], ALU.mult))
            step(v.tensor_reduce(stat[:, 4 * t:4 * t + 4], sq, AX, ALU.add))
        rms([], 8, 128)
        step(v.tensor_scalar(b_sub, b_sub, 1.0 - LAM_INIT, None, ALU.mult))
        for t in range(2):
            step(v.tensor_tensor(ob[t], ob[t], headed(stat[:, 4 * t:4 * t + 4], 4, 128), ALU.mult))
            step(v.tensor_tensor(ob[t], ob[t], b_sub.unsqueeze(1).to_broadcast([128, 4, 128]), ALU.mult))
            step(v.tensor_tensor(mixe[:, t, 512:D], mixe[:, t, 512:D], zz[:, 1][:, t, :], ALU.mult))
        dve.sem_inc(S("mixe_ready"), 1)
        dve.wait_ge(S("proj_evac"), P_OUT_E[1])
        step(v.tensor_tensor(X[:, :, :], X[:, :, :], mixo2, ALU.add), "x_even")
        prenorm(xn3, "xn3_ready")
        scale_chunks(hTe, cols[:, 24:32], None, "ho", "he_ready")
        step(v.memset(hidk, 0.0), "hid_zero")
        step(v.memset(hidv, 0.0), "hid_zero")
        dve.wait_ge(S("tr_copied"), marks["cmp"][1])
        for s in range(2):
            kv2 = kcvT[:, s, :].rearrange("p (i b) -> p b i", b=16)
            for a in range(2):
                step(v.tensor_tensor(ab[:, s, 16 * a:16 * a + 16, 0:NCMP], kv2[:, :, a:a + NCMP],
                                     peT[:, s, 16 * a:16 * a + 16].unsqueeze(2).to_broadcast([128, 16, NCMP]),
                                     ALU.add), "ab_ready")
        dve.wait_ge(S("proj_evac"), P_O[1])
        x = norm_heads(None, 48, None)
        for i, src in ((0, ckv[:, :, 256:384]), (1, kw[:, :, 0:128])):
            for t in range(2):
                s2 = src[:, t, :].rearrange("p (h c) -> p h c", c=64)
                tq = view(BIG, t2_off + 3072 + 128 * (2 * i + t), 2, 64)
                step(v.tensor_tensor(tq, s2, s2, ALU.mult))
                step(v.tensor_reduce(stat[:, 48 + 4 * i + 2 * t:50 + 4 * i + 2 * t], tq, AX, ALU.add))
        rms([], 56, 64)
        step(v.tensor_tensor(x, x, headed(stat[:, 0:48], 48, 64), ALU.mult))
        for i in range(3):
            xi = view(BIG, 1024 * i, 16, 64)
            step(v.tensor_tensor(xi, xi, b_qo[:, i, :].unsqueeze(1).to_broadcast([128, 16, 64]), ALU.mult))
        for i, src, gain in ((0, ckv[:, :, 256:384], 4), (1, kw[:, :, 0:128], 5)):
            for t in range(2):
                s2 = src[:, t, :].rearrange("p (h c) -> p h c", c=64)
                step(v.tensor_tensor(s2, s2, headed(stat[:, 48 + 4 * i + 2 * t:50 + 4 * i + 2 * t], 2, 64), ALU.mult))
                for dd in range(2):
                    step(v.tensor_tensor(view(dup[:, i, t, :], 0, 2, 2, 64)[:, :, dd, :], s2,
                                         b_qo[:, gain, :].unsqueeze(1).to_broadcast([128, 2, 64]), ALU.mult))
        dve.sem_inc(S("qko_ready"), 1)
        dve.wait_ge(S("kcmp_psum"), 1)
        kp = view(PS[:, 6, :], 0, 2, 64)[0:16]
        k0 = view(BIG, t2_off, 2, 64)[0:16]
        tq = view(BIG, t2_off + 128, 2, 64)[0:16]
        step(v.tensor_copy(k0, kp))
        step(v.tensor_tensor(tq, k0, k0, ALU.mult))
        step(v.memset(stat[:, 0:2], 1.0))
        step(v.tensor_reduce(stat[0:16, 0:2], tq, AX, ALU.add))
        rms([], 2, 64)
        step(v.tensor_tensor(k0, k0, stat[0:16, 0:2].unsqueeze(2).to_broadcast([16, 2, 64]), ALU.mult))
        for dd in range(2):
            step(v.tensor_tensor(kcmp[0:16, :, 64 * dd:64 * dd + 64], k0,
                                 b_qo[0:16, 3, :].unsqueeze(1).to_broadcast([16, 2, 64]), ALU.mult))
        dve.sem_inc(S("kcmp_ready"), 1)
        step(v.tensor_tensor(vbd2, PS[:, 7, 0:64].unsqueeze(1).to_broadcast([128, 8, 64]),
                             bdiag.unsqueeze(2).to_broadcast([128, 8, 64]), ALU.mult), "vbd2_ready")
        dve.wait_ge(S("sc_psum"), 1)
        for par in range(2):
            step(v.tensor_tensor(pc[:, :, 64 * par:64 * par + 64], view(PS[:, par, :], 0, 2, 64),
                                 cbias[:, :, 64 * par:64 * par + 64], ALU.add))
        p16 = view(pc.rearrange("p a b -> p (a b)"), 0, 16, 16)
        step(v.tensor_reduce(stat[:, 0:16], p16, AX, ALU.max))
        step(v.tensor_tensor(p16, p16, headed(stat[:, 0:16], 16, 16), ALU.subtract), "sc_shift")
        dve.wait_ge(S("sc_exp"), 1)
        step(v.tensor_tensor(pc, pc, ckeep, ALU.mult))
        step(v.tensor_reduce(stat[:, 0:16], p16, AX, ALU.add))
        step(v.tensor_scalar(stat[:, 0:16], stat[:, 0:16], 1e-30, None, ALU.max))
        step(v.reciprocal(stat[:, 0:16], stat[:, 0:16]))
        step(v.tensor_tensor(p16, p16, headed(stat[:, 0:16], 16, 16), ALU.mult), "pc_ready")
        dve.wait_ge(S("oc_psum"), 1)
        dve.wait_ge(S("gates_ready"), 1)
        g3 = gates.rearrange("p t (h j) -> p t h j", j=3)
        for t in range(2):
            step(v.tensor_tensor(ocmp[:, t, :].rearrange("p (h c) -> p h c", c=64), view(bank(6 + t), 0, 8, 64),
                                 headed(g3[:, t, :, 0], 8, 64), ALU.mult))
        dve.sem_inc(S("oc_read"), 1)

        def gated_finish(j):
            def finish(i, o, r):
                step(v.tensor_tensor(r, r, g3[:, i, :, j], ALU.mult))
                t_ = view(BIG, t2_off, 8, 64)
                step(v.tensor_tensor(t_, view(o, 0, 8, 64), headed(r, 8, 64), ALU.mult), "o_read")
                o3 = ocmp[:, i, :].rearrange("p (h c) -> p h c", c=64)
                step(v.tensor_tensor(o3, o3, t_, ALU.add))
            return finish
        attention("c", plain_finish(mixe, zz[:, 0]))
        attention("s", gated_finish(1))
        attention("w", gated_finish(2))
        for t in range(2):
            step(v.tensor_tensor(mixe[:, t, 512:D], ocmp[:, t, :], zz[:, 1][:, t, :], ALU.mult))
        dve.sem_inc(S("mixo_ready"), 1)
        dve.wait_ge(S("proj_evac"), P_OUT_O[1])
        step(v.tensor_tensor(X[:, :, :], X[:, :, :], mixo2, ALU.add), "x_final")

    ctx.close()


def kernel(**inputs):
    import concourse.bacc as _bacc
    from concourse.bass_utils import run_bass_kernel_spmd as _run

    nc = _bacc.Bacc("TRN2", target_bir_lowering=False, num_devices=1, dynamic_dma_scratch_size=4096)
    arrays, aps = {}, {}
    for name, a in [*inputs.items(), *constants().items()]:
        a = np.ascontiguousarray(a)
        arrays[f"in_{name}"] = a
        aps[name] = nc.dram_tensor(f"in_{name}", a.shape, mybir.dt.from_np(a.dtype), kind="ExternalInput").ap()
    out = nc.dram_tensor("out_x", (1, T, D), FP32, kind="ExternalOutput").ap()
    build(nc, aps, out)
    r = _run(nc, [arrays], core_ids=[0])
    return r.results[0]["out_x"]
```

```python
import numpy as np
import concourse.bass as bass
from concourse import mybir
from contextlib import ExitStack

FP32 = mybir.dt.float32
I32 = mybir.dt.int32
ALU = mybir.AluOpType
ACT = mybir.ActivationFunctionType
AX = mybir.AxisListType.X

D = 1024
T = 256
KC = D // 128
EPS = 1e-6
NEG = -1e30
E = 16
CAP = 2 * T // E
F = 2752
FG = F // 4
FH = FG // 2
FS = [128] * (FG // 128) + [FG % 128]
LAM_INIT = 0.2
HG = 4
CH = 32
NCMP = (T - 32) // 16 + 1
GU_SLOTS, GU_W = 8, F
DN_SLOTS, DN_W = 4, 2 * D
WG_SLOTS, WG_W = 3, KC * 512

def _block(matrix, what, *cols):
    return (matrix, what, list(cols) if cols else [(512 * what, 512)])


W_IN_COLS = dict(qn=0, kn=1, vn=2, qh=3, zf=4, zb=5, ih=6, gh=7)
EVEN_COLS = dict(aq=0, ak=1, av=2, az=3, bq=4, bk=5, bv=6, bz=7)
ODD_COLS = dict(cq=[(0, 512)], ck=[(512, 512)], cv=[(1024, 512)], cz=[(1536, 512)], dq=[(2048, 512)],
                kv=[(2560, 512)], kw=[(3072, 256), (3840, 24)], dz=[(3328, 512)])
GROUPS = [_block("w_mod", i) for i in range(4)]
for name, mods in (("zf", (4, 5)), ("zb", (6, 7)), ("qh", (8, 9)), ("ih", (10, 11)), ("gh", ()), ("kn", ()),
                   ("vn", ()), ("qn", ())):
    GROUPS.append(("w_in", name, [(512 * W_IN_COLS[name], 512)]))
    GROUPS += [_block("w_mod", i) for i in mods]
GROUPS += [_block("w_out", i) for i in range(2)]
GROUPS += [("w_in_e_2", n, [(512 * EVEN_COLS[n], 512)]) for n in ("aq", "ak", "av", "bq", "bk", "az", "bv", "bz")]
GROUPS += [_block("w_out_e_2", i) for i in range(2)]
for name in ("kv", "kw", "cq", "phi", "ck", "dq", "cv", "cz", "dz"):
    if name == "phi":
        GROUPS += [("phi_w1", s, []) for s in range(2)]
    else:
        GROUPS.append(("w_in_o_2", name, ODD_COLS[name]))
GROUPS += [_block("w_out_o_2", i) for i in range(2)]
GROUP_OF = {(m, w): n for n, (m, w, _) in enumerate(GROUPS)}


def constants():
    t = np.arange(T)
    p = np.arange(128)
    f32 = np.float32
    out = {"ident": np.eye(128, dtype=f32)}
    inv = (f32(10000.0) ** (-np.arange(0, 32, 2, dtype=f32) / f32(32))).astype(f32)
    ang = np.stack([(t // 64).astype(f32)[:, None] * inv, (t % 64).astype(f32)[:, None] * inv], 1)
    cos, sin = np.cos(ang).astype(f32), np.sin(ang).astype(f32)
    out["rope_cos"] = np.stack([cos, cos], 2).reshape(T, 64)
    out["rope_sin"] = np.stack([-sin, sin], 2).reshape(T, 64)
    qc, kc = np.arange(64)[:, None], np.arange(64)[None, :]
    w0 = np.clip(qc - 8, 0, 48)
    win = (kc >= w0) & (kc < w0 + 16)
    out["na_keep"] = np.tile(win.astype(f32), (2, 1))
    out["na_mask"] = np.tile(np.where(win, 0, NEG).astype(f32), (2, 1))
    dist = t[:, None] - t[None, :]
    causal = dist >= 0
    slopes = [2.0 ** -(h + 1) for h in range(8)]
    mult = causal * 1.0 + (causal & (dist % 4 == 0)) + (causal & (dist % 16 == 0))
    mult -= (dist > 128) * 1.0 * causal
    alibi = np.stack([np.where(causal, -s * dist, NEG) for s in slopes])
    dil = np.stack([np.where(mult > 0, -s * dist + np.log(np.maximum(mult, 1)), NEG) for s in slopes])

    def tiles(a):
        return np.concatenate([a[:, :128, :128], a[:, 128:, :]], 2).transpose(1, 0, 2).astype(f32)
    out["alibi"], out["dilated"] = tiles(alibi), tiles(dil)
    reset = np.ones((128, 2 * T), f32)
    reset[:, ::CH] = 0
    out["scan_reset"] = reset
    same = p[:, None] // CH == p[None, :] // CH
    fwd, bwd = same & (p[:, None] <= p[None, :]), same & (p[:, None] >= p[None, :])
    out["chunk_mask"] = np.stack([fwd, fwd, bwd, bwd], 1).astype(np.int32)
    out["slot_iota"] = np.tile(np.arange(1, CAP + 1, dtype=f32), (128, 1))
    out["ones"] = np.ones((128, 256), f32)
    cend = np.arange(16) * 16 + 31
    dc = t[:, None] - cend[None, :]
    ok = (dc >= 0) & (np.arange(16) < NCMP)[None, :]
    heads = np.array([[2 * hp + par for hp in range(4)] for par in range(2)])
    ca = np.where(ok[:, None, None, :], -np.array(slopes)[heads][None, :, :, None] * dc[:, None, None, :], NEG)
    out["cmp_bias"] = ca.reshape(2, 128, 128).transpose(1, 0, 2).astype(f32)
    out["cmp_keep"] = np.broadcast_to(ok[:, None, :], (T, 8, 16)).reshape(2, 128, 128).transpose(1, 0, 2).astype(f32)
    out["block_diag"] = ((2 * (p // 16 % 4) + p // 64)[:, None] == np.arange(8)[None, :]).astype(f32)
    sel = np.zeros((128, 128), f32)
    sel[::32] = 1
    out["sum_first"] = sel
    out["sum_groups"] = (p[:, None] % 32 == np.arange(16)[None, :]).astype(f32)
    return {k: np.ascontiguousarray(v) for k, v in out.items()}


def build(nc, A, out):
    ctx = ExitStack()

    def sb(name, shape, dt=FP32):
        return ctx.enter_context(nc.sbuf_tensor(name, shape, dt))

    sems = {}

    def S(name):
        if name not in sems:
            sems[name] = ctx.enter_context(nc.semaphore(name))
        return sems[name]

    y_dram = nc.dram_tensor("y_scratch", (E * CAP, D), FP32).ap()

    DIAG = 2 * 64 - 1
    diag = nc.dram_tensor("rpb_rows", (8, 7, 64, DIAG), FP32).ap()

    X = sb("X", [128, 2, D])
    HT = sb("HT", [128, KC * 512])
    WG = sb("WG", [128, WG_SLOTS, WG_W])
    TAB = sb("TAB", [128, 4096])
    BIG = sb("BIG", [128, GU_SLOTS * GU_W + DN_SLOTS * DN_W])
    GP2 = sb("GP2", [128, D])
    ident = sb("ident", [128, 128])
    cols = sb("cols", [128, 104])
    modc = sb("modc", [128, 48, 2])
    sc = sb("sc", [128, 768])
    BC = sb("BC", [128, 1152])
    PS = ctx.enter_context(nc.psum_tensor("PS", [128, 8, 512], FP32))

    def view(t, off, *dims):
        n = int(np.prod(dims))
        ap = t[:, off:off + n]
        if len(dims) == 2:
            ap = ap.rearrange("p (a b) -> p a b", b=dims[1])
        elif len(dims) == 3:
            ap = ap.rearrange("p (a b c) -> p a b c", b=dims[1], c=dims[2])
        elif len(dims) == 4:
            ap = ap.rearrange("p (a b c d) -> p a b c d", b=dims[1], c=dims[2], d=dims[3])
        return ap

    def laid(t, at=0):
        pos = [at]

        def place(*dims):
            n = int(np.prod(dims))
            pos[0] += n
            assert pos[0] <= t.shape[1], (pos[0], t.shape)
            return view(t, pos[0] - n, *dims)
        place.pos = pos
        return place

    s_at = laid(sc)
    stat = s_at(64)
    csil = s_at(8, 32)
    A1, A1c, A2 = s_at(8), s_at(8), s_at(8)
    lb, oml = s_at(4), s_at(4)
    lbt = s_at(12)
    negm, lsum, rls = s_at(8), s_at(96), s_at(96)
    lamt = s_at(8)
    aff = s_at(2, E)
    amax = s_at(2)
    best8 = s_at(8)

    bc_at = laid(BC)
    b_hg, b_qe, b_sub, b_qo, b_lam = bc_at(128), bc_at(4, 64), bc_at(128), bc_at(6, 64), bc_at(4, 64)

    PRE = 5
    at = laid(BIG)
    z = at(2, HG, 2 * T)
    qh = at(HG, T)
    ih = at(4, 512)
    gh = at(2, 512)
    kn = at(4, 512)
    vn = at(4, 512)
    qn = at(2, 512)
    at = laid(BIG, PRE * GU_W)
    GP1 = at(D)
    mixcat = at(2, D)
    mixo = mixcat
    free1 = at.pos[0]
    a0 = laid(BIG, 0)
    rows, xctx, xn = a0(128), a0(2, D), a0(4, D)
    a0 = laid(BIG, free1)
    mrow, sum_first, bgate = a0(2, 512), a0(128), a0(4, 512)
    ah = laid(BIG, free1)
    fgt, bcum, kk = ah(2, 512), ah(2, 512), ah(2, 512)
    kend = fgt
    qdec, kdec = ah(2, T), ah(2, T)
    eb, enb = qdec, kdec
    kendT, vbd = ah(2, 4, 128), ah(4, 4, 128)
    aT = ah(4, 128)
    states = ah(2, 10, 128)
    decay = ah(2, 16)
    reset = ah(512)
    cmask = ah(4, 128)
    rcos, rsin, na_keep, na_mask = ah(2, 64), ah(2, 64), ah(64), ah(64)
    w_rt, ones, slot = ah(KC, E), ah(T), ah(CAP)
    an = laid(BIG, free1)
    qr, kr, rt = an(2, 512), an(2, 512), an(512)
    pbuf, ptbuf = an(2, 512), an(2, 512)
    qrT, krT, qT, kcT = (view(HT, 1024 * i, 4, T) for i in range(4))
    am = laid(BIG, free1)
    mixT, h2T = view(HT, 0, KC, T), view(HT, 2048, KC, T)
    xn2 = am(2, D)
    lg = am(2, E)
    affT, work, posm, pos = am(T), am(T), am(T), am(T)
    posT = am(2, E)
    oh, ohg = am(2, E, CAP), am(2, E, CAP)

    def state_slot(n):
        return n % 2 if n < 7 else n - 5
    xs = view(HT, 0, KC, 512)
    tm = laid(TAB)
    sgt, xse, sig, hid = tm(4, T), tm(KC, CAP), tm(FG), tm(FG)
    hidT, ysb = tm(6, 128), tm(256)
    GU = view(BIG, 0, GU_SLOTS, GU_W)
    DN = view(BIG, GU_SLOTS * GU_W, DN_SLOTS, 2, D)
    na_tab = view(TAB, 0, 8, 2, T)

    ae = laid(BIG)
    ybuf = view(BIG, 0, 4, D)
    moeo = view(BIG, 4 * D, 2, D)
    qk = ae(4, 2, 512)
    vv, zz = ae(2, 2, 512), ae(2, 2, 512)
    tT = ae(4, 4, T)
    mixe = ae(2, D)
    mixeT = ae(KC, T)
    pb2, pt2 = ae(2, 512), ae(2, 512)
    tab_a, tab_c = ae(8, 384), ae(8, 384)
    t2 = ae(4096)
    xn3 = view(BIG, ae.pos[0] - 4096, 4, D)
    free2 = ae.pos[0]
    hTe = view(HT, 0, KC, T)
    mixo2 = view(HT, 2048, 2, D)
    ckv = view(BIG, 3 * 1024, 2, 512)
    kw = view(TAB, 0, 2, 280)
    to = laid(TAB, 560)
    gates = to(2, 24)
    dup = to(2, 2, 256)
    pe2, peT = to(2, 128), to(2, 32)
    w2 = to(2, 64)
    hidk, hidv = to(2, 16), to(8, 16)
    kcmp, kcmpT = to(2, 128), to(2, 16)
    cbias, ckeep = to(2, 128), to(2, 128)
    bdiag = to(8)
    ocmp = view(TAB, 560 + 2500, 2, 512)
    assert to.pos[0] <= 3060, to.pos[0]
    tab_a_off = 4096 + 2048 + 2048 + 4096 + 2048 + 2048 + 1024 + 1024
    ab = view(BIG, tab_a_off - 2048, 2, 32, 32)
    hrow, sum_groups = view(BIG, tab_a_off, 2, 2, 128), view(BIG, tab_a_off + 512, 16)
    kcvT = view(BIG, tab_a_off + 1024, 2, T)
    vbd2 = view(BIG, tab_a_off + 1536, 8, 64)
    pc = view(BIG, tab_a_off + 2048, 2, 128)
    pcT = view(BIG, tab_a_off + 2304, 2, 128)
    dupT = view(BIG, tab_a_off + 2560, 2, 256)
    dupTw = view(HT, 2048, 2, 256)

    def bank(i):
        return PS[:, i, :]

    def unit(lq, rk, tab, vblocks, outp, l, first=False, last=False, wait=None):
        return dict(s=[(0, lq, rk)] if not isinstance(lq, list) else lq, tab=tab, v=vblocks,
                    out=outp, l=l, first=first, last=last, wait=wait)

    def half(h):
        return slice(64 * (h % 2), 64 * (h % 2) + 64)

    def na_units():
        r = []
        for qt in range(2):
            for h in range(8):
                q = slice(128 * qt, 128 * qt + 128)
                s = [(0, qrT[half(h), h // 2, q], krT[half(h), h // 2, :]),
                     (T, qT[half(h), h // 2, q], kcT[half(h), h // 2, :])]
                v = [vn[:, b, 64 * h:64 * h + 64] for b in range(4)]
                r.append(dict(s=s, tab=na_tab[:, h, qt, :], v=v, c=64 * h, w=64, n=512,
                              last=h == 7, wait=None))
        return r

    def causal_units(qT_, kT_, tabs, vals, heads, per, width, group):
        r = []
        for qt in range(2):
            for i, (qi, ki, ti, vi) in enumerate(heads):
                q = slice(128 * qt, 128 * qt + 128)
                n = 128 * (qt + 1)
                s = [(0, qT_[half(qi), qi // 2, q], kT_(qi, ki)[:, 0:n])]
                tab = tabs[:, ti, 0:128] if qt == 0 else tabs[:, ti, 128:384]
                v = [vals[:, b, width * vi:width * vi + width] for b in range(qt + 1)]
                r.append(dict(s=s, tab=tab, v=v, c=width * (i % per), w=width, n=n,
                              last=i % per == per - 1, wait=None))
        return r

    aqT, akT, bqT, bkT = (tT[:, i] for i in range(4))
    cqT, ckT, dqT = aqT, akT, bqT
    av, bv = vv[:, 0], vv[:, 1]
    same_head = lambda t: (lambda qi, ki: t[half(ki), ki // 2, :])
    shared_head = lambda t: (lambda qi, ki: t[half(qi), ki, :])
    ATT = {
        "na": na_units(),
        "a": causal_units(aqT, same_head(akT), tab_a, av, [(h, h, h, h) for h in range(8)], 8, 64, 0),
        "b": causal_units(bqT, same_head(bkT), tab_c, bv,
                          [(2 * h + c, 2 * h + c, 2 * h + 1, h) for h in range(4) for c in range(2)], 4, 128, 0),
        "c": causal_units(cqT, same_head(ckT), tab_c, vv[:, 0], [(h, h, h, h) for h in range(8)], 8, 64, 0),
        "s": causal_units(dqT, shared_head(dupT), tab_c, ckv[:, :, 384:512],
                          [(h, h // 4, h, h // 4) for h in range(8)], 8, 64, 0),
        "w": causal_units(dqT, shared_head(dupTw), tab_c, kw[:, :, 128:256],
                          [(h, h // 4, h, h // 4) for h in range(8)], 8, 64, 0),
    }
    n0 = g0 = 0
    for k in ("na", "a", "b", "c", "s", "w"):
        for u in ATT[k]:
            u["i"], u["g"] = n0, g0
            n0 += 1
            g0 += u["last"]
    PB = {"na": (pbuf, ptbuf)}

    PROJ = []

    def units(matrix, what, arrays, tiles, w=512, f=ACT.Copy, scale=1.0, kind="tok"):
        first = len(PROJ)
        for t in range(tiles):
            PROJ.append((GROUP_OF[matrix, what], kind, t, w, arrays[:, t, :], f, scale))
        return first, len(PROJ)
    units("w_in", "zf", z[:, 0], HG, 2 * T, ACT.Sigmoid, kind="chan")
    units("w_in", "zb", z[:, 1], HG, 2 * T, ACT.Sigmoid, kind="chan")
    units("w_in", "qh", qh, HG, T, kind="chan")
    P_IH = units("w_in", "ih", ih, 4)[1]
    units("w_in", "gh", gh, 2, f=ACT.Sigmoid)
    units("w_in", "kn", kn, 4)
    units("w_in", "vn", vn, 4)
    P_IN = (0, units("w_in", "qn", qn, 2, scale=0.125)[1])

    def outs(matrix, dst):
        a = len(PROJ)
        for g in range(2):
            for t in range(2):
                PROJ.append((GROUP_OF[matrix, g], "tok", t, 512, dst[:, t, 512 * g:512 * g + 512], ACT.Copy, 1.0))
        return a, len(PROJ)
    P_OUT = outs("w_out", mixo)
    P_E = {}
    for name, dst, f in (("aq", qk[:, 0], ACT.Copy), ("ak", qk[:, 1], ACT.Copy), ("av", vv[:, 0], ACT.Copy),
                         ("bq", qk[:, 2], ACT.Copy), ("bk", qk[:, 3], ACT.Copy), ("az", zz[:, 0], ACT.Silu),
                         ("bv", vv[:, 1], ACT.Copy), ("bz", zz[:, 1], ACT.Silu)):
        P_E[name] = units("w_in_e_2", name, dst, 2, f=f)
    P_OUT_E = outs("w_out_e_2", X)
    P_O = {}
    for name, dst, f in (("kv", ckv, ACT.Copy), ("kw", kw, ACT.Copy), ("cq", qk[:, 0], ACT.Copy),
                         ("ck", qk[:, 1], ACT.Copy), ("dq", qk[:, 2], ACT.Copy), ("cv", vv[:, 0], ACT.Copy),
                         ("cz", zz[:, 0], ACT.Silu), ("dz", zz[:, 1], ACT.Silu)):
        P_O[name] = units("w_in_o_2", name, dst, 2, 280 if name == "kw" else 512, f=f)
    P_OUT_O = outs("w_out_o_2", X)

    FILLS = []

    def fill(parts, dst, rows_=128):
        FILLS.append((parts, dst, rows_))
        return len(FILLS)

    def tok_fills(src, dst):
        for j in range(4):
            fill([(src[:, t, 128 * k:128 * k + 128], 256 * (k % 2) + 128 * t)
                  for k in (2 * j, 2 * j + 1) for t in range(2)], dst[:, 2 * j:2 * j + 2, :])

    def head_fills(src, dst):
        for j in range(2):
            fill([(src[:, t, 128 * k:128 * k + 128], 256 * (k % 2) + 128 * t)
                  for k in (2 * j, 2 * j + 1) for t in range(2)], dst[:, 2 * j:2 * j + 2, :])
    marks = {}

    def begin(name):
        marks[name] = [len(FILLS), None]

    def end(name):
        marks[name][1] = len(FILLS)
    for h in range(HG):
        begin(f"kend{h}")
        for d in range(2):
            fill([(kend[:, d, 128 * t:128 * t + 128], 128 * t) for t in range(4)], kendT[:, d])
        end(f"kend{h}")
    begin("na")
    for src, dst in ((qr, qrT), (kr, krT), (qn, qT), (kn[:, 2:4], kcT)):
        head_fills(src, dst)
    end("na")
    begin("mix"), tok_fills(mixcat, mixT), end("mix")
    begin("h2"), tok_fills(xn2, h2T), end("h2")
    begin("aff"), fill([(aff[:, t, :], 128 * t) for t in range(2)], affT[0:E, :], E), end("aff")
    begin("pos"), fill([(posm[0:E, 128 * t:128 * t + 128], E * t) for t in range(2)], posT), end("pos")
    begin("sg")
    for j in range(2):
        fill([(ohg[:, t, 4 * b:4 * b + 4, :].rearrange("p a b -> p (a b)"), 256 * (b % 2) + 128 * t) for b in (2 * j, 2 * j + 1) for t in range(2)],
             sgt[:, 2 * j:2 * j + 2, :])
    end("sg")
    begin("he"), tok_fills(xn3, hTe), end("he")
    for i, name in enumerate(("aq", "ak", "bq", "bk")):
        begin(name), head_fills(qk[:, i], tT[:, i]), end(name)
    begin("mixe"), tok_fills(mixe, mixeT), end("mixe")
    begin("ho"), tok_fills(xn3, hTe), end("ho")
    begin("cmp")
    fill([(ckv[:, t, 128 * s:128 * s + 128], 256 * s + 128 * t) for s in range(2) for t in range(2)], kcvT)
    fill([(pe2[0:32, s], 32 * s) for s in range(2)], peT)
    end("cmp")
    begin("cq"), head_fills(qk[:, 0], tT[:, 0]), end("cq")
    begin("ck"), head_fills(qk[:, 1], tT[:, 1]), end("ck")
    begin("kcmp"), fill([(kcmp[0:16, h], 16 * h) for h in range(2)], kcmpT), end("kcmp")
    begin("dq"), head_fills(qk[:, 2], tT[:, 2]), end("dq")
    begin("dup")
    for i, dst in ((0, dupT), (1, dupTw)):
        fill([(dup[:, i, t, 128 * k:128 * k + 128], 256 * k + 128 * t) for k in range(2) for t in range(2)], dst)
    end("dup")
    begin("pc"), fill([(pc[:, t, :], 128 * t) for t in range(2)], pcT), end("pc")
    begin("mixo"), tok_fills(mixe, mixeT), end("mixo")

    need, landed = [], [0] * WG_SLOTS
    for n, (_, _, what) in enumerate(GROUPS):
        landed[n % WG_SLOTS] += 16 * (len(what) or 2)
        need.append(landed[n % WG_SLOTS])
    last_unit = {}
    for n, u in enumerate(PROJ):
        last_unit[u[0]] = n
    used_by = [("mod_ready", w + 1) if m == "w_mod" else ("phi_psum", w + 1) if m == "phi_w1"
               else ("proj_ready", last_unit[g] + 1) for g, (m, w, _) in enumerate(GROUPS)]
    DBLK, dsum = [], [0] * DN_SLOTS
    for q in range(12):
        j, part = q // 3, q % 3
        dsum[q % DN_SLOTS] += 32 if part == 2 else 16
        DBLK.append((j, [2 * part, 2 * part + 1], q % DN_SLOTS, dsum[q % DN_SLOTS]))
    assert len(set(dsum)) == 1
    DSUM = dsum[0]

    MOD_AT = {2: 1, 3: 2, 4: 3, 5: 4, 6: 1, 7: 2, 8: 5, 9: 6, 10: 7, 11: 8}

    def stepper(eng, chain):
        count = {}

        def step(ins, signal=chain):
            count[signal] = count.get(signal, 0) + 1
            ins.then_inc(S(signal), 1)
            eng.wait_ge(S(signal), count[signal])
        return step

    block = ctx.enter_context(nc.Block())

    @block.sync
    def _(sp):
        sp.dma_start(rows[0:8, :], A["g_pre1"][0].rearrange("(a b) -> a b", b=128)).then_inc(S("rows_in"), 16)
        sp.dma_start(rows[8:16, :], A["g_pre2"][0].rearrange("(a b) -> a b", b=128)).then_inc(S("rows_in"), 16)
        sp.dma_start(rows[16:24, :], A["ln_e_2"][0].rearrange("(a b) -> a b", b=128)).then_inc(S("rows_in"), 16)
        sp.dma_start(rows[24:32, :], A["ln_o_2"][0].rearrange("(a b) -> a b", b=128)).then_inc(S("rows_in"), 16)
        sp.dma_start(rows[32:40, :], A["hg_lb_logits"].rearrange("l (a b) -> (l a) b", b=128)).then_inc(S("rows_in"), 16)
        sp.dma_start(rows[40:48, :], A["c"][0].rearrange("(a b) -> a b", b=128)).then_inc(S("rows_in"), 16)
        sp.dma_start(rows[48:56, :], A["c_ctx"].rearrange("(a b) -> a b", b=128)).then_inc(S("rows_in"), 16)
        sp.dma_start(rows[56:104, :], A["b_mod"][0].rearrange("(a b) -> a b", b=128)).then_inc(S("rows_in"), 16)
        sp.dma_start(ident[:, :], A["ident"]).then_inc(S("rows_in"), 16)
        sp.dma_start(X[:, :, :], A["x"][0].rearrange("(t p) d -> p t d", p=128)).then_inc(S("x_in"), 16)
        sp.dma_start(xctx, A["ctx"][0].rearrange("(t p) d -> p t d", p=128)).then_inc(S("x_in"), 16)
        for i in range(2):
            sp.dma_start(view(bgate[0:1].rearrange("p a b -> p (a b)"), D * i, D), A["b_mod"][:, (2 + 3 * i) * D:(3 + 3 * i) * D]
                         ).then_inc(S("mod_in"), 16)

        def load_group(n):
            name, what, ranges = GROUPS[n]
            slot_ = n % WG_SLOTS
            if n >= WG_SLOTS:
                sp.wait_ge(S(used_by[n - WG_SLOTS][0]), used_by[n - WG_SLOTS][1])
            if name == "phi_w1":
                for hf in range(2):
                    sp.dma_start(WG[64 * hf:64 * hf + 64, slot_, :], A[name][what]).then_inc(S(f"wg_in{slot_}"), 16)
                return
            width = sum(w for _, w in ranges)
            dst = view(WG[:, slot_, :], 0, KC, width)
            o = 0
            for c0, w in ranges:
                sp.dma_start(dst[:, :, o:o + w],
                             A[name][0].rearrange("(k p) c -> p k c", p=128)[:, :, c0:c0 + w]
                             ).then_inc(S(f"wg_in{slot_}"), 16)
                o += w
        for n in range(GROUP_OF["w_out", 1] + 1):
            load_group(n)
        gate_d, up_d, down_d = (A[n][0] for n in ("w_gate", "w_up", "w_down"))

        def load_chunk(e, i):
            src = (gate_d if i % 2 == 0 else up_d)[e, 128 * (i // 2):128 * (i // 2) + 128, :]
            sp.dma_start(GU[:, i % GU_SLOTS, :], src).then_inc(S(f"gu_in{i % GU_SLOTS}"), 16)

        def load_expert(e, first):
            for i in range(PRE if first else 0, 2 * KC):
                if not (first and i < GU_SLOTS):
                    sp.wait_ge(S("gu_used"), 2 * KC * e + (i - GU_SLOTS + 1))
                load_chunk(e, i)
            for i, (j, (s0, s1), slot_, _) in enumerate(DBLK):
                if not (first and i < DN_SLOTS):
                    sp.wait_ge(S("dn_used"), 12 * e + (i - DN_SLOTS + 1))
                r0 = FG * j + 128 * s0
                if FS[s1] == 128:
                    sp.dma_start(DN[:, slot_, :, :], down_d[e, r0:r0 + 256, :].rearrange("(s p) d -> p s d", p=128)
                                 ).then_inc(S(f"dn_in{slot_}"), 16)
                else:
                    sp.dma_start(DN[:, slot_, 0, :], down_d[e, r0:r0 + 128, :]).then_inc(S(f"dn_in{slot_}"), 16)
                    sp.dma_start(DN[0:FS[s1], slot_, 1, :], down_d[e, r0 + 128:r0 + 128 + FS[s1], :]
                                 ).then_inc(S(f"dn_in{slot_}"), 16)
        sp.wait_ge(S("mixcat_ready"), 2)
        for i in range(PRE):
            load_chunk(0, i)
        for n in range(GROUP_OF["w_out", 1] + 1, GROUP_OF["w_out", 1] + 1 + WG_SLOTS):
            load_group(n)
        sp.wait_ge(S("xs_done"), KC)
        sp.wait_ge(S("tr_copied"), marks["sg"][1])
        load_expert(0, True)
        with sp.Fori(1, E) as e:
            load_expert(e, False)
        y_v = y_dram.rearrange("(b p) d -> p b d", p=128)
        sp.wait_ge(S("gu_used"), 2 * KC * E)
        sp.wait_ge(S("y_stored"), 16 * (E - 4))
        sp.dma_start(ybuf[:, 0:3, :], y_v[:, 0:3, :]).then_inc(S("y_back"), 16)
        sp.wait_ge(S("y_stored"), 16 * E)
        sp.dma_start(ybuf[:, 3, :], y_v[:, 3, :]).then_inc(S("y_last"), 16)
        for n in range(GROUP_OF["w_out", 1] + 1 + WG_SLOTS, len(GROUPS)):
            load_group(n)
        sp.wait_ge(S("x_final"), 1)
        sp.dma_start(out[0].rearrange("(t p) d -> p t d", p=128), X[:, :, :]).then_inc(S("out_done"), 16)
        sp.wait_ge(S("out_done"), 16)

    @block.gpsimd
    def _(pool):
        pool.dma_start(sum_first, A["sum_first"]).then_inc(S("gate_in"), 16)
        pool.dma_start(GP1, A["g_post1"][0].partition_broadcast(128)).then_inc(S("gate_in"), 16)
        pool.dma_start(GP2[:, :], A["g_post2"][0].partition_broadcast(128)).then_inc(S("gate_in"), 16)
        nc.gpsimd.memset(csil, 0.0).then_inc(S("csil_zero"), 1)
        pool.dma_start(reset, A["scan_reset"]).then_inc(S("hg_in"), 16)
        pool.dma_start(cmask.bitcast(I32), A["chunk_mask"]).then_inc(S("hg_in"), 16)
        pool.dma_start(b_hg, A["hg_norm"][0].partition_broadcast(128)).then_inc(S("hg_in"), 16)
        pool.dma_start(na_keep, A["na_keep"]).then_inc(S("na_in"), 16)
        pool.dma_start(na_mask, A["na_mask"]).then_inc(S("na_in"), 16)
        for a, n in ((rcos, "rope_cos"), (rsin, "rope_sin")):
            pool.dma_start(a, A[n].rearrange("(t p) c -> p t c", p=128)).then_inc(S("na_in"), 16)
        pool.dma_start(w_rt, A["w_router"][0].rearrange("(k p) e -> p k e", p=128)).then_inc(S("rt_in"), 16)
        pool.dma_start(ones, A["ones"]).then_inc(S("rt_in"), 16)
        pool.dma_start(slot, A["slot_iota"]).then_inc(S("rt_in"), 16)
        rpb = A["na_rpb"]
        RH, RW = rpb.shape[2], rpb.shape[3]
        for h in range(8):
            src = bass.AP(tensor=rpb.tensor, offset=rpb.offset + h * RH * RW + 4 * RW + 15 - 63,
                          ap=[[0, 64], [RW, 7], [1, DIAG]])
            pool.dma_start(diag[h].rearrange("r q c -> q r c"), src).then_inc(S("diag_out"), 16)
        pool.wait_ge(S("diag_out"), 8 * 16)
        for r in range(4):
            for h in range(8):
                src = bass.AP(tensor=diag.tensor, offset=diag.offset + (h * 7 + 3 - r) * 64 * DIAG + 63,
                              ap=[[DIAG - 1, 64], [64 * DIAG, 4], [1, 64]])
                dst = na_tab[64 * (r % 2):64 * (r % 2) + 64, h, r // 2, :].rearrange("p (a b) -> p a b", b=64)
                pool.dma_start(dst, src).then_inc(S("rpb_in"), 16)
        pool.wait_ge(S("na_in"), 64)
        pool.wait_ge(S("rpb_in"), 32 * 16)
        tab = view(TAB, 0, 64, 64)
        bro = lambda a: a.unsqueeze(1).to_broadcast([128, 64, 64])
        nc.gpsimd.tensor_tensor(tab, tab, bro(na_keep), ALU.mult).then_inc(S("na_tab"), 1)
        pool.wait_ge(S("na_tab"), 1)
        nc.gpsimd.tensor_tensor(tab, tab, bro(na_mask), ALU.add).then_inc(S("na_tab"), 1)
        pool.wait_ge(S("gp_done"), 4)
        nc.gpsimd.memset(vbd, 0.0).then_inc(S("vbd_zero"), 1)
        nc.gpsimd.memset(aT, 0.0).then_inc(S("vbd_zero"), 1)
        pool.wait_ge(S("vbd_zero"), 2)
        pool.wait_ge(S("proj_evac"), P_IH)
        for h in range(HG):
            if h:
                pool.wait_ge(S("hg_o"), h)
            for c in range(4):
                nc.gpsimd.tensor_copy(vbd[32 * c:32 * c + 32, :, c, :],
                                      ih[32 * c:32 * c + 32, :, 128 * h:128 * h + 128]).then_inc(S("vbd_ready"), 1)
        pool.wait_ge(S("x_moe"), 1)
        pool.dma_start(tab_a, A["dilated"]).then_inc(S("even_in"), 16)
        pool.dma_start(tab_c, A["alibi"]).then_inc(S("even_in"), 16)
        pool.dma_start(b_qe, A["qkn_e_2"][0].partition_broadcast(128)).then_inc(S("even_in"), 16)
        pool.dma_start(b_sub, A["subln_e_2"][0].partition_broadcast(128)).then_inc(S("even_in"), 16)
        pool.dma_start(b_lam, A["lam_e_2"][0].partition_broadcast(128)).then_inc(S("even_in"), 16)
        pool.dma_start(b_qo, A["qkn_o_2"][0].partition_broadcast(128)).then_inc(S("even_in"), 16)
        for s in range(2):
            for dd in range(2):
                pool.dma_start(pe2[0:32, s, 64 * dd:64 * dd + 64], A["phi_pe_2"][0, s]).then_inc(S("odd_in"), 16)
        pool.dma_start(w2, A["phi_w2_2"][0].rearrange("s p c -> p s c")).then_inc(S("odd_in"), 16)
        pool.dma_start(cbias, A["cmp_bias"]).then_inc(S("odd_in"), 16)
        pool.dma_start(ckeep, A["cmp_keep"]).then_inc(S("odd_in"), 16)
        pool.dma_start(bdiag, A["block_diag"]).then_inc(S("odd_in"), 16)
        pool.wait_ge(S("mixe_ready"), 1)
        pool.dma_start(sum_groups, A["sum_groups"]).then_inc(S("cmp_in"), 16)
        nc.gpsimd.memset(ab, 0.0).then_inc(S("ab_zero"), 1)

    @block.tensor
    def _(pe):
        mm = nc.tensor.matmul

        def do_fills(name):
            for i in range(*marks[name]):
                parts, dst, rows_ = FILLS[i]
                if i >= 2:
                    pe.wait_ge(S("tr_copied"), i - 1)
                for src, c in parts:
                    k, m = src.shape
                    last = nc.tensor.transpose(PS[0:m, 4 + i % 2, c:c + k], src, ident[0:k, 0:k])
                last.then_inc(S("tr_ready"), 1)

        def project(units_, lhs):
            for n in range(*units_):
                g, kind, j, w, *_ = PROJ[n]
                if PROJ[n - 1][0] != g:
                    pe.wait_ge(S(f"wg_in{g % WG_SLOTS}"), need[g])
                if n >= 2:
                    pe.wait_ge(S("proj_evac"), n - 1)
                width = sum(x for _, x in GROUPS[g][2])
                wt = view(WG[:, g % WG_SLOTS, :], 0, KC, width)
                for k in range(KC):
                    if kind == "chan":
                        last = mm(bank(n % 2)[:, 0:w], wt[:, k, 128 * j:128 * j + 128], lhs[:, k, 0:w],
                                  start=k == 0, stop=k == KC - 1)
                    else:
                        last = mm(bank(n % 2)[:, 0:w], lhs[:, k, 128 * j:128 * j + 128], wt[:, k, 0:w],
                                  start=k == 0, stop=k == KC - 1)
                last.then_inc(S("proj_ready"), 1)
        
        def attention(name, between=None):
            us = ATT[name]
            pb, pt = PB.get(name, (pb2, pt2))
            window = name == "na"

            def scores(u):
                i = u["i"]
                if i >= 2:
                    pe.wait_ge(S("exp_done" if window else "max_ready"), i - 1)
                o = bank(2 + i % 2)
                if window:
                    mm(o[:, 0:T], ident[:, :], u["tab"], start=True, stop=False)
                for c, q, k in u["s"]:
                    last = mm(o[:, c:c + k.shape[1]], q, k, start=c > 0 or not window, stop=True)
                last.then_inc(S("s_ready"), 1)

            def turn(u):
                i = u["i"]
                pe.wait_ge(S("exp_done"), i + 1)
                if i >= 2:
                    pe.wait_ge(S("pt_copied"), i - 1)
                for b in range(u["n"] // 128):
                    last = nc.tensor.transpose(bank(4 + i % 2)[:, 128 * b:128 * b + 128],
                                               pb[:, i % 2, 128 * b:128 * b + 128], ident[:, :])
                last.then_inc(S("pT_done"), 1)

            def values(u):
                i, g = u["i"], u["g"]
                pe.wait_ge(S("pt_copied"), i + 1)
                if g >= 2:
                    pe.wait_ge(S("o_read"), g - 1)
                nb = u["n"] // 128
                for b in range(nb):
                    last = mm(bank(6 + g % 2)[:, u["c"]:u["c"] + u["w"]], pt[:, i % 2, 128 * b:128 * b + 128],
                              u["v"][b], start=b == 0, stop=b == nb - 1)
                last.then_inc(S("pv_done"), 1)
            for k in range(len(us) + 2):
                if k < len(us):
                    scores(us[k])
                if between and k % 2 == 0 and between[0] + k // 2 < between[1]:
                    project((between[0] + k // 2, between[0] + k // 2 + 1), between[2])
                if 1 <= k <= len(us):
                    turn(us[k - 1])
                if k >= 2:
                    values(us[k - 2])

        pe.wait_ge(S("rows_in"), 9 * 16)
        nc.tensor.transpose(PS[:, 7, 0:104], rows[0:104, :], ident[0:104, 0:104]).then_inc(S("rowsT"), 1)

        def modulation(pair):
            for g in pair:
                n = GROUP_OF["w_mod", g]
                pe.wait_ge(S(f"wg_in{n % WG_SLOTS}"), need[n])
                if g >= 2:
                    pe.wait_ge(S("mod_evac"), g - 1)
                wt = view(WG[:, n % WG_SLOTS, :], 0, KC, 512)
                for k in (0, 2, 4, 6, 1, 3, 5, 7):
                    last = mm(PS[32 * (k // 2):32 * (k // 2) + 32, 6 + g % 2, :], csil[:, k, :], wt[:, k, :],
                              start=k % 2 == 0, stop=k % 2 == 1)
                last.then_inc(S("mod_ready"), 1)
            for g in pair:
                pe.wait_ge(S("mod_evac"), g + 1)
                if g >= 2:
                    pe.wait_ge(S("gp_done" if g in (6, 7) else "modc_done"), MOD_AT[g])
                if g % 6 in (4, 5):
                    i = (4, 5, 10, 11).index(g)
                    mm(bank(4 + g % 2), sum_first, mrow[:, g % 2, :], start=True, stop=False)
                    last = mm(bank(4 + g % 2), sum_first[0:1, :], bgate[0:1, i, :], start=False, stop=True)
                else:
                    for j in range(4):
                        last = nc.tensor.transpose(bank(4 + g % 2)[:, 128 * j:128 * j + 128],
                                                   mrow[:, g % 2, 128 * j:128 * j + 128], ident[:, :])
                last.then_inc(S("modT"), 1)
        pe.wait_ge(S("csil_ready"), 1)
        pe.wait_ge(S("gate_in"), 48)
        pe.wait_ge(S("mod_in"), 32)
        modulation((0, 1))
        modulation((2, 3))
        pe.wait_ge(S("xn_ready"), 4)
        for k in range(KC):
            if k >= 2:
                pe.wait_ge(S("hT_done"), 2 * (k - 1))
            for t in range(4):
                last = nc.tensor.transpose(bank(6 + k % 2)[:, 128 * t:128 * t + 128],
                                           xn[:, t, 128 * k:128 * k + 128], ident[:, :])
            last.then_inc(S("hT_ready"), 1)
        pe.wait_ge(S("hT_done"), 2 * KC)
        hT = view(HT, 0, KC, 512)
        project((0, 4), hT)
        modulation((4, 5))
        project((4, 8), hT)
        modulation((6, 7))
        project((8, 12), hT)
        modulation((8, 9))
        project((12, P_IH), hT)
        modulation((10, 11))
        rest = iter(range(P_IH, P_IN[1]))

        def project_next():
            n = next(rest)
            project((n, n + 1), hT)
        for h in range(HG):
            pe.wait_ge(S("hg_dec"), h + 1)
            do_fills(f"kend{h}")
            def ring_bank(i):
                if 9 * h + i >= 2:
                    pe.wait_ge(S("kv_used"), 9 * h + i - 1)
                return bank(2 + (9 * h + i) % 2)
            o = ring_bank(0)
            for d in range(2):
                for t in range(2):
                    a = 2 * d + t
                    last = mm(o[:, 128 * a:128 * a + 128], kdec[:, d, 128 * t:128 * t + 128],
                              qdec[:, d, 128 * t:128 * t + 128], start=True, stop=True)
            last.then_inc(S("kv_ready"), 1)
            project_next()
            pe.wait_ge(S("tr_copied"), marks[f"kend{h}"][1])
            pe.wait_ge(S("vbd_ready"), 4 * (h + 1))
            for j in range(8):
                d = j % 2
                t = ((2, 3, 0, 1), (3, 2, 1, 0))[d][j // 2]
                mm(ring_bank(1 + j), kendT[:, d, t, :], vbd[:, t, :, :].rearrange("p a b -> p (a b)"),
                   start=True, stop=True).then_inc(S("kv_ready"), 1)
                if j in (3, 7):
                    project_next()
            pe.wait_ge(S("states_ready"), h + 1)
            if h == 0:
                pe.wait_ge(S("mod_evac"), 12)
            for t in range(2):
                o = PS[:, 6 + t, 128 * h:128 * h + 128]
                for d in range(2):
                    mm(o, aT[:, 2 * d + t, :], ih[:, t, 128 * h:128 * h + 128], start=d == 0, stop=False)
                for d in range(2):
                    for c in range(4):
                        n = 4 * t + c
                        s = state_slot(7 + n if d == 0 else 14 - n)
                        last = mm(o[32 * c:32 * c + 32, :], qdec[:, d, 32 * n:32 * n + 32], states[:, d, s, :],
                                  start=False, stop=d == 1)
            last.then_inc(S("hg_o"), 1)
        pe.wait_ge(S("rope_ready"), 1)
        do_fills("na")
        pe.wait_ge(S("tr_copied"), marks["na"][1])
        pe.wait_ge(S("na_tab"), 2)
        pe.wait_ge(S("hg_read"), 2)
        attention("na")
        pe.wait_ge(S("mixcat_ready"), 2)
        do_fills("mix")
        pe.wait_ge(S("tr_copied"), marks["mix"][1])
        project(P_OUT, mixT)
        pe.wait_ge(S("xn2_ready"), 2)
        do_fills("h2")
        pe.wait_ge(S("h2_ready"), KC)
        pe.wait_ge(S("rt_in"), 48)
        for t in range(2):
            for k in range(KC):
                last = mm(PS[:, 6, E * t:E * t + E], h2T[:, k, 128 * t:128 * t + 128], w_rt[:, k, :],
                          start=k == 0, stop=k == KC - 1)
        last.then_inc(S("lg_ready"), 1)
        pe.wait_ge(S("aff_ready"), 1)
        do_fills("aff")
        pe.wait_ge(S("pos_ready"), 1)
        do_fills("pos")
        pe.wait_ge(S("oh_ready"), 2)
        for k in range(KC):
            if k >= 2:
                pe.wait_ge(S("xs_done"), k - 1)
            for t in range(2):
                last = mm(bank(6 + k % 2), xn2[:, t, 128 * k:128 * k + 128],
                          oh[:, t].rearrange("p a b -> p (a b)"), start=t == 0, stop=t == 1)
            last.then_inc(S("xs_psum"), 1)
        pe.wait_ge(S("ohg_ready"), 2)
        do_fills("sg")

        def expert(e, first):
            pe.wait_ge(S("xse_ready"), e + 1)
            if not first:
                pe.wait_ge(S("hid_ready"), e)
            for i in range(2 * KC):
                k, up, slot_ = i // 2, i % 2, i % GU_SLOTS
                pe.wait_ge(S(f"gu_in{slot_}"), 32 * e + 16 * (i // GU_SLOTS + 1))
                for hf in range(2):
                    for g in range(4):
                        c0 = FG * g + FH * hf
                        last = mm(PS[32 * g:32 * g + 32, 2 * up + hf, 0:FH], xse[:, k, :],
                                  GU[:, slot_, c0:c0 + FH], start=k == 0, stop=k == KC - 1)
                last.then_inc(S("gu_used"), 1)
            pe.wait_ge(S("hid_ready"), e + 1)
            if not first:
                pe.wait_ge(S("hidT_copied"), 3 * e)
            for s, n in enumerate(FS):
                last = nc.tensor.transpose(PS[0:n, 4 + s // 4, 128 * (s % 4):128 * (s % 4) + 128],
                                           hid[:, 128 * s:128 * s + n], ident[:, :])
            last.then_inc(S("hidT_done"), 1)
            pe.wait_ge(S("hidT_copied"), 3 * e + 3)
            if not first:
                pe.wait_ge(S("y_copied"), e)
            for i, (j, ss, slot_, v) in enumerate(DBLK):
                pe.wait_ge(S(f"dn_in{slot_}"), DSUM * e + v)
                for s in ss:
                    for g in range(4):
                        last = mm(PS[32 * g:32 * g + 32, 6, 0:256], hidT[0:FS[s], s, 32 * j:32 * j + 32],
                                  DN[0:FS[s], slot_, s % 2, 256 * g:256 * g + 256],
                                  start=i == 0 and s == 0, stop=i == 11 and s == ss[-1])
                last.then_inc(S("dn_used"), 1)
        expert(0, True)
        with pe.Fori(1, E) as e:
            expert(e, False)
        pe.wait_ge(S("y_back"), 16)
        pe.wait_ge(S("y_last"), 16)
        for t in range(2):
            for hf in range(2):
                for b in range(4):
                    last = mm(bank(2 * t + hf), sgt[:, b, 128 * t:128 * t + 128], ybuf[:, b, 512 * hf:512 * hf + 512],
                              start=b == 0, stop=b == 3)
                last.then_inc(S("moe_psum"), 1)
        pe.wait_ge(S("xn3_ready"), 2)
        do_fills("he")
        pe.wait_ge(S("he_ready"), KC)
        for name in ("aq", "ak", "av", "bq"):
            project(P_E[name], hTe)
        pe.wait_ge(S("heads_ready"), 1)
        do_fills("aq")
        pe.wait_ge(S("heads_ready"), 2)
        do_fills("ak")
        project(P_E["bk"], hTe)
        pe.wait_ge(S("heads_ready"), 3)
        do_fills("bq")
        pe.wait_ge(S("tr_copied"), marks["bq"][1])
        pe.wait_ge(S("even_in"), 96)
        attention("a", (P_E["az"][0], P_E["bz"][1], hTe))
        pe.wait_ge(S("pt_copied"), ATT["a"][-1]["i"] + 1)
        pe.wait_ge(S("heads_ready"), 4)
        do_fills("bk")
        pe.wait_ge(S("tr_copied"), marks["bk"][1])
        pe.wait_ge(S("proj_evac"), P_E["bz"][1])
        attention("b")
        pe.wait_ge(S("mixe_ready"), 1)
        do_fills("mixe")
        pe.wait_ge(S("tr_copied"), marks["mixe"][1])
        project(P_OUT_E, mixeT)
        pe.wait_ge(S("xn3_ready"), 4)
        do_fills("ho")
        pe.wait_ge(S("he_ready"), 2 * KC)
        project(P_O["kv"], hTe)
        project(P_O["kw"], hTe)
        pe.wait_ge(S("proj_evac"), P_O["kv"][1])
        pe.wait_ge(S("odd_in"), 8 * 16)
        do_fills("cmp")
        project(P_O["cq"], hTe)
        pe.wait_ge(S("ab_ready"), 4)
        for s in range(2):
            g = GROUP_OF["phi_w1", s]
            pe.wait_ge(S(f"wg_in{g % WG_SLOTS}"), need[g])
            wt = view(WG[:, g % WG_SLOTS, :], 0, 32, 128)
            for l in range(32):
                for h in range(2):
                    c = l % 4
                    last = mm(PS[32 * c:32 * c + 32, 2 + h, 128 * s:128 * s + 128], ab[64 * h:64 * h + 64, s, l, :],
                              wt[64 * h:64 * h + 64, l, :], start=l < 4, stop=l >= 28)
            last.then_inc(S("phi_psum"), 1)
        project(P_O["ck"], hTe)
        pe.wait_ge(S("hrow_ready"), 2)
        pe.wait_ge(S("cmp_in"), 16)
        for s in range(2):
            for h in range(2):
                last = mm(PS[:, 6, 32 * s + 16 * h:32 * s + 16 * h + 16], hrow[:, h, s, :], sum_groups, start=True, stop=True)
        last.then_inc(S("hidT_psum"), 1)
        project((P_O["dq"][0], P_O["dq"][0] + 1), hTe)
        pe.wait_ge(S("phi_hid"), 10)
        for h in range(2):
            mm(PS[0:16, 7, 64 + 64 * h:128 + 64 * h], hidk[:, h, :], w2[:, 0, :], start=True, stop=True)
        mm(PS[:, 7, 0:64], hidv.rearrange("p a b -> p (a b)"), w2[:, 1, :], start=True, stop=True
           ).then_inc(S("kcmp_psum"), 1)
        project((P_O["dq"][0] + 1, P_O["dq"][1]), hTe)
        pe.wait_ge(S("heads_ready"), 5)
        do_fills("cq")
        pe.wait_ge(S("heads_ready"), 6)
        do_fills("ck")
        project(P_O["cv"], hTe)
        pe.wait_ge(S("kcmp_ready"), 1)
        do_fills("kcmp")
        pe.wait_ge(S("heads_ready"), 7)
        do_fills("dq")
        pe.wait_ge(S("dup_ready"), 1)
        do_fills("dup")
        pe.wait_ge(S("tr_copied"), marks["dup"][1])
        for t in range(2):
            for h in (0, 2, 4, 6, 1, 3, 5, 7):
                last = mm(PS[:, 2 + h % 2, 64 * t + 16 * (h // 2):64 * t + 16 * (h // 2) + 16],
                          dqT[half(h), h // 2, 128 * t:128 * t + 128], kcmpT[half(h), h // 4, :], start=True, stop=True)
        last.then_inc(S("sc_psum"), 1)
        n = P_O["cz"][0]
        project((n, n + 1), hTe)
        pe.wait_ge(S("pc_ready"), 1)
        do_fills("pc")
        pe.wait_ge(S("tr_copied"), marks["pc"][1])
        pe.wait_ge(S("vbd2_ready"), 1)
        for t in range(2):
            last = mm(bank(6 + t), pcT[:, t, :], vbd2.rearrange("p a b -> p (a b)"), start=True, stop=True)
        last.then_inc(S("oc_psum"), 1)
        project((n + 1, n + 2), hTe)
        pe.wait_ge(S("oc_read"), 1)
        attention("c", (*P_O["dz"], hTe))
        attention("s")
        attention("w")
        pe.wait_ge(S("mixo_ready"), 1)
        do_fills("mixo")
        pe.wait_ge(S("tr_copied"), marks["mixo"][1])
        project(P_OUT_O, mixeT)

    @block.scalar
    def _(act):
        fn = nc.scalar.activation
        step = stepper(act, "act_step")
        roots = [0]

        def root(n):
            roots[0] += 1
            act.wait_ge(S("ms_ready"), roots[0])
            fn(stat[:, 0:n], stat[:, 0:n], ACT.Sqrt).then_inc(S("root_ready"), 1)

        def copy_fills(name):
            for i in range(*marks[name]):
                _, dst, rows_ = FILLS[i]
                act.wait_ge(S("tr_ready"), i + 1)
                w = int(np.prod(dst.shape[1:]))
                src = view(PS[:, 4 + i % 2, :], 0, *dst.shape[1:])
                fn(dst if rows_ == 128 or dst.shape[0] == rows_ else dst[0:rows_], src[0:rows_], ACT.Copy
                   ).then_inc(S("tr_copied"), 1)

        def evacuate(a, b):
            for n in range(a, b):
                _, _, _, w, dst, f, scale = PROJ[n]
                act.wait_ge(S("proj_ready"), n + 1)
                fn(dst, bank(n % 2)[:, 0:w], f, scale=scale).then_inc(S("proj_evac"), 1)

        def attention(name, between=None):
            pb, _ = PB.get(name, (pb2, pt2))
            for k, u in enumerate(ATT[name]):
                i, n = u["i"], u["n"]
                act.wait_ge(S("max_ready"), i + 1)
                if name == "na":
                    if i >= 2:
                        act.wait_ge(S("pT_done"), i - 1)
                    fn(pb[:, i % 2, 0:n], bank(2 + i % 2)[:, 0:n], ACT.Exp, bias=negm[:, i % 8:i % 8 + 1],
                       accum_out=lsum[:, i:i + 1]).then_inc(S("exp_done"), 1)
                else:
                    fn(pb[:, i % 2, 0:n], pb[:, i % 2, 0:n], ACT.Exp, bias=negm[:, i % 8:i % 8 + 1], scale=-1.0,
                       accum_out=lsum[:, i:i + 1]).then_inc(S("exp_done"), 1)
                if between and k % 2 == 1 and between[0] + k // 2 < between[1]:
                    evacuate(between[0] + k // 2, between[0] + k // 2 + 1)

        act.wait_ge(S("cols_ready"), 1)
        act.wait_ge(S("csil_zero"), 1)
        fn(csil[:, :, 0:2].rearrange("p k w -> p w k"), view(cols, 40, 2, 8), ACT.Sigmoid).then_inc(S("csig"), 1)
        act.wait_ge(S("lb_in"), 1)
        fn(lbt[:, 0:8], lbt[:, 0:8], ACT.Exp).then_inc(S("lb_exp"), 1)
        root(4)
        evacuate(0, P_IH)
        rest = iter(range(P_IH, P_IN[1]))

        def evacuate_next():
            n = next(rest)
            evacuate(n, n + 1)

        def hg_log(h):
            act.wait_ge(S("hg_f"), h + 1)
            fn(fgt, fgt, ACT.Ln).then_inc(S("hg_ln"), 1)
        hg_log(0)
        for h in range(HG):
            act.wait_ge(S("hg_b"), h + 1)
            if h:
                act.wait_ge(S("hg_o"), h)
            fn(eb, bcum[:, :, 0:T], ACT.Exp).then_inc(S("hg_exp"), 1)
            fn(enb, bcum[:, :, 0:T], ACT.Exp, scale=-1.0).then_inc(S("hg_exp"), 1)
            fn(kend, kend, ACT.Exp).then_inc(S("hg_exp"), 1)
            fn(decay[:, 0, :], bcum[:, 0, CH - 1::CH], ACT.Exp).then_inc(S("hg_exp"), 1)
            fn(decay[:, 1, :], bcum[:, 1, 0::CH], ACT.Exp).then_inc(S("hg_exp"), 1)
            copy_fills(f"kend{h}")
            evacuate_next()
            if h + 1 < HG:
                hg_log(h + 1)
            evacuate_next()
            evacuate_next()
        act.wait_ge(S("hg_o"), HG)
        for t in range(2):
            fn(fgt[:, t], bank(6 + t), ACT.Square).then_inc(S("hg_sq"), 1)
        root(8)
        copy_fills("na")
        attention("na")
        copy_fills("mix")
        evacuate(*P_OUT)
        root(2)
        root(2)
        copy_fills("h2")
        act.wait_ge(S("lg_shift"), 1)
        fn(lg, lg, ACT.Exp).then_inc(S("lg_exp"), 1)
        copy_fills("aff")
        copy_fills("pos")
        copy_fills("sg")

        def expert(e, first):
            act.wait_ge(S("gu_used"), 2 * KC * e + 2 * KC)
            if not first:
                act.wait_ge(S("hid_ready"), e)
            fn(view(sig, 0, 2, FH), PS[:, 0:2, 0:FH], ACT.Sigmoid).then_inc(S("sig_ready"), 1)
            act.wait_ge(S("hidT_done"), e + 1)
            if not first:
                act.wait_ge(S("dn_used"), 12 * e)
            fn(hidT[:, 0:4, :], view(PS[:, 4, :], 0, 4, 128), ACT.Copy).then_inc(S("hidT_copied"), 1)
            fn(hidT[:, 4, :], PS[:, 5, 0:128], ACT.Copy).then_inc(S("hidT_copied"), 1)
            fn(hidT[0:FS[5], 5, :], PS[0:FS[5], 5, 128:256], ACT.Copy).then_inc(S("hidT_copied"), 1)
            act.wait_ge(S("dn_used"), 12 * e + 12)
            if not first:
                act.wait_ge(S("y_stored"), 16 * e)
            fn(ysb, PS[:, 6, 0:256], ACT.Copy).then_inc(S("y_copied"), 1)
            act.wait_ge(S("y_copied"), e + 1)
            dst = y_dram.rearrange("(e s) (g c) -> e g s c", s=CAP, c=256)
            act.dma_start(dst[e], ysb).then_inc(S("y_stored"), 16)
        expert(0, True)
        with act.Fori(1, E) as e:
            expert(e, False)
        for i in range(4):
            act.wait_ge(S("moe_psum"), i + 1)
            fn(moeo[:, i // 2, 512 * (i % 2):512 * (i % 2) + 512], bank(i), ACT.Copy).then_inc(S("moe_evac"), 1)
        root(2)
        root(2)
        copy_fills("he")
        evacuate(P_E["aq"][0], P_E["aq"][1])
        act.wait_ge(S("lam_in"), 1)
        fn(lamt[:, 0:2], lamt[:, 0:2], ACT.Exp).then_inc(S("lam_exp"), 1)
        evacuate(P_E["ak"][0], P_E["ak"][0] + 1)
        root(16)
        evacuate(P_E["ak"][0] + 1, P_E["av"][1])
        root(16)
        evacuate(*P_E["bq"])
        copy_fills("aq")
        copy_fills("ak")
        root(16)
        evacuate(*P_E["bk"])
        copy_fills("bq")
        root(16)
        attention("a", (P_E["az"][0], P_E["bz"][1]))
        copy_fills("bk")
        attention("b")
        root(8)
        copy_fills("mixe")
        root(2)
        copy_fills("ho")
        evacuate(P_O["kv"][0], P_O["kw"][1])
        act.wait_ge(S("proj_evac"), P_O["kw"][1])
        fn(gates, kw[:, :, 256:280], ACT.Sigmoid).then_inc(S("gates_ready"), 1)
        copy_fills("cmp")
        evacuate(*P_O["cq"])
        root(16)
        act.wait_ge(S("phi_psum"), 2)
        act.wait_ge(S("cmp_in"), 16)
        for h in range(2):
            fn(hrow[:, h], view(PS[:, 2 + h, :], 0, 2, 128), ACT.Copy).then_inc(S("hrow_ready"), 1)
        evacuate(*P_O["ck"])
        act.wait_ge(S("hid_zero"), 2)
        act.wait_ge(S("hidT_psum"), 1)
        for h in range(2):
            fn(hidk[:, h, 0:NCMP], PS[:, 6, 16 * h:16 * h + NCMP], ACT.Silu).then_inc(S("phi_hid"), 1)
        for h in range(8):
            fn(hidv[:, h, 0:NCMP], PS[:, 6, 32 + 16 * (h % 4 // 2):32 + 16 * (h % 4 // 2) + NCMP], ACT.Silu
               ).then_inc(S("phi_hid"), 1)
        root(16)
        evacuate(*P_O["dq"])
        copy_fills("cq")
        copy_fills("ck")
        root(2)
        root(24)
        evacuate(*P_O["cv"])
        copy_fills("kcmp")
        copy_fills("dq")
        copy_fills("dup")
        evacuate(P_O["cz"][0], P_O["cz"][0] + 1)
        act.wait_ge(S("sc_shift"), 1)
        fn(pc, pc, ACT.Exp).then_inc(S("sc_exp"), 1)
        copy_fills("pc")
        evacuate(P_O["cz"][0] + 1, P_O["cz"][1])
        attention("c", P_O["dz"])
        attention("s")
        attention("w")
        copy_fills("mixo")

    @block.vector
    def _(dve):
        v = nc.vector
        step = stepper(dve, "dve_step")
        roots = [0]

        def rms(items, n, width):
            for src, junk, c in items:
                step(v.tensor_tensor_reduce(out=junk, in0=src, in1=src, scale=1.0, scalar=0.0, op0=ALU.mult,
                                            op1=ALU.add, accum_out=stat[:, c:c + 1]))
            roots[0] += 1
            step(v.tensor_scalar(stat[:, 0:n], stat[:, 0:n], 1.0 / width, EPS, ALU.mult, ALU.add), "ms_ready")
            dve.wait_ge(S("root_ready"), roots[0])
            step(v.reciprocal(stat[:, 0:n], stat[:, 0:n]))

        def prenorm(dst, signal):
            rms([(X[:, t, :], dst[:, t, :], t) for t in range(2)], 2, D)
            for t in range(2):
                step(v.tensor_scalar(dst[:, t, :], X[:, t, :], stat[:, t:t + 1], None, ALU.mult), signal)

        def postnorm(src, gain, junk, signal="dve_step"):
            rms([(src[:, t, :], junk[:, t, :], t) for t in range(2)], 2, D)
            for t in range(2):
                step(v.scalar_tensor_tensor(src[:, t, :], src[:, t, :], stat[:, t:t + 1], gain, ALU.mult, ALU.mult))
            step(v.tensor_tensor(X[:, :, :], X[:, :, :], src, ALU.add), signal)

        def scale_chunks(hT_, col0, shift, name, signal):
            dve.wait_ge(S("tr_copied"), marks[name][1])
            for k in range(KC):
                step(v.tensor_scalar(hT_[:, k, :], hT_[:, k, :], col0[:, k:k + 1],
                                     None if shift is None else shift[:, k:k + 1], ALU.mult,
                                     ALU.bypass if shift is None else ALU.add), signal)

        def headed(ap, n, w):
            return ap.unsqueeze(2).to_broadcast([128, n, w])

        def attention(name, finish):
            us = ATT[name]
            pb, pt = PB.get(name, (pb2, pt2))
            for k in range(len(us) + 2):
                if k < len(us):
                    i, n = us[k]["i"], us[k]["n"]
                    dve.wait_ge(S("s_ready"), i + 1)
                    if i >= 8:
                        dve.wait_ge(S("exp_done"), i - 7)
                    if name == "na":
                        v.tensor_reduce(negm[:, i % 8:i % 8 + 1], bank(2 + i % 2)[:, 0:n], AX, ALU.max, negate=True
                                        ).then_inc(S("max_ready"), 1)
                    else:
                        if i >= 2:
                            dve.wait_ge(S("pT_done"), i - 1)
                        v.tensor_tensor_reduce(out=pb[:, i % 2, 0:n], in0=bank(2 + i % 2)[:, 0:n], in1=us[k]["tab"],
                                               scale=-1.0, scalar=3e38, op0=ALU.add, op1=ALU.min,
                                               accum_out=negm[:, i % 8:i % 8 + 1]).then_inc(S("max_ready"), 1)
                if 1 <= k <= len(us):
                    i, n = us[k - 1]["i"], us[k - 1]["n"]
                    dve.wait_ge(S("pT_done"), i + 1)
                    if i >= 2:
                        dve.wait_ge(S("pv_done"), i - 1)
                    v.tensor_copy(pt[:, i % 2, 0:n], bank(4 + i % 2)[:, 0:n]).then_inc(S("pt_copied"), 1)
                if k >= 2 and us[k - 2]["last"]:
                    u = us[k - 2]
                    per = 512 // u["w"]
                    i0 = u["i"] - per + 1
                    dve.wait_ge(S("pv_done"), u["i"] + 1)
                    dve.wait_ge(S("exp_done"), u["i"] + 1)
                    step(v.reciprocal(rls[:, i0:i0 + per], lsum[:, i0:i0 + per]))
                    finish((k - 2) // per, bank(6 + u["g"] % 2), rls[:, i0:i0 + per])

        dve.wait_ge(S("rowsT"), 1)
        step(v.tensor_copy(cols[:, :], PS[:, 7, 0:104]), "cols_ready")
        dve.wait_ge(S("csig"), 1)
        cs = csil[:, :, 0:2].rearrange("p k w -> p w k")
        step(v.tensor_tensor(cs, cs, view(cols, 40, 2, 8), ALU.mult), "csil_ready")
        step(v.tensor_tensor(lbt[:, 8:12], cols[:, 32:36], cols[:, 36:40], ALU.max))
        step(v.tensor_tensor(lbt[:, 4:8], cols[:, 36:40], lbt[:, 8:12], ALU.subtract))
        step(v.tensor_tensor(lbt[:, 0:4], cols[:, 32:36], lbt[:, 8:12], ALU.subtract), "lb_in")
        dve.wait_ge(S("lb_exp"), 1)
        step(v.tensor_tensor(lbt[:, 8:12], lbt[:, 0:4], lbt[:, 4:8], ALU.add))
        step(v.reciprocal(lbt[:, 8:12], lbt[:, 8:12]))
        step(v.tensor_tensor(lb, lbt[:, 0:4], lbt[:, 8:12], ALU.mult))
        step(v.tensor_scalar(oml, lb, -1.0, 1.0, ALU.mult, ALU.add))
        dve.wait_ge(S("x_in"), 32)
        toks = [X[:, 0, :], X[:, 1, :], xctx[:, 0, :], xctx[:, 1, :]]
        rms([(a, xn[:, t, :], t) for t, a in enumerate(toks)], 4, D)
        for t, a in enumerate(toks):
            step(v.tensor_scalar(xn[:, t, :], a, stat[:, t:t + 1], None, ALU.mult), "xn_ready")

        def modulation(pair):
            for g in pair:
                dve.wait_ge(S("mod_ready"), g + 1)
                step(v.tensor_copy(mrow[:, g % 2, :], bank(6 + g % 2)), "mod_evac")
            for g in pair:
                dve.wait_ge(S("modT"), g + 1)
                if g % 6 in (4, 5):
                    gp = view(GP1 if g < 6 else GP2[:, :], 512 * (g % 2), 512)
                    step(v.tensor_tensor(gp, gp, bank(4 + g % 2), ALU.mult), "gp_done")
                else:
                    parts = bank(4 + g % 2).rearrange("p (b g f) -> p b f g", g=4, f=32)[:, :, 0:2, :]
                    m = modc[:, 4 * g:4 * g + 4, :]
                    step(v.tensor_reduce(m, parts, AX, ALU.add))
                    step(v.tensor_tensor(m, m, headed(cols[:, 56 + 4 * g:60 + 4 * g], 4, 2), ALU.add), "modc_done")
        modulation((0, 1))
        modulation((2, 3))
        for dst, w in ((A1, 0), (A1c, 1)):
            step(v.scalar_tensor_tensor(dst, modc[:, 8:16, w], 1.0, cols[:, 0:8], ALU.add, ALU.mult))
        for k in range(KC):
            dve.wait_ge(S("hT_ready"), k + 1)
            for w, a in ((0, A1), (1, A1c)):
                step(v.tensor_scalar(view(HT, 0, KC, 512)[:, k, T * w:T * w + T], bank(6 + k % 2)[:, T * w:T * w + T],
                                     a[:, k:k + 1], modc[:, k, w:w + 1], ALU.mult, ALU.add), "hT_done")
        for pair in ((4, 5), (6, 7), (8, 9), (10, 11)):
            modulation(pair)
        step(v.scalar_tensor_tensor(A2, modc[:, 32:40, 0], 1.0, cols[:, 8:16], ALU.add, ALU.mult))
        dve.wait_ge(S("hg_in"), 48)

        def hg_gates(h):
            if h == 0:
                dve.wait_ge(S("proj_evac"), 12)
                dve.wait_ge(S("modT"), 12)
            else:
                dve.wait_ge(S("tr_copied"), marks[f"kend{h - 1}"][1])
            for d in range(2):
                step(v.tensor_scalar(fgt[:, d], z[:, d, h, :], oml[:, h:h + 1], lb[:, h:h + 1], ALU.mult, ALU.add))
            step(v.tensor_scalar(kk, fgt, -1.0, 1.0, ALU.mult, ALU.add), "hg_f")
            dve.wait_ge(S("hg_ln"), h + 1)
            step(v.tensor_tensor_scan(bcum[:, 0], reset, fgt[:, 0], 0.0, ALU.mult, ALU.add))
            step(v.tensor_tensor_scan(bcum[:, 1, ::-1], reset, fgt[:, 1, ::-1], 0.0, ALU.mult, ALU.add))
            for d in range(2):
                b = bcum[:, d].rearrange("p (n c) -> p n c", c=CH)
                e = b[:, :, CH - 1:CH] if d == 0 else b[:, :, 0:1]
                step(v.tensor_tensor(kend[:, d].rearrange("p (n c) -> p n c", c=CH),
                                     e.to_broadcast([128, 16, CH]), b, ALU.subtract))
            dve.sem_inc(S("hg_b"), 1)

        def hg_decay(h):
            dve.wait_ge(S("hg_exp"), 5 * h + 5)
            step(v.tensor_tensor(kdec, kk[:, :, 0:T], enb, ALU.mult))
            for d in range(2):
                step(v.tensor_tensor(qdec[:, d], qh[:, h], eb[:, d], ALU.mult))
            step(v.tensor_tensor(kend, kend, kk, ALU.mult), "hg_dec")
        hg_gates(0)
        hg_decay(0)
        dve.wait_ge(S("vbd_zero"), 2)
        for h in range(HG):
            dve.wait_ge(S("kv_ready"), 9 * h + 1)
            if h:
                dve.wait_ge(S("hg_o"), h)
            step(v.copy_predicated(aT, cmask.bitcast(I32), view(bank(2 + 9 * h % 2), 0, 4, 128)), "kv_used")
            if h + 1 < HG:
                hg_gates(h + 1)
            for j in range(8):
                d, s = j % 2, j // 2
                t = ((2, 3, 0, 1), (3, 2, 1, 0))[d][s]
                dve.wait_ge(S("kv_ready"), 9 * h + j + 2)
                for i in range(4):
                    c = i if d == 0 else 3 - i
                    kv = bank(2 + (9 * h + j + 1) % 2)[:, 128 * c:128 * c + 128]
                    n = 4 * s + i
                    sig_ = "kv_used" if i == 3 else "dve_step"
                    if n == 0:
                        step(v.tensor_copy(states[:, d, 0, :], kv))
                    elif n < 15:
                        step(v.scalar_tensor_tensor(states[:, d, state_slot(n), :], states[:, d, state_slot(n - 1), :],
                                                    decay[:, d, 4 * t + c:4 * t + c + 1], kv, ALU.mult, ALU.add), sig_)
                    else:
                        step(v.tensor_copy(stat[:, 0:1], kv[:, 0:1]), sig_)
            dve.sem_inc(S("states_ready"), 1)
            if h + 1 < HG:
                hg_decay(h + 1)
        dve.wait_ge(S("hg_sq"), 2)
        step(v.tensor_reduce(stat[:, 0:8], view(fgt.rearrange("p a b -> p (a b)"), 0, 8, 128), AX, ALU.add))
        rms([], 8, HG * 32)
        for t in range(2):
            m = mixcat[:, t, 512:D].rearrange("p (h c) -> p h c", c=128)
            step(v.tensor_tensor(m, view(bank(6 + t), 0, 4, 128), headed(stat[:, 4 * t:4 * t + 4], 4, 128), ALU.mult), "hg_read")
            step(v.tensor_tensor(m, m, b_hg.unsqueeze(1).to_broadcast([128, 4, 128]), ALU.mult))
            step(v.tensor_tensor(mixcat[:, t, 512:D], mixcat[:, t, 512:D], gh[:, t, :], ALU.mult))
        dve.wait_ge(S("proj_evac"), P_IN[1])
        dve.wait_ge(S("na_in"), 64)
        for src, dst in ((qn, qr), (kn, kr)):
            for t in range(2):
                x3 = src[:, t, :].rearrange("p (h c) -> p h c", c=64)
                y3 = dst[:, t, :].rearrange("p (h c) -> p h c", c=64)
                step(v.tensor_tensor(y3, x3, rcos[:, t, :].unsqueeze(1).to_broadcast([128, 8, 64]), ALU.mult))
                for hf in range(2):
                    for j in range(2):
                        a, b = 32 * hf + 16 * j, 32 * hf + 16 * (1 - j)
                        step(v.tensor_tensor(view(rt, 0, 8, 64)[:, :, a:a + 16], x3[:, :, b:b + 16],
                                             rsin[:, t, a:a + 16].unsqueeze(1).to_broadcast([128, 8, 16]), ALU.mult))
                step(v.tensor_tensor(dst[:, t, :], dst[:, t, :], rt, ALU.add))
        dve.sem_inc(S("rope_ready"), 1)

        def na_finish(i, o, r):
            step(v.tensor_tensor(mixcat[:, i, 0:512].rearrange("p (h c) -> p h c", c=64), view(o, 0, 8, 64),
                                 headed(r, 8, 64), ALU.mult), "o_read")
            dve.sem_inc(S("mixcat_ready"), 1)
        attention("na", na_finish)
        dve.wait_ge(S("proj_evac"), P_OUT[1])
        postnorm(mixo, GP1, xn2)
        prenorm(xn2, "xn2_ready")
        scale_chunks(h2T, A2, modc[:, 24:32, 0], "h2", "h2_ready")
        dve.wait_ge(S("lg_ready"), 1)
        step(v.tensor_reduce(amax, view(PS[:, 6, :], 0, 2, E), AX, ALU.max, negate=True))
        step(v.tensor_tensor(lg, view(PS[:, 6, :], 0, 2, E), headed(amax, 2, E), ALU.add), "lg_shift")
        dve.wait_ge(S("lg_exp"), 1)
        step(v.tensor_reduce(amax, lg, AX, ALU.add))
        step(v.reciprocal(amax, amax))
        step(v.tensor_tensor(aff, lg, headed(amax, 2, E), ALU.mult), "aff_ready")
        dve.wait_ge(S("tr_copied"), marks["aff"][1])
        src = affT
        for i in range(CAP // 8):
            step(v.max(best8[0:E, :], src[0:E, :]))
            step(v.match_replace(work[0:E, :], best8[0:E, :], src[0:E, :], -1.0))
            src = work
        dve.wait_ge(S("rt_in"), 48)
        step(v.tensor_scalar(work[0:E, :], work[0:E, :], -1.0, None, ALU.is_equal))
        step(v.tensor_tensor_scan(pos[0:E, :], ones[0:E, :], work[0:E, :], 0.0, ALU.mult, ALU.add))
        step(v.tensor_tensor(posm[0:E, :], pos[0:E, :], work[0:E, :], ALU.mult), "pos_ready")
        dve.wait_ge(S("tr_copied"), marks["pos"][1])
        for t in range(2):
            step(v.tensor_tensor(oh[:, t], headed(posT[:, t, :], E, CAP),
                                 slot.unsqueeze(1).to_broadcast([128, E, CAP]), ALU.is_equal), "oh_ready")
        for t in range(2):
            step(v.tensor_tensor(ohg[:, t], oh[:, t], headed(aff[:, t, :], E, CAP), ALU.mult), "ohg_ready")
        for k in range(KC):
            dve.wait_ge(S("xs_psum"), k + 1)
            step(v.tensor_scalar(xs[:, k, :], bank(6 + k % 2), A2[:, k:k + 1], modc[:, 24 + k, 0:1],
                                 ALU.mult, ALU.add), "xs_done")

        def expert(e, first):
            if not first:
                dve.wait_ge(S("gu_used"), 2 * KC * e)
            v.tensor_copy(xse, xs[:, :, bass.ds(e * CAP, CAP)]).then_inc(S("xse_ready"), 1)
            dve.wait_ge(S("sig_ready"), e + 1)
            if not first:
                dve.wait_ge(S("hidT_done"), e)
            v.tensor_tensor(view(sig, 0, 2, FH), view(sig, 0, 2, FH), PS[:, 0:2, 0:FH], ALU.mult
                            ).then_inc(S("silu_ready"), 1)
            dve.wait_ge(S("silu_ready"), e + 1)
            v.tensor_tensor(view(hid, 0, 2, FH), view(sig, 0, 2, FH), PS[:, 2:4, 0:FH], ALU.mult
                            ).then_inc(S("hid_ready"), 1)
        expert(0, True)
        with dve.Fori(1, E) as e:
            expert(e, False)
        dve.wait_ge(S("moe_evac"), 4)
        postnorm(moeo, GP2[:, :], view(BIG, 6 * D, 2, D), "x_moe")

        def norm_heads(i, evac, gain):
            dve.wait_ge(S("proj_evac"), evac)
            x, sq = view(BIG, 1024 * i, 16, 64), view(BIG, t2_off, 16, 64)
            step(v.tensor_tensor(sq, x, x, ALU.mult))
            step(v.tensor_reduce(stat[:, 0:16], sq, AX, ALU.add))
            rms([], 16, 64)
            step(v.tensor_tensor(x, x, headed(stat[:, 0:16], 16, 64), ALU.mult))
            step(v.tensor_tensor(x, x, gain.unsqueeze(1).to_broadcast([128, 16, 64]), ALU.mult), "heads_ready")
        t2_off = ae.pos[0] - 4096
        prenorm(xn3, "xn3_ready")
        scale_chunks(hTe, cols[:, 16:24], None, "he", "he_ready")
        dve.wait_ge(S("even_in"), 96)
        for b in (b_qe, b_qo):
            step(v.tensor_scalar(b[:, 0::2, :][:, 0:2], b[:, 0::2, :][:, 0:2], 0.125, None, ALU.mult))
        step(v.tensor_tensor(b_lam[:, 0::2, :], b_lam[:, 0::2, :], b_lam[:, 1::2, :], ALU.mult))
        step(v.tensor_reduce(lamt[:, 0:2], b_lam[:, 0::2, :], AX, ALU.add), "lam_in")
        dve.wait_ge(S("lam_exp"), 1)
        step(v.tensor_tensor(lamt[:, 2:3], lamt[:, 0:1], lamt[:, 1:2], ALU.subtract))
        step(v.tensor_scalar(lamt[:, 2:3], lamt[:, 2:3], LAM_INIT, None, ALU.add))
        for i, name in enumerate(("aq", "ak", "bq", "bk")):
            norm_heads(i, P_E[name][1], b_qe[:, i, :])

        def plain_finish(dst, zz_):
            def finish(i, o, r):
                m = dst[:, i, 0:512].rearrange("p (h c) -> p h c", c=64)
                step(v.tensor_tensor(m, view(o, 0, 8, 64), headed(r, 8, 64), ALU.mult), "o_read")
                step(v.tensor_tensor(dst[:, i, 0:512], dst[:, i, 0:512], zz_[:, i, :], ALU.mult))
            return finish

        def diff_finish(i, o, r):
            qt, pair = i // 2, i % 2
            ov = view(o, 0, 2, 2, 128)
            r2 = r.rearrange("p (h c) -> p h c", c=2)
            step(v.tensor_scalar(r2[:, :, 1], r2[:, :, 1], lamt[:, 2:3], None, ALU.mult))
            t0, t1 = view(BIG, t2_off, 2, 128), view(BIG, t2_off + 256, 2, 128)
            for c, t_ in ((0, t0), (1, t1)):
                step(v.tensor_tensor(t_, ov[:, :, c, :], headed(r2[:, :, c], 2, 128), ALU.mult))
            m = mixe[:, qt, 512 + 256 * pair:768 + 256 * pair].rearrange("p (h c) -> p h c", c=128)
            step(v.tensor_tensor(m, t0, t1, ALU.subtract), "o_read")
        attention("a", plain_finish(mixe, zz[:, 0]))
        attention("b", diff_finish)
        ob = [mixe[:, t, 512:D].rearrange("p (h c) -> p h c", c=128) for t in range(2)]
        for t in range(2):
            sq = view(BIG, t2_off + 512 * t, 4, 128)
            step(v.tensor_tensor(sq, ob[t], ob[t], ALU.mult))
            step(v.tensor_reduce(stat[:, 4 * t:4 * t + 4], sq, AX, ALU.add))
        rms([], 8, 128)
        step(v.tensor_scalar(b_sub, b_sub, 1.0 - LAM_INIT, None, ALU.mult))
        for t in range(2):
            step(v.tensor_tensor(ob[t], ob[t], headed(stat[:, 4 * t:4 * t + 4], 4, 128), ALU.mult))
            step(v.tensor_tensor(ob[t], ob[t], b_sub.unsqueeze(1).to_broadcast([128, 4, 128]), ALU.mult))
            step(v.tensor_tensor(mixe[:, t, 512:D], mixe[:, t, 512:D], zz[:, 1][:, t, :], ALU.mult))
        dve.sem_inc(S("mixe_ready"), 1)

        def add_units(a, b):
            for n in range(a, b):
                _, _, _, w, dst, _, _ = PROJ[n]
                dve.wait_ge(S("proj_ready"), n + 1)
                v.tensor_tensor(dst, dst, bank(n % 2), ALU.add).then_inc(S("proj_evac"), 1)
                dve.wait_ge(S("proj_evac"), n + 1)
        add_units(*P_OUT_E)
        prenorm(xn3, "xn3_ready")
        scale_chunks(hTe, cols[:, 24:32], None, "ho", "he_ready")
        step(v.memset(hidk, 0.0), "hid_zero")
        step(v.memset(hidv, 0.0), "hid_zero")
        dve.wait_ge(S("tr_copied"), marks["cmp"][1])
        dve.wait_ge(S("ab_zero"), 1)
        for s in range(2):
            kv2 = kcvT[:, s, :].rearrange("p (i b) -> p b i", b=16)
            for a in range(2):
                step(v.tensor_tensor(ab[:, s, 16 * a:16 * a + 16, 0:NCMP], kv2[:, :, a:a + NCMP],
                                     peT[:, s, 16 * a:16 * a + 16].unsqueeze(2).to_broadcast([128, 16, NCMP]),
                                     ALU.add), "ab_ready")
        norm_heads(0, P_O["cq"][1], b_qo[:, 0, :])
        norm_heads(1, P_O["ck"][1], b_qo[:, 1, :])
        dve.wait_ge(S("kcmp_psum"), 1)
        kp = view(PS[:, 7, :], 64, 2, 64)[0:16]
        k0 = view(BIG, t2_off, 2, 64)[0:16]
        tq = view(BIG, t2_off + 128, 2, 64)[0:16]
        step(v.tensor_copy(k0, kp))
        step(v.tensor_tensor(tq, k0, k0, ALU.mult))
        step(v.memset(stat[:, 0:2], 1.0))
        step(v.tensor_reduce(stat[0:16, 0:2], tq, AX, ALU.add))
        rms([], 2, 64)
        step(v.tensor_tensor(k0, k0, stat[0:16, 0:2].unsqueeze(2).to_broadcast([16, 2, 64]), ALU.mult))
        for dd in range(2):
            step(v.tensor_tensor(kcmp[0:16, :, 64 * dd:64 * dd + 64], k0,
                                 b_qo[0:16, 3, :].unsqueeze(1).to_broadcast([16, 2, 64]), ALU.mult))
        dve.sem_inc(S("kcmp_ready"), 1)
        dve.wait_ge(S("proj_evac"), P_O["dq"][1])
        x, sq = view(BIG, 2048, 16, 64), view(BIG, t2_off, 16, 64)
        step(v.tensor_tensor(sq, x, x, ALU.mult))
        step(v.tensor_reduce(stat[:, 0:16], sq, AX, ALU.add))
        for i, src in ((0, ckv[:, :, 256:384]), (1, kw[:, :, 0:128])):
            for t in range(2):
                s2 = src[:, t, :].rearrange("p (h c) -> p h c", c=64)
                tq = view(BIG, t2_off + 3072 + 128 * (2 * i + t), 2, 64)
                step(v.tensor_tensor(tq, s2, s2, ALU.mult))
                step(v.tensor_reduce(stat[:, 16 + 4 * i + 2 * t:18 + 4 * i + 2 * t], tq, AX, ALU.add))
        rms([], 24, 64)
        step(v.tensor_tensor(x, x, headed(stat[:, 0:16], 16, 64), ALU.mult))
        step(v.tensor_tensor(x, x, b_qo[:, 2, :].unsqueeze(1).to_broadcast([128, 16, 64]), ALU.mult), "heads_ready")
        for i, src, gain in ((0, ckv[:, :, 256:384], 4), (1, kw[:, :, 0:128], 5)):
            for t in range(2):
                s2 = src[:, t, :].rearrange("p (h c) -> p h c", c=64)
                step(v.tensor_tensor(s2, s2, headed(stat[:, 16 + 4 * i + 2 * t:18 + 4 * i + 2 * t], 2, 64), ALU.mult))
                for dd in range(2):
                    step(v.tensor_tensor(view(dup[:, i, t, :], 0, 2, 2, 64)[:, :, dd, :], s2,
                                         b_qo[:, gain, :].unsqueeze(1).to_broadcast([128, 2, 64]), ALU.mult))
        dve.sem_inc(S("dup_ready"), 1)
        step(v.tensor_tensor(vbd2, PS[:, 7, 0:64].unsqueeze(1).to_broadcast([128, 8, 64]),
                             bdiag.unsqueeze(2).to_broadcast([128, 8, 64]), ALU.mult), "vbd2_ready")
        dve.wait_ge(S("sc_psum"), 1)
        for par in range(2):
            step(v.tensor_tensor(pc[:, :, 64 * par:64 * par + 64], view(PS[:, 2 + par, :], 0, 2, 64),
                                 cbias[:, :, 64 * par:64 * par + 64], ALU.add))
        p16 = view(pc.rearrange("p a b -> p (a b)"), 0, 16, 16)
        step(v.tensor_reduce(stat[:, 0:16], p16, AX, ALU.max))
        step(v.tensor_tensor(p16, p16, headed(stat[:, 0:16], 16, 16), ALU.subtract), "sc_shift")
        dve.wait_ge(S("sc_exp"), 1)
        step(v.tensor_tensor(pc, pc, ckeep, ALU.mult))
        step(v.tensor_reduce(stat[:, 0:16], p16, AX, ALU.add))
        step(v.tensor_scalar(stat[:, 0:16], stat[:, 0:16], 1e-30, None, ALU.max))
        step(v.reciprocal(stat[:, 0:16], stat[:, 0:16]))
        step(v.tensor_tensor(p16, p16, headed(stat[:, 0:16], 16, 16), ALU.mult), "pc_ready")
        dve.wait_ge(S("oc_psum"), 1)
        dve.wait_ge(S("gates_ready"), 1)
        g3 = gates.rearrange("p t (h j) -> p t h j", j=3)
        for t in range(2):
            step(v.tensor_tensor(ocmp[:, t, :].rearrange("p (h c) -> p h c", c=64), view(bank(6 + t), 0, 8, 64),
                                 headed(g3[:, t, :, 0], 8, 64), ALU.mult))
        dve.sem_inc(S("oc_read"), 1)

        def gated_finish(j):
            def finish(i, o, r):
                step(v.tensor_tensor(r, r, g3[:, i, :, j], ALU.mult))
                t_ = view(BIG, t2_off, 8, 64)
                step(v.tensor_tensor(t_, view(o, 0, 8, 64), headed(r, 8, 64), ALU.mult), "o_read")
                o3 = ocmp[:, i, :].rearrange("p (h c) -> p h c", c=64)
                step(v.tensor_tensor(o3, o3, t_, ALU.add))
            return finish
        dve.wait_ge(S("proj_evac"), P_O["cz"][1])
        attention("c", plain_finish(mixe, zz[:, 0]))
        attention("s", gated_finish(1))
        attention("w", gated_finish(2))
        for t in range(2):
            step(v.tensor_tensor(mixe[:, t, 512:D], ocmp[:, t, :], zz[:, 1][:, t, :], ALU.mult))
        dve.sem_inc(S("mixo_ready"), 1)
        add_units(*P_OUT_O)
        dve.sem_inc(S("x_final"), 1)

    ctx.close()


def kernel(**inputs):
    import concourse.bacc as _bacc
    from concourse.bass_utils import run_bass_kernel_spmd as _run

    nc = _bacc.Bacc("TRN2", target_bir_lowering=False, num_devices=1, dynamic_dma_scratch_size=4096)
    arrays, aps = {}, {}
    w1 = np.asarray(inputs.pop("phi_w1_2"))[0].reshape(2, 32, 64, 128)
    inputs["phi_w1"] = w1.transpose(0, 2, 1, 3).reshape(2, 64, 32 * 128)
    for name, a in [*inputs.items(), *constants().items()]:
        a = np.ascontiguousarray(a)
        arrays[f"in_{name}"] = a
        aps[name] = nc.dram_tensor(f"in_{name}", a.shape, mybir.dt.from_np(a.dtype), kind="ExternalInput").ap()
    out = nc.dram_tensor("out_x", (1, T, D), FP32, kind="ExternalOutput").ap()
    build(nc, aps, out)
    r = _run(nc, [arrays], core_ids=[0])
    return r.results[0]["out_x"]
```

```python
import numpy as np
import concourse.bass as bass
from concourse import mybir
from contextlib import ExitStack

FP32 = mybir.dt.float32
I32 = mybir.dt.int32
ALU = mybir.AluOpType
ACT = mybir.ActivationFunctionType
AX = mybir.AxisListType.X

D = 1024
T = 256
KC = D // 128
EPS = 1e-6
NEG = -1e30
E = 16
CAP = 2 * T // E
F = 2752
FG = F // 4
FH = FG // 2
FS = [128] * (FG // 128) + [FG % 128]
LAM_INIT = 0.2
HG = 4
CH = 32
NCMP = (T - 32) // 16 + 1
GU_SLOTS, GU_W = 8, F
DN_SLOTS, DN_W = 4, 2 * D
WG_SLOTS, WG_W = 3, KC * 512

def _block(matrix, what, *cols):
    return (matrix, what, list(cols) if cols else [(512 * what, 512)])


W_IN_COLS = dict(qn=0, kn=1, vn=2, qh=3, zf=4, zb=5, ih=6, gh=7)
EVEN_COLS = dict(aq=0, ak=1, av=2, az=3, bq=4, bk=5, bv=6, bz=7)
ODD_COLS = dict(cq=[(0, 512)], ck=[(512, 512)], cv=[(1024, 512)], cz=[(1536, 512)], dq=[(2048, 512)],
                kv=[(2560, 512)], kw=[(3072, 256), (3840, 24)], dz=[(3328, 512)])
GROUPS = [_block("w_mod", i) for i in range(4)]
for name, mods in (("zf", (4, 5)), ("zb", (6, 7)), ("qh", (8, 9)), ("ih", (10, 11)), ("qn", ()), ("kn", ()),
                   ("vn", ()), ("gh", ())):
    GROUPS.append(("w_in", name, [(512 * W_IN_COLS[name], 512)]))
    GROUPS += [_block("w_mod", i) for i in mods]
GROUPS += [_block("w_out", i) for i in range(2)]
GROUPS += [("w_in_e_2", n, [(512 * EVEN_COLS[n], 512)]) for n in ("aq", "ak", "av", "bq", "bk", "az", "bv", "bz")]
GROUPS += [_block("w_out_e_2", i) for i in range(2)]
for name in ("kv", "kw", "cq", "phi", "ck", "dq", "cv", "cz", "dz"):
    if name == "phi":
        GROUPS += [("phi_w1", s, []) for s in range(2)]
    else:
        GROUPS.append(("w_in_o_2", name, ODD_COLS[name]))
GROUPS += [_block("w_out_o_2", i) for i in range(2)]
GROUP_OF = {(m, w): n for n, (m, w, _) in enumerate(GROUPS)}


def constants():
    t = np.arange(T)
    p = np.arange(128)
    f32 = np.float32
    out = {"ident": np.eye(128, dtype=f32)}
    inv = (f32(10000.0) ** (-np.arange(0, 32, 2, dtype=f32) / f32(32))).astype(f32)
    ang = np.stack([(t // 64).astype(f32)[:, None] * inv, (t % 64).astype(f32)[:, None] * inv], 1)
    cos, sin = np.cos(ang).astype(f32), np.sin(ang).astype(f32)
    out["rope_cos"] = np.stack([cos, cos], 2).reshape(T, 64)
    out["rope_sin"] = np.stack([-sin, sin], 2).reshape(T, 64)
    qc, kc = np.arange(64)[:, None], np.arange(64)[None, :]
    w0 = np.clip(qc - 8, 0, 48)
    win = (kc >= w0) & (kc < w0 + 16)
    out["na_keep"] = np.tile(win.astype(f32), (2, 1))
    out["na_mask"] = np.tile(np.where(win, 0, NEG).astype(f32), (2, 1))
    dist = t[:, None] - t[None, :]
    causal = dist >= 0
    slopes = [2.0 ** -(h + 1) for h in range(8)]
    mult = causal * 1.0 + (causal & (dist % 4 == 0)) + (causal & (dist % 16 == 0))
    mult -= (dist > 128) * 1.0 * causal
    alibi = np.stack([np.where(causal, -s * dist, NEG) for s in slopes])
    dil = np.stack([np.where(mult > 0, -s * dist + np.log(np.maximum(mult, 1)), NEG) for s in slopes])

    def tiles(a):
        return np.concatenate([a[:, :128, :128], a[:, 128:, :]], 2).transpose(1, 0, 2).astype(f32)
    out["alibi"], out["dilated"] = tiles(alibi), tiles(dil)
    reset = np.ones((128, 2 * T), f32)
    reset[:, ::CH] = 0
    out["scan_reset"] = reset
    same = p[:, None] // CH == p[None, :] // CH
    fwd, bwd = same & (p[:, None] <= p[None, :]), same & (p[:, None] >= p[None, :])
    out["chunk_mask"] = np.stack([fwd, fwd, bwd, bwd], 1).astype(np.int32)
    out["slot_iota"] = np.tile(np.arange(1, CAP + 1, dtype=f32), (128, 1))
    out["ones"] = np.ones((128, 256), f32)
    cend = np.arange(16) * 16 + 31
    dc = t[:, None] - cend[None, :]
    ok = (dc >= 0) & (np.arange(16) < NCMP)[None, :]
    heads = np.array([[2 * hp + par for hp in range(4)] for par in range(2)])
    ca = np.where(ok[:, None, None, :], -np.array(slopes)[heads][None, :, :, None] * dc[:, None, None, :], NEG)
    out["cmp_bias"] = ca.reshape(2, 128, 128).transpose(1, 0, 2).astype(f32)
    out["cmp_keep"] = np.broadcast_to(ok[:, None, :], (T, 8, 16)).reshape(2, 128, 128).transpose(1, 0, 2).astype(f32)
    out["block_diag"] = ((2 * (p // 16 % 4) + p // 64)[:, None] == np.arange(8)[None, :]).astype(f32)
    sel = np.zeros((128, 128), f32)
    sel[::32] = 1
    out["sum_first"] = sel
    out["sum_groups"] = (p[:, None] % 32 == np.arange(16)[None, :]).astype(f32)
    return {k: np.ascontiguousarray(v) for k, v in out.items()}


def build(nc, A, out):
    ctx = ExitStack()

    def sb(name, shape, dt=FP32):
        return ctx.enter_context(nc.sbuf_tensor(name, shape, dt))

    sems = {}

    def S(name):
        if name not in sems:
            sems[name] = ctx.enter_context(nc.semaphore(name))
        return sems[name]

    y_dram = nc.dram_tensor("y_scratch", (E * CAP, D), FP32).ap()

    DIAG = 2 * 64 - 1
    diag = nc.dram_tensor("rpb_rows", (8, 7, 64, DIAG), FP32).ap()

    X = sb("X", [128, 2, D])
    HT = sb("HT", [128, KC * 512])
    WG = sb("WG", [128, WG_SLOTS, WG_W])
    TAB = sb("TAB", [128, 4096])
    BIG = sb("BIG", [128, GU_SLOTS * GU_W + DN_SLOTS * DN_W])
    GP2 = sb("GP2", [128, D])
    ident = sb("ident", [128, 128])
    cols = sb("cols", [128, 104])
    modc = sb("modc", [128, 48, 2])
    sc = sb("sc", [128, 768])
    BC = sb("BC", [128, 1152])
    PS = ctx.enter_context(nc.psum_tensor("PS", [128, 8, 512], FP32))

    def view(t, off, *dims):
        n = int(np.prod(dims))
        ap = t[:, off:off + n]
        if len(dims) == 2:
            ap = ap.rearrange("p (a b) -> p a b", b=dims[1])
        elif len(dims) == 3:
            ap = ap.rearrange("p (a b c) -> p a b c", b=dims[1], c=dims[2])
        elif len(dims) == 4:
            ap = ap.rearrange("p (a b c d) -> p a b c d", b=dims[1], c=dims[2], d=dims[3])
        return ap

    def laid(t, at=0):
        pos = [at]

        def place(*dims):
            n = int(np.prod(dims))
            pos[0] += n
            assert pos[0] <= t.shape[1], (pos[0], t.shape)
            return view(t, pos[0] - n, *dims)
        place.pos = pos
        return place

    s_at = laid(sc)
    stat = s_at(64)
    csil = s_at(8, 32)
    A1, A1c, A2 = s_at(8), s_at(8), s_at(8)
    lb, oml = s_at(4), s_at(4)
    lbt = s_at(12)
    negm, lsum, rls = s_at(8), s_at(96), s_at(96)
    lamt = s_at(8)
    aff = s_at(2, E)
    amax = s_at(2)
    best8 = s_at(8)
    eps = s_at(1)
    nst = s_at(4)

    bc_at = laid(BC)
    b_hg, b_qe, b_sub, b_qo, b_lam = bc_at(128), bc_at(4, 64), bc_at(128), bc_at(6, 64), bc_at(4, 64)

    at = laid(BIG)
    z = at(2, HG, 2 * T)
    qh = at(HG, T)
    vn = at(4, 512)
    EARLY = -(-at.pos[0] // GU_W)
    ih = at(4, 512)
    gh = at(2, 512)
    kn = at(4, 512)
    qn = at(2, 512)
    free1 = at.pos[0]
    dn_at = [laid(BIG, GU_SLOTS * GU_W + DN_W * i) for i in range(DN_SLOTS)]
    GP1, mixo0 = dn_at[0](D), dn_at[0](D)
    xn2 = dn_at[1](2, D)
    w_rt, ones, slot = dn_at[2](KC, E), dn_at[2](T), dn_at[2](CAP)
    rcos, rsin, na_keep, na_mask = dn_at[2](2, 64), dn_at[2](2, 64), dn_at[2](64), dn_at[2](64)
    lg = dn_at[2](2, E)
    affT, work, posm, pos = dn_at[2](T), dn_at[2](T), dn_at[2](T), dn_at[2](T)
    posT = dn_at[2](2, E)
    assert dn_at[2].pos[0] <= GU_SLOTS * GU_W + 3 * DN_W
    mixcat = dn_at[3](2, D)
    mixo = [mixo0, view(TAB, 0, D)]
    a0 = laid(BIG, 0)
    rows, xctx, xn = a0(128), a0(2, D), a0(4, D)
    mrow, sum_first = view(BIG, dn_at[3].pos[0] - 2 * D, 2, 512), view(BIG, dn_at[3].pos[0] - D, 128)
    bgate = view(BIG, dn_at[0].pos[0] - D, 4, 512)
    ah = laid(BIG, free1)
    fgt, bcum, kk = ah(2, 512), ah(2, 512), ah(2, 512)
    kend = fgt
    kendT, vbd = ah(2, 4, 128), ah(4, 4, 128)
    ah2 = laid(BIG, dn_at[3].pos[0] - 2 * D)
    qdec, kdec = [ah(2, T), ah2(2, T)], [ah(2, T), ah2(2, T)]
    eb, enb = qdec, kdec
    aT = [ah(4, 128), ah2(4, 128)]
    reset = ah(512)
    cmask = ah(4, 128)
    assert ah.pos[0] <= GU_SLOTS * GU_W
    ah = laid(BIG, dn_at[0].pos[0] - D)
    states = ah(2, 11, 128)
    decay = [ah(2, 16), ah(2, 16)]
    assert ah.pos[0] <= GU_SLOTS * GU_W + 2 * DN_W
    an = laid(BIG, 0)
    qr, kr, rt = an(2, 512), an(2, 512), an(512)
    pbuf, ptbuf = an(2, 512), an(2, 512)
    qrT, krT, qT, kcT = (view(HT, 1024 * i, 4, T) for i in range(4))
    mixT, h2T = view(BIG, (GU_SLOTS - 1) * GU_W, KC, T), view(HT, 2048, KC, T)
    am = laid(TAB, 2 * D)
    oh, ohg = am(2, E, CAP), am(2, E, CAP)

    def state_slot(n, h):
        return n % 2 if n < 7 else (2, 10)[h % 2] if n == 7 else n - 5
    xs = view(HT, 0, KC, 512)
    tm = laid(TAB)
    sgt, xse, sig, hid = tm(4, T), tm(KC, CAP), tm(FG), tm(FG)
    hidT, ysb = tm(6, 128), tm(256)
    GU = view(BIG, 0, GU_SLOTS, GU_W)
    EXT = WG_SLOTS * WG_W // GU_W
    GX = view(WG.rearrange("p a b -> p (a b)"), 0, EXT, GU_W)
    assert EXT == GU_SLOTS // 2 == KC // 2

    def early_place(e, i):
        quarter, j = i // EXT, i % EXT
        where = ((0, 1, "x", 0), ("x", 1, 0, 1))[e][quarter]
        value = ((16, 16, 16, 32), (32, 32, 48, 48))[e][quarter]
        free = ((-EXT, -EXT, -EXT, 1), (9, 5, 13, 21))[e][quarter] + j
        if where == "x":
            return GX[:, j, :], f"gu_ext{j}", value, free
        return GU[:, EXT * where + j, :], f"gu_in{EXT * where + j}", value, free
    DN = view(BIG, GU_SLOTS * GU_W, DN_SLOTS, 2, D)
    na_tab = view(TAB, 0, 8, 2, T)

    ae = laid(BIG)
    Y_GROUP = GROUP_OF["w_out", 1] + WG_SLOTS
    ybuf = view(WG[:, Y_GROUP % WG_SLOTS, :], 0, 4, D)
    moeo = view(BIG, 4 * D, 2, D)
    sg_last = view(BIG, 6 * D, 4, T)
    qk = ae(4, 2, 512)
    vv, zz = ae(2, 2, 512), ae(2, 2, 512)
    tT = ae(4, 4, T)
    mixe = ae(2, D)
    mixeT = ae(KC, T)
    pb2, pt2 = ae(2, 512), ae(2, 512)
    tab_a, tab_c = ae(8, 384), ae(8, 384)
    xn3 = ae(2, D)
    t2_off = ae.pos[0]
    ae(2048)
    hTe = view(HT, 0, KC, T)
    ckv = view(BIG, 3 * 1024, 2, 512)
    kw = view(TAB, 0, 2, 280)
    to = laid(TAB, 560)
    gates = to(2, 24)
    dup = to(2, 2, 256)
    pe2, peT = to(2, 128), to(2, 32)
    w2 = to(2, 64)
    hidk, hidv = to(2, 16), to(8, 16)
    kcmp, kcmpT = to(2, 128), to(2, 16)
    cbias, ckeep = to(2, 128), to(2, 128)
    bdiag = to(8)
    ocmp = view(TAB, 560 + 2500, 2, 512)
    assert to.pos[0] <= 3060
    tab_a_off = 4096 + 2048 + 2048 + 4096 + 2048 + 2048 + 1024 + 1024
    ab = view(BIG, tab_a_off - 2048, 2, 32, 32)
    hrow, sum_groups = view(BIG, tab_a_off, 2, 2, 128), view(BIG, tab_a_off + 512, 16)
    kcvT = view(BIG, tab_a_off + 1024, 2, T)
    vbd2 = view(BIG, tab_a_off + 1536, 8, 64)
    pc = view(BIG, tab_a_off + 2048, 2, 128)
    pcT = view(BIG, tab_a_off + 2304, 2, 128)
    dupT = view(BIG, tab_a_off + 2560, 2, 256)
    dupTw = view(HT, 2048, 2, 256)

    def bank(i):
        return PS[:, i, :]

    def o_bank(g):
        return bank(6 + g % 2 if g else 0)

    def half(h):
        return slice(64 * (h % 2), 64 * (h % 2) + 64)

    def na_units():
        r = []
        for qt in range(2):
            for h in range(8):
                q = slice(128 * qt, 128 * qt + 128)
                s = [(0, qrT[half(h), h // 2, q], krT[half(h), h // 2, :]),
                     (T, qT[half(h), h // 2, q], kcT[half(h), h // 2, :])]
                v = [vn[:, b, 64 * h:64 * h + 64] for b in range(4)]
                r.append(dict(s=s, tab=na_tab[:, h, qt, :], v=v, c=64 * h, w=64, n=512, last=h == 7))
        return r

    def causal_units(qT_, kT_, tabs, vals, heads, per, width):
        r = []
        for qt in range(2):
            for i, (qi, ki, ti, vi) in enumerate(heads):
                q = slice(128 * qt, 128 * qt + 128)
                n = 128 * (qt + 1)
                s = [(0, qT_[half(qi), qi // 2, q], kT_(qi, ki)[:, 0:n])]
                tab = tabs[:, ti, 0:128] if qt == 0 else tabs[:, ti, 128:384]
                v = [vals[:, b, width * vi:width * vi + width] for b in range(qt + 1)]
                r.append(dict(s=s, tab=tab, v=v, c=width * (i % per), w=width, n=n,
                              last=i % per == per - 1))
        return r

    aqT, akT, bqT, bkT = (tT[:, i] for i in range(4))
    cqT, ckT, dqT = aqT, akT, bqT
    av, bv = vv[:, 0], vv[:, 1]
    same_head = lambda t: (lambda qi, ki: t[half(ki), ki // 2, :])
    shared_head = lambda t: (lambda qi, ki: t[half(qi), ki, :])
    ATT = {
        "na": na_units(),
        "a": causal_units(aqT, same_head(akT), tab_a, av, [(h, h, h, h) for h in range(8)], 8, 64),
        "b": causal_units(bqT, same_head(bkT), tab_c, bv,
                          [(2 * h + c, 2 * h + c, 2 * h + 1, h) for h in range(4) for c in range(2)], 4, 128),
        "c": causal_units(cqT, same_head(ckT), tab_c, vv[:, 0], [(h, h, h, h) for h in range(8)], 8, 64),
        "s": causal_units(dqT, shared_head(dupT), tab_c, ckv[:, :, 384:512],
                          [(h, h // 4, h, h // 4) for h in range(8)], 8, 64),
        "w": causal_units(dqT, shared_head(dupTw), tab_c, kw[:, :, 128:256],
                          [(h, h // 4, h, h // 4) for h in range(8)], 8, 64),
    }
    n0 = g0 = 0
    for part in "csw":
        for u in ATT[part]:
            u["part"] = part
    ATT["odd"] = [u for qt in range(2) for part in "csw" for u in ATT[part][8 * qt:8 * qt + 8]]
    for k in ("na", "a", "b", "odd"):
        for u in ATT[k]:
            u["i"], u["g"] = n0, g0
            n0 += 1
            g0 += u["last"]
    PB = {"na": (pbuf, ptbuf)}

    PROJ = []

    def units(matrix, what, arrays, tiles, w=512, f=ACT.Copy, scale=1.0, kind="tok"):
        first = len(PROJ)
        for t in range(tiles):
            PROJ.append((GROUP_OF[matrix, what], kind, t, w, arrays[:, t, :], f, scale))
        return first, len(PROJ)
    units("w_in", "zf", z[:, 0], HG, 2 * T, ACT.Sigmoid, kind="chan")
    units("w_in", "zb", z[:, 1], HG, 2 * T, ACT.Sigmoid, kind="chan")
    units("w_in", "qh", qh, HG, T, kind="chan")
    P_IH = units("w_in", "ih", ih, 4)[1]
    units("w_in", "qn", qn, 2, scale=0.125)
    P_KN = units("w_in", "kn", kn, 4)[1]
    units("w_in", "vn", vn, 4)
    P_IN = (0, units("w_in", "gh", gh, 2, f=ACT.Sigmoid)[1])

    def outs(matrix, dst):
        a = len(PROJ)
        for t in range(2):
            for g in range(2):
                PROJ.append((GROUP_OF[matrix, g], "tok", t, 512, dst[t][:, 512 * g:512 * g + 512], ACT.Copy, 1.0))
        return a, len(PROJ)
    P_OUT = outs("w_out", mixo)
    P_E = {}
    for name, dst, f in (("aq", qk[:, 0], ACT.Copy), ("ak", qk[:, 1], ACT.Copy), ("av", vv[:, 0], ACT.Copy),
                         ("bq", qk[:, 2], ACT.Copy), ("bk", qk[:, 3], ACT.Copy), ("az", zz[:, 0], ACT.Silu),
                         ("bv", vv[:, 1], ACT.Copy), ("bz", zz[:, 1], ACT.Silu)):
        P_E[name] = units("w_in_e_2", name, dst, 2, f=f)
    P_OUT_E = outs("w_out_e_2", [X[:, t, :] for t in range(2)])
    P_O = {}
    for name, dst, f in (("kv", ckv, ACT.Copy), ("kw", kw, ACT.Copy), ("cq", qk[:, 0], ACT.Copy),
                         ("ck", qk[:, 1], ACT.Copy), ("dq", qk[:, 2], ACT.Copy), ("cv", vv[:, 0], ACT.Copy),
                         ("cz", zz[:, 0], ACT.Silu), ("dz", zz[:, 1], ACT.Silu)):
        P_O[name] = units("w_in_o_2", name, dst, 2, 280 if name == "kw" else 512, f=f)
    P_OUT_O = outs("w_out_o_2", [X[:, t, :] for t in range(2)])

    FILLS = []

    def fill(parts, dst, rows_=128, affine=None):
        FILLS.append((parts, dst, rows_, affine))

    def tok_fills(name, src, dst, gain=None, shift=None):
        for t in range(2):
            begin(f"{name}{t}")
            for j in range(2):
                fill([(src[:, t, 128 * k:128 * k + 128], 128 * (k % 4)) for k in range(4 * j, 4 * j + 4)],
                     dst[:, 4 * j:4 * j + 4, 128 * t:128 * t + 128],
                     affine=None if gain is None else
                     [(gain[:, k:k + 1], 0.0 if shift is None else shift[:, k:k + 1]) for k in range(4 * j, 4 * j + 4)])
            end(f"{name}{t}")

    def head_fills(src, dst):
        for j in range(2):
            fill([(src[:, t, 128 * k:128 * k + 128], 256 * (k % 2) + 128 * t)
                  for k in (2 * j, 2 * j + 1) for t in range(2)], dst[:, 2 * j:2 * j + 2, :])
    marks = {}

    def begin(name):
        marks[name] = [len(FILLS), None]

    def end(name):
        marks[name][1] = len(FILLS)
    for h in range(HG):
        begin(f"kend{h}")
        for d in range(2):
            fill([(kend[:, d, 128 * t:128 * t + 128], 128 * t) for t in range(4)], kendT[:, d])
        end(f"kend{h}")
    begin("na")
    for src, dst in ((qr, qrT), (kr, krT), (qn, qT), (kn[:, 2:4], kcT)):
        head_fills(src, dst)
    end("na")
    tok_fills("mix", mixcat, mixT)
    tok_fills("h2", xn2, h2T, A2, modc[:, 24:32, 0])
    begin("aff"), fill([(aff[:, t, :], 128 * t) for t in range(2)], affT[0:E, :], E), end("aff")
    begin("pos"), fill([(posm[0:E, 128 * t:128 * t + 128], E * t) for t in range(2)], posT), end("pos")
    begin("sg")
    for j in range(2):
        fill([(ohg[:, t, 4 * b:4 * b + 4, :].rearrange("p a b -> p (a b)"), 256 * (b % 2) + 128 * t) for b in (2 * j, 2 * j + 1) for t in range(2)],
             sgt[:, 2 * j:2 * j + 2, :])
    end("sg")
    tok_fills("he", xn3, hTe, cols[:, 16:24])
    for i, name in enumerate(("aq", "ak", "bq", "bk")):
        begin(name), head_fills(qk[:, i], tT[:, i]), end(name)
    tok_fills("mixe", mixe, mixeT)
    tok_fills("ho", xn3, hTe, cols[:, 24:32])
    begin("cmp")
    fill([(ckv[:, t, 128 * s:128 * s + 128], 256 * s + 128 * t) for s in range(2) for t in range(2)], kcvT)
    fill([(pe2[0:32, s], 32 * s) for s in range(2)], peT)
    end("cmp")
    begin("cq"), head_fills(qk[:, 0], tT[:, 0]), end("cq")
    begin("ck"), head_fills(qk[:, 1], tT[:, 1]), end("ck")
    begin("kcmp"), fill([(kcmp[0:16, h], 16 * h) for h in range(2)], kcmpT), end("kcmp")
    begin("dq"), head_fills(qk[:, 2], tT[:, 2]), end("dq")
    begin("dup")
    for i, dst in ((0, dupT), (1, dupTw)):
        fill([(dup[:, i, t, 128 * k:128 * k + 128], 256 * k + 128 * t) for k in range(2) for t in range(2)], dst)
    end("dup")
    begin("pc"), fill([(pc[:, t, :], 128 * t) for t in range(2)], pcT), end("pc")
    tok_fills("mixo", mixe, mixeT)

    need, landed = [], [0] * WG_SLOTS
    for n, (_, _, what) in enumerate(GROUPS):
        landed[n % WG_SLOTS] += 16 * (len(what) or 2)
        need.append(landed[n % WG_SLOTS])
    last_unit = {}
    for n, u in enumerate(PROJ):
        last_unit[u[0]] = n
    used_by = [("mod_ready", w + 1) if m == "w_mod" else ("phi_psum", w + 1) if m == "phi_w1"
               else ("proj_ready", last_unit[g] + 1) for g, (m, w, _) in enumerate(GROUPS)]
    DBLK, dsum = [], [0] * DN_SLOTS
    for q in range(12):
        j, part = q // 3, q % 3
        dsum[q % DN_SLOTS] += 32 if part == 2 else 16
        DBLK.append((j, [2 * part, 2 * part + 1], q % DN_SLOTS, dsum[q % DN_SLOTS]))
    assert len(set(dsum)) == 1
    DSUM = dsum[0]

    MOD_AT = {2: 1, 3: 2, 4: 3, 5: 4, 6: 1, 7: 2, 8: 5, 9: 6, 10: 7, 11: 8}

    def stepper(eng, chain):
        count = {}

        def step(ins, signal=chain):
            count[signal] = count.get(signal, 0) + 1
            ins.then_inc(S(signal), 1)
            eng.wait_ge(S(signal), count[signal])
        return step

    block = ctx.enter_context(nc.Block())

    @block.sync
    def _(sp):
        sp.dma_start(rows[0:8, :], A["g_pre1"][0].rearrange("(a b) -> a b", b=128)).then_inc(S("rows_in"), 16)
        sp.dma_start(rows[8:16, :], A["g_pre2"][0].rearrange("(a b) -> a b", b=128)).then_inc(S("rows_in"), 16)
        sp.dma_start(rows[16:24, :], A["ln_e_2"][0].rearrange("(a b) -> a b", b=128)).then_inc(S("rows_in"), 16)
        sp.dma_start(rows[24:32, :], A["ln_o_2"][0].rearrange("(a b) -> a b", b=128)).then_inc(S("rows_in"), 16)
        sp.dma_start(rows[32:40, :], A["hg_lb_logits"].rearrange("l (a b) -> (l a) b", b=128)).then_inc(S("rows_in"), 16)
        sp.dma_start(rows[40:48, :], A["c"][0].rearrange("(a b) -> a b", b=128)).then_inc(S("rows_in"), 16)
        sp.dma_start(rows[48:56, :], A["c_ctx"].rearrange("(a b) -> a b", b=128)).then_inc(S("rows_in"), 16)
        sp.dma_start(rows[56:104, :], A["b_mod"][0].rearrange("(a b) -> a b", b=128)).then_inc(S("rows_in"), 16)
        sp.dma_start(ident[:, :], A["ident"]).then_inc(S("rows_in"), 16)
        sp.dma_start(X[:, :, :], A["x"][0].rearrange("(t p) d -> p t d", p=128)).then_inc(S("x_in"), 16)
        sp.dma_start(xctx, A["ctx"][0].rearrange("(t p) d -> p t d", p=128)).then_inc(S("x_in"), 16)
        for i in range(2):
            sp.dma_start(view(bgate[0:1].rearrange("p a b -> p (a b)"), D * i, D), A["b_mod"][:, (2 + 3 * i) * D:(3 + 3 * i) * D]
                         ).then_inc(S("mod_in"), 16)

        def load_group(n):
            name, what, ranges = GROUPS[n]
            slot_ = n % WG_SLOTS
            if n >= WG_SLOTS:
                sp.wait_ge(S(used_by[n - WG_SLOTS][0]), used_by[n - WG_SLOTS][1])
            if name == "phi_w1":
                for hf in range(2):
                    sp.dma_start(WG[64 * hf:64 * hf + 64, slot_, :], A[name][what]).then_inc(S(f"wg_in{slot_}"), 16)
                return
            width = sum(w for _, w in ranges)
            dst = view(WG[:, slot_, :], 0, KC, width)
            o = 0
            for c0, w in ranges:
                sp.dma_start(dst[:, :, o:o + w],
                             A[name][0].rearrange("(k p) c -> p k c", p=128)[:, :, c0:c0 + w]
                             ).then_inc(S(f"wg_in{slot_}"), 16)
                o += w
        for n in range(GROUP_OF["w_out", 1] + 1):
            load_group(n)
        gate_d, up_d, down_d = (A[n][0] for n in ("w_gate", "w_up", "w_down"))

        def chunk(e, i):
            return (gate_d if i % 2 == 0 else up_d)[e, 128 * (i // 2):128 * (i // 2) + 128, :]

        def load_early(e, i):
            dst, signal, _, free = early_place(e, i)
            if free > 0:
                sp.wait_ge(S("gu_used"), free)
            sp.dma_start(dst, chunk(e, i)).then_inc(S(signal), 16)

        def load_block(e, i):
            j, (s0, s1), slot_, _ = DBLK[i]
            r0 = FG * j + 128 * s0
            if FS[s1] == 128:
                sp.dma_start(DN[:, slot_, :, :], down_d[e, r0:r0 + 256, :].rearrange("(s p) d -> p s d", p=128)
                             ).then_inc(S(f"dn_in{slot_}"), 16)
            else:
                sp.dma_start(DN[:, slot_, 0, :], down_d[e, r0:r0 + 128, :]).then_inc(S(f"dn_in{slot_}"), 16)
                sp.dma_start(DN[0:FS[s1], slot_, 1, :], down_d[e, r0 + 128:r0 + 128 + FS[s1], :]
                             ).then_inc(S(f"dn_in{slot_}"), 16)

        y_v = y_dram.rearrange("(b p) d -> p b d", p=128)

        def load_expert(e, first=False, second=False, last=False):
            if first:
                for i in range(3 * EXT, 4 * EXT):
                    load_early(0, i)
            elif second:
                for i in range(2 * EXT, 4 * EXT):
                    load_early(1, i)
            else:
                for i in range(2 * KC):
                    sp.wait_ge(S("gu_used"), 2 * KC * e + (i - GU_SLOTS + 1))
                    sp.dma_start(GU[:, i % GU_SLOTS, :], chunk(e, i)).then_inc(S(f"gu_in{i % GU_SLOTS}"), 16)
            if first:
                sp.wait_ge(S("xs_done"), 2 * KC)
                sp.wait_ge(S("ohg_ready"), 2)
                load_block(0, 1)
                load_block(0, 2)
                for i in (*range(EXT, 2 * EXT), *range(EXT)):
                    load_early(1, i)
            if last:
                sp.wait_ge(S("y_stored"), 16 * (E - 4))
                sp.dma_start(ybuf[:, 0:3, :], y_v[:, 0:3, :]).then_inc(S("y_back"), 16)
                sp.wait_ge(S("y_stored"), 16 * (E - 1))
                sp.dma_start(ybuf[0:3 * CAP, 3, :], y_v[0:3 * CAP, 3, :]).then_inc(S("y_last"), 16)
            for i in range(DN_SLOTS if first else 0, len(DBLK)):
                sp.wait_ge(S("dn_used"), 12 * e + (i - DN_SLOTS + 1))
                load_block(e, i)
        sp.wait_ge(S("tr_copied"), marks["na"][1])
        sp.wait_ge(S("gh_used"), 2)
        for i in range(EARLY, GU_SLOTS - 1):
            load_early(0, i)
        sp.wait_ge(S("mixcat_ready"), 2)
        for i in range(EARLY):
            load_early(0, i)
        sp.wait_ge(S("tr_copied"), marks["mix1"][1])
        load_block(0, 3)
        sp.wait_ge(S("proj_ready"), P_OUT[1])
        for i in range(GU_SLOTS - 1, GU_SLOTS + EXT):
            load_early(0, i)
        sp.wait_ge(S("xn2_ready"), 2)
        load_block(0, 0)
        load_expert(0, first=True)
        load_expert(1, second=True)
        with sp.Fori(2, E - 1) as e:
            load_expert(e)
        load_expert(E - 1, last=True)
        for n in range(GROUP_OF["w_out", 1] + 1, len(GROUPS)):
            if n == GROUP_OF["w_out", 1] + 1:
                sp.wait_ge(S("y_last"), 16)
            if n == Y_GROUP:
                sp.wait_ge(S("moe_psum"), 4)
            load_group(n)
        for t in range(2):
            sp.wait_ge(S("x_final"), t + 1)
            sp.dma_start(out[0, 128 * t:128 * t + 128, :], X[:, t, :]).then_inc(S("out_done"), 16)
        sp.wait_ge(S("out_done"), 32)

    @block.gpsimd
    def _(pool):
        pool.dma_start(sum_first, A["sum_first"]).then_inc(S("gate_in"), 16)
        nc.gpsimd.memset(csil, 0.0).then_inc(S("csil_zero"), 1)
        pool.wait_ge(S("mod_ready"), 4)
        pool.dma_start(GP1, A["g_post1"][0].partition_broadcast(128)).then_inc(S("gain_in"), 16)
        pool.dma_start(GP2[:, :], A["g_post2"][0].partition_broadcast(128)).then_inc(S("gain_in"), 16)
        pool.dma_start(reset, A["scan_reset"]).then_inc(S("hg_in"), 16)
        pool.dma_start(cmask.bitcast(I32), A["chunk_mask"]).then_inc(S("hg_in"), 16)
        pool.dma_start(b_hg, A["hg_norm"][0].partition_broadcast(128)).then_inc(S("hg_in"), 16)
        pool.dma_start(na_keep, A["na_keep"]).then_inc(S("na_in"), 16)
        pool.dma_start(na_mask, A["na_mask"]).then_inc(S("na_in"), 16)
        for a, n in ((rcos, "rope_cos"), (rsin, "rope_sin")):
            pool.dma_start(a, A[n].rearrange("(t p) c -> p t c", p=128)).then_inc(S("na_in"), 16)
        pool.dma_start(w_rt, A["w_router"][0].rearrange("(k p) e -> p k e", p=128)).then_inc(S("rt_in"), 16)
        pool.dma_start(ones, A["ones"]).then_inc(S("rt_in"), 16)
        pool.dma_start(slot, A["slot_iota"]).then_inc(S("rt_in"), 16)
        rpb = A["na_rpb"]
        RH, RW = rpb.shape[2], rpb.shape[3]
        for h in range(8):
            src = bass.AP(tensor=rpb.tensor, offset=rpb.offset + h * RH * RW + 4 * RW + 15 - 63,
                          ap=[[0, 64], [RW, 7], [1, DIAG]])
            pool.dma_start(diag[h].rearrange("r q c -> q r c"), src).then_inc(S("diag_out"), 16)
        pool.wait_ge(S("diag_out"), 8 * 16)
        for r in range(4):
            for h in range(8):
                src = bass.AP(tensor=diag.tensor, offset=diag.offset + (h * 7 + 3 - r) * 64 * DIAG + 63,
                              ap=[[DIAG - 1, 64], [64 * DIAG, 4], [1, 64]])
                dst = na_tab[64 * (r % 2):64 * (r % 2) + 64, h, r // 2, :].rearrange("p (a b) -> p a b", b=64)
                pool.dma_start(dst, src).then_inc(S("rpb_in"), 16)
        pool.wait_ge(S("na_in"), 64)
        pool.wait_ge(S("rpb_in"), 32 * 16)
        tab = view(TAB, 0, 64, 64)
        bro = lambda a: a.unsqueeze(1).to_broadcast([128, 64, 64])
        nc.gpsimd.tensor_tensor(tab, tab, bro(na_keep), ALU.mult).then_inc(S("na_tab"), 1)
        pool.wait_ge(S("na_tab"), 1)
        nc.gpsimd.tensor_tensor(tab, tab, bro(na_mask), ALU.add).then_inc(S("na_tab"), 1)
        pool.wait_ge(S("gp_done"), 4)
        nc.gpsimd.memset(vbd, 0.0).then_inc(S("vbd_zero"), 1)
        for a in aT:
            nc.gpsimd.memset(a, 0.0).then_inc(S("vbd_zero"), 1)
        pool.wait_ge(S("vbd_zero"), 3)
        pool.wait_ge(S("proj_evac"), P_IH)
        for h in range(HG):
            if h:
                pool.wait_ge(S("kv_ready"), 9 * h)
            for c in range(4):
                nc.gpsimd.tensor_copy(vbd[32 * c:32 * c + 32, :, c, :],
                                      ih[32 * c:32 * c + 32, :, 128 * h:128 * h + 128]).then_inc(S("vbd_ready"), 1)
        pool.wait_ge(S("gu_used"), 2 * KC * E)
        nc.gpsimd.memset(sg_last, 0.0).then_inc(S("sg_zero"), 1)
        pool.wait_ge(S("sg_zero"), 1)
        for g in range(4):
            pool.dma_start(sg_last[32 * g:32 * g + 32, g, :], sgt[3 * CAP:4 * CAP, 3, :]).then_inc(S("sg_last_in"), 16)
        pool.wait_ge(S("y_stored"), 16 * E)
        pool.wait_ge(S("x_moe"), 2)
        pool.dma_start(tab_a, A["dilated"]).then_inc(S("even_in"), 16)
        pool.dma_start(tab_c, A["alibi"]).then_inc(S("even_in"), 16)
        pool.dma_start(b_qe, A["qkn_e_2"][0].partition_broadcast(128)).then_inc(S("even_in"), 16)
        pool.dma_start(b_sub, A["subln_e_2"][0].partition_broadcast(128)).then_inc(S("even_in"), 16)
        pool.dma_start(b_lam, A["lam_e_2"][0].partition_broadcast(128)).then_inc(S("even_in"), 16)
        pool.dma_start(b_qo, A["qkn_o_2"][0].partition_broadcast(128)).then_inc(S("even_in"), 16)
        for s in range(2):
            for dd in range(2):
                pool.dma_start(pe2[0:32, s, 64 * dd:64 * dd + 64], A["phi_pe_2"][0, s]).then_inc(S("odd_in"), 16)
        pool.dma_start(w2, A["phi_w2_2"][0].rearrange("s p c -> p s c")).then_inc(S("odd_in"), 16)
        pool.dma_start(cbias, A["cmp_bias"]).then_inc(S("odd_in"), 16)
        pool.dma_start(ckeep, A["cmp_keep"]).then_inc(S("odd_in"), 16)
        pool.dma_start(bdiag, A["block_diag"]).then_inc(S("odd_in"), 16)
        pool.wait_ge(S("mixe_ready"), 2)
        pool.dma_start(sum_groups, A["sum_groups"]).then_inc(S("cmp_in"), 16)
        nc.gpsimd.memset(ab, 0.0).then_inc(S("ab_zero"), 1)

    @block.tensor
    def _(pe):
        mm = nc.tensor.matmul

        def do_fills(name):
            for i in range(*marks[name]):
                parts, *_ = FILLS[i]
                if i >= 2:
                    pe.wait_ge(S("tr_copied"), i - 1)
                for src, c in parts:
                    k, m = src.shape
                    last = nc.tensor.transpose(PS[0:m, 4 + i % 2, c:c + k], src, ident[0:k, 0:k])
                last.then_inc(S("tr_ready"), 1)

        def project(units_, lhs):
            for n in range(*units_):
                g, kind, j, w, *_ = PROJ[n]
                if PROJ[n - 1][0] != g:
                    pe.wait_ge(S(f"wg_in{g % WG_SLOTS}"), need[g])
                if n >= 2:
                    pe.wait_ge(S("proj_evac"), n - 1)
                width = sum(x for _, x in GROUPS[g][2])
                wt = view(WG[:, g % WG_SLOTS, :], 0, KC, width)
                for k in range(KC):
                    if n == 0:
                        pe.wait_ge(S("hT_done"), 2 * (k + 1))
                    if kind == "chan":
                        last = mm(bank(n % 2)[:, 0:w], wt[:, k, 128 * j:128 * j + 128], lhs[:, k, 0:w],
                                  start=k == 0, stop=k == KC - 1)
                    else:
                        last = mm(bank(n % 2)[:, 0:w], lhs[:, k, 128 * j:128 * j + 128], wt[:, k, 0:w],
                                  start=k == 0, stop=k == KC - 1)
                last.then_inc(S("proj_ready"), 1)
        
        def attention(name, between=None, beside=None):
            us = ATT[name]
            pb, pt = PB.get(name, (pb2, pt2))
            window = name == "na"

            def scores(u):
                i = u["i"]
                if i >= 2:
                    pe.wait_ge(S("exp_done" if window else "max_ready"), i - 1)
                o = bank(2 + i % 2)
                if window:
                    mm(o[:, 0:T], ident[:, :], u["tab"], start=True, stop=False)
                for c, q, k in u["s"]:
                    last = mm(o[:, c:c + k.shape[1]], q, k, start=c > 0 or not window, stop=True)
                last.then_inc(S("s_ready"), 1)

            def turn(u):
                i = u["i"]
                pe.wait_ge(S("exp_done"), i + 1)
                if i >= 2:
                    pe.wait_ge(S("pt_copied"), i - 1)
                for b in range(u["n"] // 128):
                    last = nc.tensor.transpose(bank(4 + i % 2)[:, 128 * b:128 * b + 128],
                                               pb[:, i % 2, 128 * b:128 * b + 128], ident[:, :])
                last.then_inc(S("pT_done"), 1)

            def values(u):
                i, g = u["i"], u["g"]
                pe.wait_ge(S("pt_copied"), i + 1)
                if g == 1:
                    pe.wait_ge(S("hg_read"), 2)
                if g >= 2:
                    pe.wait_ge(S("o_read"), g - 1)
                nb = u["n"] // 128
                for b in range(nb):
                    last = mm(o_bank(g)[:, u["c"]:u["c"] + u["w"]], pt[:, i % 2, 128 * b:128 * b + 128],
                              u["v"][b], start=b == 0, stop=b == nb - 1)
                last.then_inc(S("pv_done"), 1)
            for k in range(len(us) + 2):
                if k < len(us):
                    scores(us[k])
                if between and k % 2 == 0 and between[0] + k // 2 < between[1]:
                    project((between[0] + k // 2, between[0] + k // 2 + 1), between[2])
                if beside:
                    beside(k)
                if 1 <= k <= len(us):
                    turn(us[k - 1])
                if k >= 2:
                    values(us[k - 2])

        def project_mix(name, ready, us, k0, units_, lhs, later=False):
            def beside(k):
                if k == k0:
                    pe.wait_ge(S(ready), 1)
                    pe.wait_ge(S("pt_copied"), us[k - 2]["i"] + 1)
                    do_fills(f"{name}0")
                    pe.wait_ge(S("tr_copied"), marks[f"{name}0"][1])
                if k == k0 + 1 or k == k0 + 3 and not later:
                    n = units_[0] + (k - k0) // 2
                    project((n, n + 1), lhs)
            return beside

        def project_mix_rest(name, ready, last, units_, lhs, later=False):
            if later:
                project((units_[0] + 1, units_[0] + 2), lhs)
            pe.wait_ge(S(ready), 2)
            pe.wait_ge(S("pt_copied"), last["i"] + 1)
            do_fills(f"{name}1")
            pe.wait_ge(S("tr_copied"), marks[f"{name}1"][1])
            project((units_[0] + 2, units_[1]), lhs)

        pe.wait_ge(S("rows_in"), 9 * 16)
        nc.tensor.transpose(PS[:, 7, 0:104], rows[0:104, :], ident[0:104, 0:104]).then_inc(S("rowsT"), 1)

        def modulation(pair):
            for g in pair:
                n = GROUP_OF["w_mod", g]
                pe.wait_ge(S(f"wg_in{n % WG_SLOTS}"), need[n])
                if g >= 2:
                    pe.wait_ge(S("mod_evac"), g - 1)
                wt = view(WG[:, n % WG_SLOTS, :], 0, KC, 512)
                for k in (0, 2, 4, 6, 1, 3, 5, 7):
                    last = mm(PS[32 * (k // 2):32 * (k // 2) + 32, 6 + g % 2, :], csil[:, k, :], wt[:, k, :],
                              start=k % 2 == 0, stop=k % 2 == 1)
                last.then_inc(S("mod_ready"), 1)
            for g in pair:
                pe.wait_ge(S("mod_evac"), g + 1)
                if g >= 2:
                    pe.wait_ge(S("gp_done" if g in (6, 7) else "modc_done"), MOD_AT[g])
                if g % 6 in (4, 5):
                    i = (4, 5, 10, 11).index(g)
                    mm(bank(4 + g % 2), sum_first, mrow[:, g % 2, :], start=True, stop=False)
                    last = mm(bank(4 + g % 2), sum_first[0:1, :], bgate[0:1, i, :], start=False, stop=True)
                else:
                    for j in range(4):
                        last = nc.tensor.transpose(bank(4 + g % 2)[:, 128 * j:128 * j + 128],
                                                   mrow[:, g % 2, 128 * j:128 * j + 128], ident[:, :])
                last.then_inc(S("modT"), 1)
        pe.wait_ge(S("csil_ready"), 1)
        pe.wait_ge(S("gate_in"), 16)
        pe.wait_ge(S("mod_in"), 32)
        modulation((0, 1))
        pe.wait_ge(S("xn_ready"), 4)
        for k in range(KC):
            if k >= 2:
                pe.wait_ge(S("hT_copied"), k - 1)
            for t in range(4):
                last = nc.tensor.transpose(bank(2 + k % 2)[:, 128 * t:128 * t + 128],
                                           xn[:, t, 128 * k:128 * k + 128], ident[:, :])
            last.then_inc(S("hT_ready"), 1)
        modulation((2, 3))
        hT = view(HT, 0, KC, 512)
        project((0, 4), hT)
        modulation((4, 5))
        project((4, 8), hT)
        modulation((6, 7))
        project((8, 12), hT)
        modulation((8, 9))
        project((12, P_IH), hT)
        modulation((10, 11))
        rest = iter(range(P_IH, P_IN[1]))

        def project_next():
            n = next(rest)
            project((n, n + 1), hT)
        def sums(h, t):
            o = PS[:, 6 + t, 128 * h:128 * h + 128]
            if t == 0:
                pe.wait_ge(S("states_ready"), h + 1)
            for d in range(2):
                mm(o, aT[h % 2][:, 2 * d + t, :], ih[:, t, 128 * h:128 * h + 128], start=d == 0, stop=False)
            for d in range(2):
                for c in range(4):
                    n = 4 * t + c
                    s = state_slot(7 + n if d == 0 else 14 - n, h)
                    last = mm(o[32 * c:32 * c + 32, :], qdec[h % 2][:, d, 32 * n:32 * n + 32], states[:, d, s, :],
                              start=False, stop=d == 1)
            if t == 1:
                last.then_inc(S("hg_o"), 1)

        for h in range(HG):
            pe.wait_ge(S("hg_dec"), h + 1)
            if h == 0:
                pe.wait_ge(S("gp_done"), 4)
            do_fills(f"kend{h}")
            def ring_bank(i):
                if 9 * h + i >= 2:
                    pe.wait_ge(S("kv_used"), 9 * h + i - 1)
                return bank(2 + (9 * h + i) % 2)

            def updates(*js):
                for j in js:
                    d = j % 2
                    t = ((2, 3, 0, 1), (3, 2, 1, 0))[d][j // 2]
                    mm(ring_bank(1 + j), kendT[:, d, t, :], vbd[:, t, :, :].rearrange("p a b -> p (a b)"),
                       start=True, stop=True).then_inc(S("kv_ready"), 1)
            o = ring_bank(0)
            for d in range(2):
                for t in range(2):
                    a = 2 * d + t
                    last = mm(o[:, 128 * a:128 * a + 128], kdec[h % 2][:, d, 128 * t:128 * t + 128],
                              qdec[h % 2][:, d, 128 * t:128 * t + 128], start=True, stop=True)
            last.then_inc(S("kv_ready"), 1)
            project_next()
            pe.wait_ge(S("tr_copied"), marks[f"kend{h}"][1])
            pe.wait_ge(S("vbd_ready"), 4 * (h + 1))
            updates(0, 1)
            if h == 1:
                pe.wait_ge(S("mod_evac"), 12)
            if h:
                sums(h - 1, 0)
            updates(2, 3)
            if h:
                sums(h - 1, 1)
            updates(4, 5)
            project_next()
            updates(6, 7)
            project_next()
        pe.wait_ge(S("rope_ready"), 1)
        do_fills("na")
        sums(HG - 1, 0)
        sums(HG - 1, 1)
        pe.wait_ge(S("tr_copied"), marks["na"][1])
        pe.wait_ge(S("proj_evac"), P_IN[1])
        pe.wait_ge(S("na_tab"), 2)
        attention("na", beside=project_mix("mix", "mixcat_ready", ATT["na"], 11, P_OUT, mixT))
        project_mix_rest("mix", "mixcat_ready", ATT["na"][-1], P_OUT, mixT)
        pe.wait_ge(S("rt_in"), 48)
        for t in range(2):
            pe.wait_ge(S("xn2_ready"), t + 1)
            do_fills(f"h2{t}")
            pe.wait_ge(S("tr_copied"), marks[f"h2{t}"][1])
            for k in range(KC):
                last = mm(PS[:, 6, E * t:E * t + E], h2T[:, k, 128 * t:128 * t + 128], w_rt[:, k, :],
                          start=k == 0, stop=k == KC - 1)
        last.then_inc(S("lg_ready"), 1)
        pe.wait_ge(S("aff_ready"), 1)
        do_fills("aff")
        pe.wait_ge(S("pos_ready"), 1)
        do_fills("pos")
        pe.wait_ge(S("oh_ready"), 2)

        def gather(k, o, c0, c1):
            for t in range(2):
                last = mm(o, xn2[:, t, 128 * k:128 * k + 128], oh[:, t].rearrange("p a b -> p (a b)")[:, c0:c1],
                          start=t == 0, stop=t == 1)
            last.then_inc(S("xs_psum"), 1)
        for k in range(KC):
            gather(k, PS[:, 6 + k // 4, 128 * (k % 4):128 * (k % 4) + 128], 0, 128)

        def scatter(b, t, hf):
            n = 3 * CAP if b == 3 else 4 * CAP
            mm(bank(2 * t + hf), sgt[0:n, b, 128 * t:128 * t + 128], ybuf[0:n, b, 512 * hf:512 * hf + 512],
               start=b == 0, stop=False)

        def expert(e, first=False, second=False, last_=False):
            pe.wait_ge(S("xse_ready"), e + 1)
            if not first:
                pe.wait_ge(S("hid_ready"), e)
            for i in range(2 * KC):
                k, up, slot_ = i // 2, i % 2, i % GU_SLOTS
                if first or second:
                    w_, signal, value, _ = early_place(int(second), i)
                    pe.wait_ge(S(signal), value)
                else:
                    w_ = GU[:, slot_, :]
                    pe.wait_ge(S(f"gu_in{slot_}"), 32 * e + 16 * (i // GU_SLOTS))
                for hf in range(2):
                    for g in range(4):
                        c0 = FG * g + FH * hf
                        last = mm(PS[32 * g:32 * g + 32, 2 * up + hf, 0:FH], xse[:, k, :],
                                  w_[:, c0:c0 + FH], start=k == 0, stop=k == KC - 1)
                last.then_inc(S("gu_used"), 1)
                if first and 1 <= i <= KC:
                    pe.wait_ge(S("xs_done"), KC + i - 2 if i > 2 else KC)
                    gather(i - 1, bank(6 + i % 2)[:, 0:512 - 128], 128, 512)
                if first and i == KC + 1:
                    pe.wait_ge(S("ohg_ready"), 2)
                    do_fills("sg")
            if first:
                pe.wait_ge(S("tr_copied"), marks["sg"][1])
            pe.wait_ge(S("hid_ready"), e + 1)
            if not first:
                pe.wait_ge(S("hidT_copied"), 3 * e)
            for s, n in enumerate(FS):
                last = nc.tensor.transpose(PS[0:n, 4 + s // 4, 128 * (s % 4):128 * (s % 4) + 128],
                                           hid[:, 128 * s:128 * s + n], ident[:, :])
            last.then_inc(S("hidT_done"), 1)
            pe.wait_ge(S("hidT_copied"), 3 * e + 3)
            if not first:
                pe.wait_ge(S("y_copied"), e)
            for i, (j, ss, slot_, v) in enumerate(DBLK):
                pe.wait_ge(S(f"dn_in{slot_}"), DSUM * e + v)
                for s in ss:
                    for g in range(4):
                        last = mm(PS[32 * g:32 * g + 32, 6, 0:256], hidT[0:FS[s], s, 32 * j:32 * j + 32],
                                  DN[0:FS[s], slot_, s % 2, 256 * g:256 * g + 256],
                                  start=i == 0 and s == 0, stop=i == 11 and s == ss[-1])
                last.then_inc(S("dn_used"), 1)
                if last_:
                    if i == 0:
                        pe.wait_ge(S("y_back"), 16)
                    scatter(i // 4, i // 2 % 2, i % 2)
                    if i == 4:
                        pe.wait_ge(S("y_last"), 16)
                    if 4 <= i < 8:
                        scatter(3, i // 2 % 2, i % 2)
        expert(0, first=True)
        expert(1, second=True)
        with pe.Fori(2, E - 1) as e:
            expert(e)
        expert(E - 1, last_=True)
        pe.wait_ge(S("sg_last_in"), 64)
        pe.wait_ge(S("y_copied"), E)
        for t in range(2):
            for g in range(4):
                last = mm(PS[:, 2 * t + g // 2, 256 * (g % 2):256 * (g % 2) + 256], sg_last[:, g, 128 * t:128 * t + 128],
                          ysb, start=False, stop=g % 2 == 1)
                if g % 2:
                    last.then_inc(S("moe_psum"), 1)

        def project_normed(name, ready, n, lhs):
            for t in range(2):
                pe.wait_ge(S("xn3_ready"), ready + t + 1)
                do_fills(f"{name}{t}")
                pe.wait_ge(S("tr_copied"), marks[f"{name}{t}"][1])
                project((n + t, n + t + 1), lhs)
        project_normed("he", 0, P_E["aq"][0], hTe)
        for name in ("ak", "av", "bq"):
            project(P_E[name], hTe)
        pe.wait_ge(S("heads_ready"), 1)
        do_fills("aq")
        pe.wait_ge(S("heads_ready"), 2)
        do_fills("ak")
        project(P_E["bk"], hTe)
        pe.wait_ge(S("heads_ready"), 3)
        do_fills("bq")
        pe.wait_ge(S("tr_copied"), marks["bq"][1])
        pe.wait_ge(S("even_in"), 96)
        attention("a", (P_E["az"][0], P_E["bv"][1], hTe))
        pe.wait_ge(S("pt_copied"), ATT["a"][-1]["i"] + 1)
        pe.wait_ge(S("heads_ready"), 4)
        do_fills("bk")
        pe.wait_ge(S("tr_copied"), marks["bk"][1])
        pe.wait_ge(S("proj_evac"), P_E["bv"][1])
        attention("b", (*P_E["bz"], hTe), project_mix("mixe", "mixe_ready", ATT["b"], 12, P_OUT_E, mixeT, True))
        project_mix_rest("mixe", "mixe_ready", ATT["b"][-1], P_OUT_E, mixeT, True)
        project_normed("ho", 2, P_O["kv"][0], hTe)
        project(P_O["kw"], hTe)
        pe.wait_ge(S("proj_evac"), P_O["kv"][1])
        pe.wait_ge(S("odd_in"), 8 * 16)
        do_fills("cmp")
        project(P_O["cq"], hTe)
        pe.wait_ge(S("ab_ready"), 4)
        for s in range(2):
            g = GROUP_OF["phi_w1", s]
            pe.wait_ge(S(f"wg_in{g % WG_SLOTS}"), need[g])
            wt = view(WG[:, g % WG_SLOTS, :], 0, 32, 128)
            for l in range(32):
                for h in range(2):
                    c = l % 4
                    last = mm(PS[32 * c:32 * c + 32, 2 + h, 128 * s:128 * s + 128], ab[64 * h:64 * h + 64, s, l, :],
                              wt[64 * h:64 * h + 64, l, :], start=l < 4, stop=l >= 28)
            last.then_inc(S("phi_psum"), 1)
        project(P_O["ck"], hTe)
        pe.wait_ge(S("hrow_ready"), 2)
        pe.wait_ge(S("cmp_in"), 16)
        for s in range(2):
            for h in range(2):
                last = mm(PS[:, 6, 32 * s + 16 * h:32 * s + 16 * h + 16], hrow[:, h, s, :], sum_groups, start=True, stop=True)
        last.then_inc(S("hidT_psum"), 1)
        project((P_O["dq"][0], P_O["dq"][0] + 1), hTe)
        pe.wait_ge(S("phi_hid"), 10)
        for h in range(2):
            mm(PS[0:16, 7, 64 + 64 * h:128 + 64 * h], hidk[:, h, :], w2[:, 0, :], start=True, stop=True)
        mm(PS[:, 7, 0:64], hidv.rearrange("p a b -> p (a b)"), w2[:, 1, :], start=True, stop=True
           ).then_inc(S("kcmp_psum"), 1)
        project((P_O["dq"][0] + 1, P_O["dq"][1]), hTe)
        pe.wait_ge(S("heads_ready"), 5)
        do_fills("cq")
        pe.wait_ge(S("heads_ready"), 6)
        do_fills("ck")
        project(P_O["cv"], hTe)
        pe.wait_ge(S("kcmp_ready"), 1)
        do_fills("kcmp")
        pe.wait_ge(S("heads_ready"), 7)
        do_fills("dq")
        pe.wait_ge(S("dup_ready"), 1)
        do_fills("dup")
        pe.wait_ge(S("tr_copied"), marks["dup"][1])
        for t in range(2):
            for h in (0, 2, 4, 6, 1, 3, 5, 7):
                last = mm(PS[:, 2 + h % 2, 64 * t + 16 * (h // 2):64 * t + 16 * (h // 2) + 16],
                          dqT[half(h), h // 2, 128 * t:128 * t + 128], kcmpT[half(h), h // 4, :], start=True, stop=True)
        last.then_inc(S("sc_psum"), 1)
        n = P_O["cz"][0]
        project((n, n + 1), hTe)
        pe.wait_ge(S("pc_ready"), 1)
        do_fills("pc")
        pe.wait_ge(S("tr_copied"), marks["pc"][1])
        pe.wait_ge(S("vbd2_ready"), 1)
        for t in range(2):
            last = mm(bank(6 + t), pcT[:, t, :], vbd2.rearrange("p a b -> p (a b)"), start=True, stop=True)
        last.then_inc(S("oc_psum"), 1)
        project((n + 1, n + 2), hTe)
        pe.wait_ge(S("oc_read"), 1)
        attention("odd", (*P_O["dz"], hTe), project_mix("mixo", "mixo_ready", ATT["odd"], 28, P_OUT_O, mixeT, True))
        project_mix_rest("mixo", "mixo_ready", ATT["odd"][-1], P_OUT_O, mixeT, True)

    @block.scalar
    def _(act):
        fn = nc.scalar.activation
        step = stepper(act, "act_step")
        means = [0]

        def root(n):
            means[0] += 1
            act.wait_ge(S("ms_ready"), means[0])
            fn(stat[:, 0:n], stat[:, 0:n], ACT.Sqrt).then_inc(S("root_ready"), 1)

        def norm(src, junk, c):
            step(fn(junk, src, ACT.Square, accum_out=nst[:, c:c + 1]))
            fn(nst[:, c:c + 1], nst[:, c:c + 1], ACT.Sqrt, bias=eps, scale=1.0 / D).then_inc(S("root_ready"), 1)

        def copy_fills(name):
            for i in range(*marks[name]):
                _, dst, rows_, affine = FILLS[i]
                act.wait_ge(S("tr_ready"), i + 1)
                src = view(PS[:, 4 + i % 2, :], 0, *dst.shape[1:])
                if affine:
                    for k, (gain, shift) in enumerate(affine):
                        last = fn(dst[:, k], src[:, k], ACT.Identity, scale=gain, bias=shift)
                    last.then_inc(S("tr_copied"), 1)
                    continue
                fn(dst if rows_ == 128 or dst.shape[0] == rows_ else dst[0:rows_], src[0:rows_], ACT.Copy
                   ).then_inc(S("tr_copied"), 1)

        def evacuate(a, b):
            for n in range(a, b):
                _, _, _, w, dst, f, scale = PROJ[n]
                act.wait_ge(S("proj_ready"), n + 1)
                fn(dst, bank(n % 2)[:, 0:w], f, scale=scale).then_inc(S("proj_evac"), 1)

        def attention(name, between=None, beside=None):
            pb, _ = PB.get(name, (pb2, pt2))
            for k, u in enumerate(ATT[name]):
                i, n = u["i"], u["n"]
                act.wait_ge(S("max_ready"), i + 1)
                if name == "na":
                    if i >= 2:
                        act.wait_ge(S("pT_done"), i - 1)
                    fn(pb[:, i % 2, 0:n], bank(2 + i % 2)[:, 0:n], ACT.Exp, bias=negm[:, i % 8:i % 8 + 1],
                       accum_out=lsum[:, i:i + 1]).then_inc(S("exp_done"), 1)
                else:
                    fn(pb[:, i % 2, 0:n], pb[:, i % 2, 0:n], ACT.Exp, bias=negm[:, i % 8:i % 8 + 1], scale=-1.0,
                       accum_out=lsum[:, i:i + 1]).then_inc(S("exp_done"), 1)
                if between and k % 2 == 1 and between[0] + k // 2 < between[1]:
                    evacuate(between[0] + k // 2, between[0] + k // 2 + 1)
                if beside:
                    beside(k)

        act.wait_ge(S("cols_ready"), 1)
        act.wait_ge(S("csil_zero"), 1)
        fn(csil[:, :, 0:2].rearrange("p k w -> p w k"), view(cols, 40, 2, 8), ACT.Sigmoid).then_inc(S("csig"), 1)
        act.wait_ge(S("lb_in"), 1)
        fn(lbt[:, 0:8], lbt[:, 0:8], ACT.Exp).then_inc(S("lb_exp"), 1)
        root(4)
        for k in range(KC):
            act.wait_ge(S("hT_ready"), k + 1)
            fn(view(HT, 0, KC, 512)[:, k, :], bank(2 + k % 2), ACT.Copy).then_inc(S("hT_copied"), 1)
        evacuate(0, 8)
        rest = iter(range(P_IH, P_IN[1]))

        def evacuate_next():
            n = next(rest)
            evacuate(n, n + 1)

        def hg_log(h):
            act.wait_ge(S("hg_f"), h + 1)
            fn(fgt, fgt, ACT.Ln).then_inc(S("hg_ln"), 1)

        def hg_exps(h):
            act.wait_ge(S("hg_b"), h + 1)
            if h >= 2:
                act.wait_ge(S("hg_o"), h - 1)
            fn(eb[h % 2], bcum[:, :, 0:T], ACT.Exp).then_inc(S("hg_exp"), 1)
            fn(enb[h % 2], bcum[:, :, 0:T], ACT.Exp, scale=-1.0).then_inc(S("hg_exp"), 1)
            fn(kend, kend, ACT.Exp).then_inc(S("hg_exp"), 1)
            fn(decay[h % 2][:, 0, :], bcum[:, 0, CH - 1::CH], ACT.Exp).then_inc(S("hg_exp"), 1)
            fn(decay[h % 2][:, 1, :], bcum[:, 1, 0::CH], ACT.Exp).then_inc(S("hg_exp"), 1)
        hg_log(0)
        evacuate(8, 12)
        hg_exps(0)
        evacuate(12, P_IH)
        for h in range(HG):
            copy_fills(f"kend{h}")
            if h + 1 < HG:
                hg_log(h + 1)
            evacuate_next()
            if h + 1 < HG:
                hg_exps(h + 1)
            evacuate_next()
            evacuate_next()
        copy_fills("na")

        def readout(k):
            if k == 0:
                act.wait_ge(S("hg_o"), HG)
                for t in range(2):
                    fn(fgt[:, t], bank(6 + t), ACT.Square).then_inc(S("hg_sq"), 1)
            if k == 1:
                root(8)
            if k == 11:
                copy_fills("mix0")
            if k in (13, 15):
                evacuate(P_OUT[0] + (k - 13) // 2, P_OUT[0] + (k - 13) // 2 + 1)
        attention("na", beside=readout)
        copy_fills("mix1")
        for t in range(2):
            if t:
                evacuate(P_OUT[0] + 2, P_OUT[1])
            act.wait_ge(S("proj_evac"), P_OUT[0] + 2 * t + 2)
            norm(mixo[t], xn2[:, t, :], t)
            if t:
                copy_fills("h20")
            act.wait_ge(S("x_mid"), t + 1)
            norm(X[:, t, :], xn2[:, t, :], 2 + t)
        copy_fills("h21")
        act.wait_ge(S("lg_shift"), 1)
        fn(lg, lg, ACT.Exp).then_inc(S("lg_exp"), 1)
        copy_fills("aff")
        copy_fills("pos")

        def expert(e, first):
            if first:
                copy_fills("sg")
            act.wait_ge(S("gu_used"), 2 * KC * e + 2 * KC)
            if not first:
                act.wait_ge(S("hid_ready"), e)
            fn(view(sig, 0, 2, FH), PS[:, 0:2, 0:FH], ACT.Sigmoid).then_inc(S("sig_ready"), 1)
            act.wait_ge(S("hidT_done"), e + 1)
            if not first:
                act.wait_ge(S("dn_used"), 12 * e)
            fn(hidT[:, 0:4, :], view(PS[:, 4, :], 0, 4, 128), ACT.Copy).then_inc(S("hidT_copied"), 1)
            fn(hidT[:, 4, :], PS[:, 5, 0:128], ACT.Copy).then_inc(S("hidT_copied"), 1)
            fn(hidT[0:FS[5], 5, :], PS[0:FS[5], 5, 128:256], ACT.Copy).then_inc(S("hidT_copied"), 1)
            act.wait_ge(S("dn_used"), 12 * e + 12)
            if not first:
                act.wait_ge(S("y_stored"), 16 * e)
            fn(ysb, PS[:, 6, 0:256], ACT.Copy).then_inc(S("y_copied"), 1)
            act.wait_ge(S("y_copied"), e + 1)
            dst = y_dram.rearrange("(e s) (g c) -> e g s c", s=CAP, c=256)
            act.dma_start(dst[e], ysb).then_inc(S("y_stored"), 16)
        expert(0, True)
        with act.Fori(1, E) as e:
            expert(e, False)
        for t in range(2):
            act.wait_ge(S("moe_psum"), 2 * t + 2)
            norm(PS[:, 2 * t:2 * t + 2, :], view(moeo[:, t, :], 0, 2, 512), t)
        act.wait_ge(S("x_moe"), 1)
        norm(X[:, 0, :], xn3[:, 0, :], 2)
        copy_fills("he0")
        act.wait_ge(S("x_moe"), 2)
        norm(X[:, 1, :], xn3[:, 1, :], 3)
        evacuate(P_E["aq"][0], P_E["aq"][0] + 1)
        copy_fills("he1")
        evacuate(P_E["aq"][0] + 1, P_E["aq"][1])
        act.wait_ge(S("lam_in"), 1)
        fn(lamt[:, 0:2], lamt[:, 0:2], ACT.Exp).then_inc(S("lam_exp"), 1)
        evacuate(P_E["ak"][0], P_E["ak"][0] + 1)
        root(16)
        evacuate(P_E["ak"][0] + 1, P_E["av"][1])
        root(16)
        evacuate(*P_E["bq"])
        copy_fills("aq")
        copy_fills("ak")
        root(16)
        evacuate(*P_E["bk"])
        copy_fills("bq")
        root(16)
        attention("a", (P_E["az"][0], P_E["bv"][1]))
        copy_fills("bk")

        def first_tile(k):
            if k == 10:
                root(4)
            if k == 12:
                copy_fills("mixe0")
        attention("b", P_E["bz"], first_tile)
        root(4)
        copy_fills("mixe1")
        act.wait_ge(S("proj_evac"), P_OUT_E[0] + 2)
        norm(X[:, 0, :], xn3[:, 0, :], 2)
        copy_fills("ho0")
        act.wait_ge(S("proj_evac"), P_OUT_E[1])
        norm(X[:, 1, :], xn3[:, 1, :], 3)
        evacuate(P_O["kv"][0], P_O["kv"][0] + 1)
        copy_fills("ho1")
        evacuate(P_O["kv"][0] + 1, P_O["kw"][1])
        act.wait_ge(S("proj_evac"), P_O["kw"][1])
        fn(gates, kw[:, :, 256:280], ACT.Sigmoid).then_inc(S("gates_ready"), 1)
        copy_fills("cmp")
        evacuate(*P_O["cq"])
        root(16)
        act.wait_ge(S("phi_psum"), 2)
        act.wait_ge(S("cmp_in"), 16)
        for h in range(2):
            fn(hrow[:, h], view(PS[:, 2 + h, :], 0, 2, 128), ACT.Copy).then_inc(S("hrow_ready"), 1)
        evacuate(*P_O["ck"])
        act.wait_ge(S("hid_zero"), 2)
        act.wait_ge(S("hidT_psum"), 1)
        for h in range(2):
            fn(hidk[:, h, 0:NCMP], PS[:, 6, 16 * h:16 * h + NCMP], ACT.Silu).then_inc(S("phi_hid"), 1)
        for h in range(8):
            fn(hidv[:, h, 0:NCMP], PS[:, 6, 32 + 16 * (h % 4 // 2):32 + 16 * (h % 4 // 2) + NCMP], ACT.Silu
               ).then_inc(S("phi_hid"), 1)
        root(16)
        evacuate(*P_O["dq"])
        copy_fills("cq")
        copy_fills("ck")
        root(2)
        root(24)
        evacuate(*P_O["cv"])
        copy_fills("kcmp")
        copy_fills("dq")
        copy_fills("dup")
        act.wait_ge(S("sc_shift"), 1)
        fn(pc, pc, ACT.Exp).then_inc(S("sc_exp"), 1)
        evacuate(P_O["cz"][0], P_O["cz"][0] + 1)
        copy_fills("pc")
        evacuate(P_O["cz"][0] + 1, P_O["cz"][1])

        def first_tile_odd(k):
            if k == 28:
                copy_fills("mixo0")
        attention("odd", P_O["dz"], first_tile_odd)
        copy_fills("mixo1")

    @block.vector
    def _(dve):
        v = nc.vector
        step = stepper(dve, "dve_step")
        roots = [0]

        def mean(n, width):
            roots[0] += 1
            step(v.tensor_scalar(stat[:, 0:n], stat[:, 0:n], 1.0 / width, EPS, ALU.mult, ALU.add), "ms_ready")

        def inverse(n):
            dve.wait_ge(S("root_ready"), roots[0])
            step(v.reciprocal(stat[:, 0:n], stat[:, 0:n]))

        def inverse_norm(c):
            roots[0] += 1
            dve.wait_ge(S("root_ready"), roots[0])
            step(v.reciprocal(nst[:, c:c + 1], nst[:, c:c + 1]))

        def rms(items, n, width):
            for src, junk, c in items:
                step(v.tensor_tensor_reduce(out=junk, in0=src, in1=src, scale=1.0, scalar=0.0, op0=ALU.mult,
                                            op1=ALU.add, accum_out=stat[:, c:c + 1]))
            mean(n, width)
            inverse(n)

        def prenorm(t, dst, signal):
            inverse_norm(2 + t)
            step(v.tensor_scalar(dst[:, t, :], X[:, t, :], nst[:, 2 + t:3 + t], None, ALU.mult), signal)

        def postnorm(t, src, gain, dst, signal):
            inverse_norm(t)
            step(v.scalar_tensor_tensor(dst, src, nst[:, t:t + 1], gain, ALU.mult, ALU.mult))
            x = X[:, t, :] if len(dst.shape) == 2 else view(X[:, t, :], 0, 2, 512)
            step(v.tensor_tensor(x, x, dst, ALU.add), signal)

        def headed(ap, n, w):
            return ap.unsqueeze(2).to_broadcast([128, n, w])

        def attention(name, finish, beside=None):
            us = ATT[name]
            pb, pt = PB.get(name, (pb2, pt2))
            for k in range(len(us) + 2):
                if k < len(us):
                    i, n = us[k]["i"], us[k]["n"]
                    dve.wait_ge(S("s_ready"), i + 1)
                    if i >= 8:
                        dve.wait_ge(S("exp_done"), i - 7)
                    if name == "na":
                        v.tensor_reduce(negm[:, i % 8:i % 8 + 1], bank(2 + i % 2)[:, 0:n], AX, ALU.max, negate=True
                                        ).then_inc(S("max_ready"), 1)
                    else:
                        if i >= 2:
                            dve.wait_ge(S("pT_done"), i - 1)
                        v.tensor_tensor_reduce(out=pb[:, i % 2, 0:n], in0=bank(2 + i % 2)[:, 0:n], in1=us[k]["tab"],
                                               scale=-1.0, scalar=3e38, op0=ALU.add, op1=ALU.min,
                                               accum_out=negm[:, i % 8:i % 8 + 1]).then_inc(S("max_ready"), 1)
                if 1 <= k <= len(us):
                    i, n = us[k - 1]["i"], us[k - 1]["n"]
                    dve.wait_ge(S("pT_done"), i + 1)
                    if i >= 2:
                        dve.wait_ge(S("pv_done"), i - 1)
                    v.tensor_copy(pt[:, i % 2, 0:n], bank(4 + i % 2)[:, 0:n]).then_inc(S("pt_copied"), 1)
                if k >= 2 and us[k - 2]["last"]:
                    u = us[k - 2]
                    per = 512 // u["w"]
                    i0 = u["i"] - per + 1
                    dve.wait_ge(S("pv_done"), u["i"] + 1)
                    dve.wait_ge(S("exp_done"), u["i"] + 1)
                    step(v.reciprocal(rls[:, i0:i0 + per], lsum[:, i0:i0 + per]))
                    finish((k - 2) // per, o_bank(u["g"]), rls[:, i0:i0 + per])
                if beside:
                    beside(k)

        step(v.memset(eps, EPS))
        dve.wait_ge(S("rowsT"), 1)
        step(v.tensor_copy(cols[:, :], PS[:, 7, 0:104]), "cols_ready")
        dve.wait_ge(S("csig"), 1)
        cs = csil[:, :, 0:2].rearrange("p k w -> p w k")
        step(v.tensor_tensor(cs, cs, view(cols, 40, 2, 8), ALU.mult), "csil_ready")
        step(v.tensor_tensor(lbt[:, 8:12], cols[:, 32:36], cols[:, 36:40], ALU.max))
        step(v.tensor_tensor(lbt[:, 4:8], cols[:, 36:40], lbt[:, 8:12], ALU.subtract))
        step(v.tensor_tensor(lbt[:, 0:4], cols[:, 32:36], lbt[:, 8:12], ALU.subtract), "lb_in")
        dve.wait_ge(S("lb_exp"), 1)
        step(v.tensor_tensor(lbt[:, 8:12], lbt[:, 0:4], lbt[:, 4:8], ALU.add))
        step(v.reciprocal(lbt[:, 8:12], lbt[:, 8:12]))
        step(v.tensor_tensor(lb, lbt[:, 0:4], lbt[:, 8:12], ALU.mult))
        step(v.tensor_scalar(oml, lb, -1.0, 1.0, ALU.mult, ALU.add))
        dve.wait_ge(S("x_in"), 32)
        toks = [X[:, 0, :], X[:, 1, :], xctx[:, 0, :], xctx[:, 1, :]]
        rms([(a, xn[:, t, :], t) for t, a in enumerate(toks)], 4, D)
        for t, a in enumerate(toks):
            step(v.tensor_scalar(xn[:, t, :], a, stat[:, t:t + 1], None, ALU.mult), "xn_ready")

        def modulation(pair):
            for g in pair:
                dve.wait_ge(S("mod_ready"), g + 1)
                step(v.tensor_copy(mrow[:, g % 2, :], bank(6 + g % 2)), "mod_evac")
            for g in pair:
                dve.wait_ge(S("modT"), g + 1)
                if g == 4:
                    dve.wait_ge(S("gain_in"), 32)
                if g % 6 in (4, 5):
                    gp = view(GP1 if g < 6 else GP2[:, :], 512 * (g % 2), 512)
                    step(v.tensor_tensor(gp, gp, bank(4 + g % 2), ALU.mult), "gp_done")
                else:
                    parts = bank(4 + g % 2).rearrange("p (b g f) -> p b f g", g=4, f=32)[:, :, 0:2, :]
                    m = modc[:, 4 * g:4 * g + 4, :]
                    step(v.tensor_reduce(m, parts, AX, ALU.add))
                    step(v.tensor_tensor(m, m, headed(cols[:, 56 + 4 * g:60 + 4 * g], 4, 2), ALU.add), "modc_done")
        modulation((0, 1))
        modulation((2, 3))
        for dst, w in ((A1, 0), (A1c, 1)):
            step(v.scalar_tensor_tensor(dst, modc[:, 8:16, w], 1.0, cols[:, 0:8], ALU.add, ALU.mult))
        for k in range(KC):
            dve.wait_ge(S("hT_copied"), k + 1)
            for w, a in ((0, A1), (1, A1c)):
                hT = view(HT, 0, KC, 512)[:, k, T * w:T * w + T]
                step(v.tensor_scalar(hT, hT, a[:, k:k + 1], modc[:, k, w:w + 1], ALU.mult, ALU.add), "hT_done")
        modulation((4, 5))
        modulation((6, 7))
        dve.wait_ge(S("hg_in"), 48)

        def hg_gates(h):
            if h == 0:
                dve.wait_ge(S("proj_evac"), 8)
            else:
                dve.wait_ge(S("tr_copied"), marks[f"kend{h - 1}"][1])
            for d in range(2):
                step(v.tensor_scalar(fgt[:, d], z[:, d, h, :], oml[:, h:h + 1], lb[:, h:h + 1], ALU.mult, ALU.add))
            step(v.tensor_scalar(kk, fgt, -1.0, 1.0, ALU.mult, ALU.add), "hg_f")

        def hg_sums(h):
            dve.wait_ge(S("hg_ln"), h + 1)
            step(v.tensor_tensor_scan(bcum[:, 0], reset, fgt[:, 0], 0.0, ALU.mult, ALU.add))
            step(v.tensor_tensor_scan(bcum[:, 1, ::-1], reset, fgt[:, 1, ::-1], 0.0, ALU.mult, ALU.add))
            for d in range(2):
                b = bcum[:, d].rearrange("p (n c) -> p n c", c=CH)
                e = b[:, :, CH - 1:CH] if d == 0 else b[:, :, 0:1]
                step(v.tensor_tensor(kend[:, d].rearrange("p (n c) -> p n c", c=CH),
                                     e.to_broadcast([128, 16, CH]), b, ALU.subtract))
            dve.sem_inc(S("hg_b"), 1)

        def hg_decay(h):
            if h == 0:
                dve.wait_ge(S("proj_evac"), 12)
            dve.wait_ge(S("hg_exp"), 5 * h + 5)
            step(v.tensor_tensor(kdec[h % 2], kk[:, :, 0:T], enb[h % 2], ALU.mult))
            for d in range(2):
                step(v.tensor_tensor(qdec[h % 2][:, d], qh[:, h], eb[h % 2][:, d], ALU.mult))
            step(v.tensor_tensor(kend, kend, kk, ALU.mult), "hg_dec")

        def rope(src, dst):
            for t in range(2):
                x3 = src[:, t, :].rearrange("p (h c) -> p h c", c=64)
                y3 = dst[:, t, :].rearrange("p (h c) -> p h c", c=64)
                step(v.tensor_tensor(y3, x3, rcos[:, t, :].unsqueeze(1).to_broadcast([128, 8, 64]), ALU.mult))
                for hf in range(2):
                    for j in range(2):
                        a, b = 32 * hf + 16 * j, 32 * hf + 16 * (1 - j)
                        step(v.tensor_tensor(view(rt, 0, 8, 64)[:, :, a:a + 16], x3[:, :, b:b + 16],
                                             rsin[:, t, a:a + 16].unsqueeze(1).to_broadcast([128, 8, 16]), ALU.mult))
                step(v.tensor_tensor(dst[:, t, :], dst[:, t, :], rt, ALU.add))
        hg_gates(0)
        hg_sums(0)
        modulation((8, 9))
        step(v.scalar_tensor_tensor(A2, modc[:, 32:40, 0], 1.0, cols[:, 8:16], ALU.add, ALU.mult))
        hg_decay(0)
        modulation((10, 11))
        dve.wait_ge(S("vbd_zero"), 3)
        for h in range(HG):
            dve.wait_ge(S("kv_ready"), 9 * h + 1)
            if h >= 2:
                dve.wait_ge(S("hg_o"), h - 1)
            step(v.copy_predicated(aT[h % 2], cmask.bitcast(I32), view(bank(2 + 9 * h % 2), 0, 4, 128)), "kv_used")
            if h + 1 < HG:
                hg_gates(h + 1)
            else:
                dve.wait_ge(S("proj_evac"), P_KN)
                dve.wait_ge(S("na_in"), 64)
                rope(qn, qr)
            for j in range(8):
                if j == 4:
                    if h + 1 < HG:
                        hg_sums(h + 1)
                    else:
                        rope(kn, kr)
                        dve.sem_inc(S("rope_ready"), 1)
                    if h:
                        dve.wait_ge(S("hg_o"), h)
                if j == 6 and h + 1 < HG:
                    hg_decay(h + 1)
                d, s = j % 2, j // 2
                t = ((2, 3, 0, 1), (3, 2, 1, 0))[d][s]
                dve.wait_ge(S("kv_ready"), 9 * h + j + 2)
                for i in range(4):
                    c = i if d == 0 else 3 - i
                    kv = bank(2 + (9 * h + j + 1) % 2)[:, 128 * c:128 * c + 128]
                    n = 4 * s + i
                    sig_ = "kv_used" if i == 3 else "dve_step"
                    if n == 0:
                        step(v.tensor_copy(states[:, d, 0, :], kv))
                    elif n < 15:
                        step(v.scalar_tensor_tensor(states[:, d, state_slot(n, h), :], states[:, d, state_slot(n - 1, h), :],
                                                    decay[h % 2][:, d, 4 * t + c:4 * t + c + 1], kv, ALU.mult, ALU.add), sig_)
                    else:
                        step(v.tensor_copy(stat[:, 0:1], kv[:, 0:1]), sig_)
            dve.sem_inc(S("states_ready"), 1)

        def readout(k):
            if k == 1:
                dve.wait_ge(S("hg_sq"), 2)
                step(v.tensor_reduce(stat[:, 0:8], view(fgt.rearrange("p a b -> p (a b)"), 0, 8, 128), AX, ALU.add))
                mean(8, HG * 32)
            if k == 2:
                inverse(8)
            if k in (2, 4):
                t = k // 2 - 1
                m = mixcat[:, t, 512:D].rearrange("p (h c) -> p h c", c=128)
                step(v.tensor_tensor(m, view(bank(6 + t), 0, 4, 128), headed(stat[:, 4 * t:4 * t + 4], 4, 128), ALU.mult), "hg_read")
                step(v.tensor_tensor(m, m, b_hg.unsqueeze(1).to_broadcast([128, 4, 128]), ALU.mult))
                step(v.tensor_tensor(mixcat[:, t, 512:D], mixcat[:, t, 512:D], gh[:, t, :], ALU.mult), "gh_used")

        def na_finish(i, o, r):
            step(v.tensor_tensor(mixcat[:, i, 0:512].rearrange("p (h c) -> p h c", c=64), view(o, 0, 8, 64),
                                 headed(r, 8, 64), ALU.mult), "o_read")
            dve.sem_inc(S("mixcat_ready"), 1)
        attention("na", na_finish, readout)
        for t in range(2):
            postnorm(t, mixo[t], GP1, mixo[t], "x_mid")
            prenorm(t, xn2, "xn2_ready")
        dve.wait_ge(S("lg_ready"), 1)
        step(v.tensor_reduce(amax, view(PS[:, 6, :], 0, 2, E), AX, ALU.max, negate=True))
        step(v.tensor_tensor(lg, view(PS[:, 6, :], 0, 2, E), headed(amax, 2, E), ALU.add), "lg_shift")
        dve.wait_ge(S("lg_exp"), 1)
        step(v.tensor_reduce(amax, lg, AX, ALU.add))
        step(v.reciprocal(amax, amax))
        step(v.tensor_tensor(aff, lg, headed(amax, 2, E), ALU.mult), "aff_ready")
        dve.wait_ge(S("tr_copied"), marks["aff"][1])
        src = affT
        for i in range(CAP // 8):
            step(v.max(best8[0:E, :], src[0:E, :]))
            step(v.match_replace(work[0:E, :], best8[0:E, :], src[0:E, :], -1.0))
            src = work
        dve.wait_ge(S("rt_in"), 48)
        step(v.tensor_scalar(work[0:E, :], work[0:E, :], -1.0, None, ALU.is_equal))
        step(v.tensor_tensor_scan(pos[0:E, :], ones[0:E, :], work[0:E, :], 0.0, ALU.mult, ALU.add))
        step(v.tensor_tensor(posm[0:E, :], pos[0:E, :], work[0:E, :], ALU.mult), "pos_ready")
        dve.wait_ge(S("tr_copied"), marks["pos"][1])
        for t in range(2):
            step(v.tensor_tensor(oh[:, t], headed(posT[:, t, :], E, CAP),
                                 slot.unsqueeze(1).to_broadcast([128, E, CAP]), ALU.is_equal), "oh_ready")
        def gathered(k, o, c0, c1):
            dve.wait_ge(S("xs_psum"), KC + k + 1 if c0 else 4 * (k // 4) + 4)
            step(v.tensor_scalar(xs[:, k, c0:c1], o, A2[:, k:k + 1], modc[:, 24 + k, 0:1], ALU.mult, ALU.add), "xs_done")
        for k in range(KC):
            gathered(k, PS[:, 6 + k // 4, 128 * (k % 4):128 * (k % 4) + 128], 0, 128)

        def expert(e, first):
            if not first:
                dve.wait_ge(S("gu_used"), 2 * KC * e)
            v.tensor_copy(xse, xs[:, :, bass.ds(e * CAP, CAP)]).then_inc(S("xse_ready"), 1)
            if first:
                for t in range(2):
                    step(v.tensor_tensor(ohg[:, t], oh[:, t], headed(aff[:, t, :], E, CAP), ALU.mult), "ohg_ready")
                for k in range(KC):
                    gathered(k, bank(6 + (k + 1) % 2)[:, 0:512 - 128], 128, 512)
            dve.wait_ge(S("sig_ready"), e + 1)
            if not first:
                dve.wait_ge(S("hidT_done"), e)
            v.tensor_tensor(view(sig, 0, 2, FH), view(sig, 0, 2, FH), PS[:, 0:2, 0:FH], ALU.mult
                            ).then_inc(S("silu_ready"), 1)
            dve.wait_ge(S("silu_ready"), e + 1)
            v.tensor_tensor(view(hid, 0, 2, FH), view(sig, 0, 2, FH), PS[:, 2:4, 0:FH], ALU.mult
                            ).then_inc(S("hid_ready"), 1)
        expert(0, True)
        with dve.Fori(1, E) as e:
            expert(e, False)
        for t in range(2):
            postnorm(t, PS[:, 2 * t:2 * t + 2, :], view(GP2[:, :], 0, 2, 512), view(moeo[:, t, :], 0, 2, 512), "x_moe")
        for t in range(2):
            prenorm(t, xn3, "xn3_ready")

        def norm_heads(i, evac, gain):
            dve.wait_ge(S("proj_evac"), evac)
            x, sq = view(BIG, 1024 * i, 16, 64), view(BIG, t2_off, 16, 64)
            step(v.tensor_tensor(sq, x, x, ALU.mult))
            step(v.tensor_reduce(stat[:, 0:16], sq, AX, ALU.add))
            rms([], 16, 64)
            step(v.tensor_tensor(x, x, headed(stat[:, 0:16], 16, 64), ALU.mult))
            step(v.tensor_tensor(x, x, gain.unsqueeze(1).to_broadcast([128, 16, 64]), ALU.mult), "heads_ready")
        dve.wait_ge(S("even_in"), 96)
        for b in (b_qe, b_qo):
            step(v.tensor_scalar(b[:, 0::2, :][:, 0:2], b[:, 0::2, :][:, 0:2], 0.125, None, ALU.mult))
        step(v.tensor_tensor(b_lam[:, 0::2, :], b_lam[:, 0::2, :], b_lam[:, 1::2, :], ALU.mult))
        step(v.tensor_reduce(lamt[:, 0:2], b_lam[:, 0::2, :], AX, ALU.add), "lam_in")
        dve.wait_ge(S("lam_exp"), 1)
        step(v.tensor_tensor(lamt[:, 2:3], lamt[:, 0:1], lamt[:, 1:2], ALU.subtract))
        step(v.tensor_scalar(lamt[:, 2:3], lamt[:, 2:3], LAM_INIT, None, ALU.add))
        for i, name in enumerate(("aq", "ak", "bq", "bk")):
            norm_heads(i, P_E[name][1], b_qe[:, i, :])

        def plain_finish(dst, zz_):
            def finish(i, o, r):
                m = dst[:, i, 0:512].rearrange("p (h c) -> p h c", c=64)
                step(v.tensor_tensor(m, view(o, 0, 8, 64), headed(r, 8, 64), ALU.mult), "o_read")
                step(v.tensor_tensor(dst[:, i, 0:512], dst[:, i, 0:512], zz_[:, i, :], ALU.mult))
            return finish

        def diff_finish(i, o, r):
            qt, pair = i // 2, i % 2
            ov = view(o, 0, 2, 2, 128)
            r2 = r.rearrange("p (h c) -> p h c", c=2)
            step(v.tensor_scalar(r2[:, :, 1], r2[:, :, 1], lamt[:, 2:3], None, ALU.mult))
            t0, t1 = view(BIG, t2_off, 2, 128), view(BIG, t2_off + 256, 2, 128)
            for c, t_ in ((0, t0), (1, t1)):
                step(v.tensor_tensor(t_, ov[:, :, c, :], headed(r2[:, :, c], 2, 128), ALU.mult))
            m = mixe[:, qt, 512 + 256 * pair:768 + 256 * pair].rearrange("p (h c) -> p h c", c=128)
            step(v.tensor_tensor(m, t0, t1, ALU.subtract), "o_read")
        attention("a", plain_finish(mixe, zz[:, 0]))
        def add_units(a, b):
            for n in range(a, b):
                _, _, _, w, dst, _, _ = PROJ[n]
                dve.wait_ge(S("proj_ready"), n + 1)
                v.tensor_tensor(dst, dst, bank(n % 2), ALU.add).then_inc(S("proj_evac"), 1)
                dve.wait_ge(S("proj_evac"), n + 1)
        step(v.tensor_scalar(b_sub, b_sub, 1.0 - LAM_INIT, None, ALU.mult))

        def sub_norm_sums(t):
            ob, sq = mixe[:, t, 512:D].rearrange("p (h c) -> p h c", c=128), view(BIG, t2_off + 512, 4, 128)
            step(v.tensor_tensor(sq, ob, ob, ALU.mult))
            step(v.tensor_reduce(stat[:, 0:4], sq, AX, ALU.add))
            mean(4, 128)

        def sub_norm(t):
            ob = mixe[:, t, 512:D].rearrange("p (h c) -> p h c", c=128)
            inverse(4)
            step(v.tensor_tensor(ob, ob, headed(stat[:, 0:4], 4, 128), ALU.mult))
            step(v.tensor_tensor(ob, ob, b_sub.unsqueeze(1).to_broadcast([128, 4, 128]), ALU.mult))
            dve.wait_ge(S("proj_evac"), P_E["bz"][1])
            step(v.tensor_tensor(mixe[:, t, 512:D], mixe[:, t, 512:D], zz[:, 1][:, t, :], ALU.mult), "mixe_ready")

        def first_tile(k):
            if k == 9:
                sub_norm_sums(0)
            if k == 10:
                sub_norm(0)
            if k == 14:
                add_units(P_OUT_E[0], P_OUT_E[0] + 1)
        attention("b", diff_finish, first_tile)
        sub_norm_sums(1)
        sub_norm(1)
        add_units(P_OUT_E[0] + 1, P_OUT_E[0] + 2)
        prenorm(0, xn3, "xn3_ready")
        add_units(P_OUT_E[0] + 2, P_OUT_E[1])
        prenorm(1, xn3, "xn3_ready")
        step(v.memset(hidk, 0.0), "hid_zero")
        step(v.memset(hidv, 0.0), "hid_zero")
        dve.wait_ge(S("tr_copied"), marks["cmp"][1])
        dve.wait_ge(S("ab_zero"), 1)
        for s in range(2):
            kv2 = kcvT[:, s, :].rearrange("p (i b) -> p b i", b=16)
            for a in range(2):
                step(v.tensor_tensor(ab[:, s, 16 * a:16 * a + 16, 0:NCMP], kv2[:, :, a:a + NCMP],
                                     peT[:, s, 16 * a:16 * a + 16].unsqueeze(2).to_broadcast([128, 16, NCMP]),
                                     ALU.add), "ab_ready")
        norm_heads(0, P_O["cq"][1], b_qo[:, 0, :])
        norm_heads(1, P_O["ck"][1], b_qo[:, 1, :])
        dve.wait_ge(S("kcmp_psum"), 1)
        kp = view(PS[:, 7, :], 64, 2, 64)[0:16]
        k0 = view(BIG, t2_off, 2, 64)[0:16]
        tq = view(BIG, t2_off + 128, 2, 64)[0:16]
        step(v.tensor_copy(k0, kp))
        step(v.tensor_tensor(tq, k0, k0, ALU.mult))
        step(v.memset(stat[:, 0:2], 1.0))
        step(v.tensor_reduce(stat[0:16, 0:2], tq, AX, ALU.add))
        rms([], 2, 64)
        step(v.tensor_tensor(k0, k0, stat[0:16, 0:2].unsqueeze(2).to_broadcast([16, 2, 64]), ALU.mult))
        for dd in range(2):
            step(v.tensor_tensor(kcmp[0:16, :, 64 * dd:64 * dd + 64], k0,
                                 b_qo[0:16, 3, :].unsqueeze(1).to_broadcast([16, 2, 64]), ALU.mult))
        dve.sem_inc(S("kcmp_ready"), 1)
        dve.wait_ge(S("proj_evac"), P_O["dq"][1])
        x, sq = view(BIG, 2048, 16, 64), view(BIG, t2_off, 16, 64)
        step(v.tensor_tensor(sq, x, x, ALU.mult))
        step(v.tensor_reduce(stat[:, 0:16], sq, AX, ALU.add))
        for i, src in ((0, ckv[:, :, 256:384]), (1, kw[:, :, 0:128])):
            for t in range(2):
                s2 = src[:, t, :].rearrange("p (h c) -> p h c", c=64)
                tq = view(BIG, t2_off + 1024 + 128 * (2 * i + t), 2, 64)
                step(v.tensor_tensor(tq, s2, s2, ALU.mult))
                step(v.tensor_reduce(stat[:, 16 + 4 * i + 2 * t:18 + 4 * i + 2 * t], tq, AX, ALU.add))
        rms([], 24, 64)
        step(v.tensor_tensor(x, x, headed(stat[:, 0:16], 16, 64), ALU.mult))
        step(v.tensor_tensor(x, x, b_qo[:, 2, :].unsqueeze(1).to_broadcast([128, 16, 64]), ALU.mult), "heads_ready")
        for i, src, gain in ((0, ckv[:, :, 256:384], 4), (1, kw[:, :, 0:128], 5)):
            for t in range(2):
                s2 = src[:, t, :].rearrange("p (h c) -> p h c", c=64)
                step(v.tensor_tensor(s2, s2, headed(stat[:, 16 + 4 * i + 2 * t:18 + 4 * i + 2 * t], 2, 64), ALU.mult))
                for dd in range(2):
                    step(v.tensor_tensor(view(dup[:, i, t, :], 0, 2, 2, 64)[:, :, dd, :], s2,
                                         b_qo[:, gain, :].unsqueeze(1).to_broadcast([128, 2, 64]), ALU.mult))
        dve.sem_inc(S("dup_ready"), 1)
        step(v.tensor_tensor(vbd2, PS[:, 7, 0:64].unsqueeze(1).to_broadcast([128, 8, 64]),
                             bdiag.unsqueeze(2).to_broadcast([128, 8, 64]), ALU.mult), "vbd2_ready")
        dve.wait_ge(S("sc_psum"), 1)
        for par in range(2):
            step(v.tensor_tensor(pc[:, :, 64 * par:64 * par + 64], view(PS[:, 2 + par, :], 0, 2, 64),
                                 cbias[:, :, 64 * par:64 * par + 64], ALU.add))
        p16 = view(pc.rearrange("p a b -> p (a b)"), 0, 16, 16)
        step(v.tensor_reduce(stat[:, 0:16], p16, AX, ALU.max))
        step(v.tensor_tensor(p16, p16, headed(stat[:, 0:16], 16, 16), ALU.subtract), "sc_shift")
        dve.wait_ge(S("sc_exp"), 1)
        step(v.tensor_tensor(pc, pc, ckeep, ALU.mult))
        step(v.tensor_reduce(stat[:, 0:16], p16, AX, ALU.add))
        step(v.tensor_scalar(stat[:, 0:16], stat[:, 0:16], 1e-30, None, ALU.max))
        step(v.reciprocal(stat[:, 0:16], stat[:, 0:16]))
        step(v.tensor_tensor(p16, p16, headed(stat[:, 0:16], 16, 16), ALU.mult), "pc_ready")
        dve.wait_ge(S("oc_psum"), 1)
        dve.wait_ge(S("gates_ready"), 1)
        g3 = gates.rearrange("p t (h j) -> p t h j", j=3)
        for t in range(2):
            step(v.tensor_tensor(ocmp[:, t, :].rearrange("p (h c) -> p h c", c=64), view(bank(6 + t), 0, 8, 64),
                                 headed(g3[:, t, :, 0], 8, 64), ALU.mult))
        dve.sem_inc(S("oc_read"), 1)

        def gated_finish(j):
            def finish(i, o, r):
                step(v.tensor_tensor(r, r, g3[:, i, :, j], ALU.mult))
                t_ = view(BIG, t2_off, 8, 64)
                step(v.tensor_tensor(t_, view(o, 0, 8, 64), headed(r, 8, 64), ALU.mult), "o_read")
                o3 = ocmp[:, i, :].rearrange("p (h c) -> p h c", c=64)
                step(v.tensor_tensor(o3, o3, t_, ALU.add))
            return finish
        dve.wait_ge(S("proj_evac"), P_O["cz"][1])
        parts = (plain_finish(mixe, zz[:, 0]), gated_finish(1), gated_finish(2))

        def odd_finish(i, o, r):
            parts[i % 3](i // 3, o, r)

        def gate_tile(t):
            step(v.tensor_tensor(mixe[:, t, 512:D], ocmp[:, t, :], zz[:, 1][:, t, :], ALU.mult), "mixo_ready")

        def first_tile_odd(k):
            if k == 25:
                dve.wait_ge(S("proj_evac"), P_O["dz"][1])
                gate_tile(0)
            if k == 30:
                add_units(P_OUT_O[0], P_OUT_O[0] + 1)
        attention("odd", odd_finish, first_tile_odd)
        gate_tile(1)
        add_units(P_OUT_O[0] + 1, P_OUT_O[0] + 2)
        dve.sem_inc(S("x_final"), 1)
        add_units(P_OUT_O[0] + 2, P_OUT_O[1])
        dve.sem_inc(S("x_final"), 1)

    ctx.close()


def kernel(**inputs):
    import concourse.bacc as _bacc
    from concourse.bass_utils import run_bass_kernel_spmd as _run

    nc = _bacc.Bacc("TRN2", target_bir_lowering=False, num_devices=1, dynamic_dma_scratch_size=4096)
    arrays, aps = {}, {}
    w1 = np.asarray(inputs.pop("phi_w1_2"))[0].reshape(2, 32, 64, 128)
    inputs["phi_w1"] = w1.transpose(0, 2, 1, 3).reshape(2, 64, 32 * 128)
    for name, a in [*inputs.items(), *constants().items()]:
        a = np.ascontiguousarray(a)
        arrays[f"in_{name}"] = a
        aps[name] = nc.dram_tensor(f"in_{name}", a.shape, mybir.dt.from_np(a.dtype), kind="ExternalInput").ap()
    out = nc.dram_tensor("out_x", (1, T, D), FP32, kind="ExternalOutput").ap()
    build(nc, aps, out)
    r = _run(nc, [arrays], core_ids=[0])
    return r.results[0]["out_x"]
```
